# Optimizing a Trainium2 kernel written in Bass

```python
import jax, jax.numpy as jnp
from jax import lax
import numpy as np

D_MODEL = 1024
BATCH = 1
SEQ = 1024
DEPTH = 1
DEC_BATCH = 8
DEC_SEQ = 1
PAST_LEN = 4096
PAGE_SIZE = 128

HEAD_DIM = 64
D_ATTN = D_MODEL // 2
N_HEADS = D_ATTN // HEAD_DIM
D_CONV = D_MODEL - D_ATTN
CONV_WIDTH = 3
WIN_KEYS = 128
DILATIONS = (1, 4, 16)
MAX_WINDOW = WIN_KEYS * max(DILATIONS)
N_GROUPS = 4
EXPERTS_PER_GROUP = 8
N_EXPERTS = N_GROUPS * EXPERTS_PER_GROUP
TOP_K = 2
D_EXPERT = D_MODEL // 2
MOE_BLOCK = 128
EPS = 1e-6
NEG = -1e30

kernel_name = 'hymba_dilated_shortconv_hmoe_step'

def _rmsnorm(x, g):
    xf = x.astype(jnp.float32)
    y = xf * lax.rsqrt(jnp.mean(xf * xf, axis=-1, keepdims=True) + EPS) * g.astype(jnp.float32)
    return y.astype(x.dtype)

def _mix_in(h, w_in):
    proj = h @ w_in
    q, k, v, b, c, hv = jnp.split(
        proj, [D_ATTN, 2 * D_ATTN, 3 * D_ATTN, 3 * D_ATTN + D_CONV, 3 * D_ATTN + 2 * D_CONV], axis=-1)
    shp = h.shape[:-1] + (N_HEADS, HEAD_DIM)
    return q.reshape(shp), k.reshape(shp), v.reshape(shp), b, c * hv

def _combine(parts):
    m = jnp.stack([p[0] for p in parts])
    l = jnp.stack([p[1] for p in parts])
    acc = jnp.stack([p[2] for p in parts])
    w = jnp.exp(m - m.max(axis=0))
    return (w[..., None] * acc).sum(0) / (w * l).sum(0)[..., None]

def _branch_prompt(q, k, v, dil):
    B, S, H, Dh = q.shape
    span = dil * WIN_KEYS
    Sp = -(-S // span) * span
    nb = Sp // span

    def blocks(t):
        t = jnp.pad(t, ((0, 0), (0, Sp - S), (0, 0), (0, 0))).reshape(B, Sp // dil, dil, H, Dh)
        return t.transpose(0, 2, 1, 3, 4).reshape(B, dil, nb, WIN_KEYS, H, Dh)

    def with_prev(t):
        prev = jnp.pad(t[:, :, :-1], ((0, 0), (0, 0), (1, 0), (0, 0), (0, 0), (0, 0)))
        return jnp.concatenate([prev, t], axis=3)

    qb = blocks(q)
    kw, vw = with_prev(blocks(k)), with_prev(blocks(v))
    s = jnp.einsum('bgnrhd,bgnchd->bgnhrc', qb, kw,
                   preferred_element_type=jnp.float32) * (HEAD_DIM ** -0.5)
    r = jnp.arange(WIN_KEYS)[:, None]
    c = jnp.arange(2 * WIN_KEYS)[None, :]
    band = (c >= r) & (c <= r + WIN_KEYS)
    has_prev = (jnp.arange(nb) > 0)[:, None, None] | (c >= WIN_KEYS)[None]
    valid = band[None] & has_prev
    s = jnp.where(valid[None, None, :, None], s, NEG)
    m = s.max(-1)
    p = jnp.exp(s - m[..., None])
    l = p.sum(-1)
    acc = jnp.einsum('bgnhrc,bgnchd->bgnrhd', p, vw.astype(jnp.float32))
    m = m.transpose(0, 2, 4, 1, 3).reshape(B, Sp, H)[:, :S]
    l = l.transpose(0, 2, 4, 1, 3).reshape(B, Sp, H)[:, :S]
    acc = acc.transpose(0, 2, 3, 1, 4, 5).reshape(B, Sp, H, Dh)[:, :S]
    return m, l, acc

def _branch_sample(q, kk, vv, dil, w_buf):
    DS = q.shape[1]
    idx = (w_buf + jnp.arange(DS))[:, None] - dil * jnp.arange(WIN_KEYS + 1)[None, :]
    valid = idx >= 0
    idx = jnp.maximum(idx, 0)
    kg = jnp.take(kk, idx, axis=1)
    vg = jnp.take(vv, idx, axis=1)
    s = jnp.einsum('bjhd,bjihd->bjhi', q, kg,
                   preferred_element_type=jnp.float32) * (HEAD_DIM ** -0.5)
    s = jnp.where(valid[None, :, None, :], s, NEG)
    m = s.max(-1)
    p = jnp.exp(s - m[..., None])
    l = p.sum(-1)
    acc = jnp.einsum('bjhi,bjihd->bjhd', p, vg.astype(jnp.float32))
    return m, l, acc

def _short_conv(u, state, w):
    cat = jnp.concatenate([state.astype(u.dtype), u], axis=1)
    L = u.shape[1]
    z = cat[:, 0:L] * w[0]
    for j in range(1, CONV_WIDTH):
        z = z + cat[:, j:j + L] * w[j]
    return z, cat[:, -(CONV_WIDTH - 1):]

def _mix_out(attn, conv, g_a, g_c, w_out):
    a = attn.reshape(attn.shape[:-2] + (D_ATTN,))
    o = jnp.concatenate([_rmsnorm(a, g_a), _rmsnorm(conv, g_c)], axis=-1)
    return o @ w_out

def _moe(x, w_rg, b_rg, w_re, b_re, w_gate, w_up, w_down):
    T, D = x.shape
    lg = jnp.matmul(x, w_rg, preferred_element_type=jnp.float32) + b_rg
    p_group = jax.nn.softmax(lg, axis=-1)
    g_sel = jnp.argmax(lg, axis=-1)
    le = (jnp.matmul(x, w_re, preferred_element_type=jnp.float32) + b_re).reshape(
        T, N_GROUPS, EXPERTS_PER_GROUP)
    le_sel = jnp.take_along_axis(le, g_sel[:, None, None], axis=1)[:, 0]
    top_v, top_i = lax.top_k(le_sel, TOP_K)
    gates = jax.nn.softmax(top_v, axis=-1) * jnp.take_along_axis(p_group, g_sel[:, None], axis=1)
    e_flat = (g_sel[:, None] * EXPERTS_PER_GROUP + top_i).reshape(-1)
    A = T * TOP_K
    tok_flat = jnp.repeat(jnp.arange(T), TOP_K)
    order = jnp.argsort(e_flat)
    e_s, tok_s, gate_s = e_flat[order], tok_flat[order], gates.reshape(-1)[order]
    counts = jax.ops.segment_sum(jnp.ones((A,), jnp.int32), e_flat, num_segments=N_EXPERTS)
    start = jnp.cumsum(counts) - counts
    padded = (counts + MOE_BLOCK - 1) // MOE_BLOCK * MOE_BLOCK
    pend = jnp.cumsum(padded)
    pstart = pend - padded
    dest = pstart[e_s] + jnp.arange(A) - start[e_s]
    n_blocks = -(-A // MOE_BLOCK) + N_EXPERTS
    xbuf = jnp.zeros((n_blocks * MOE_BLOCK, D), x.dtype).at[dest].set(x[tok_s])
    block_e = jnp.minimum(
        jnp.searchsorted(pend, jnp.arange(n_blocks) * MOE_BLOCK, side='right'), N_EXPERTS - 1)

    def expert_block(args):
        xb, e = args
        hid = jax.nn.silu(xb @ w_gate[e]) * (xb @ w_up[e])
        return hid @ w_down[e]

    ybuf = lax.map(expert_block, (xbuf.reshape(n_blocks, MOE_BLOCK, D), block_e)).reshape(-1, D)
    out = jax.ops.segment_sum(gate_s[:, None] * ybuf[dest].astype(jnp.float32), tok_s, num_segments=T)
    return out.astype(x.dtype)

def setup_inputs(seed: int = 0) -> dict:
    key = jax.random.key(seed)
    ks = jax.random.split(key, 20)
    w_buf = min(MAX_WINDOW, PAST_LEN)

    def nrm(k, shape, scale):
        return jax.random.normal(k, shape, jnp.float32) * scale

    def gain(k, shape):
        return 1.0 + 0.01 * jax.random.normal(k, shape, jnp.float32)

    return {
        'x_prompt': nrm(ks[0], (BATCH, SEQ, D_MODEL), 1.0),
        'x_sample': nrm(ks[1], (DEC_BATCH, DEC_SEQ, D_MODEL), 1.0),
        'cache_k': nrm(ks[2], (DEPTH, DEC_BATCH, w_buf, N_HEADS, HEAD_DIM), 1.0),
        'cache_v': nrm(ks[3], (DEPTH, DEC_BATCH, w_buf, N_HEADS, HEAD_DIM), 1.0),
        'state_conv': nrm(ks[4], (DEPTH, DEC_BATCH, CONV_WIDTH - 1, D_CONV), 1.0),
        'norm_mix': gain(ks[5], (DEPTH, D_MODEL)),
        'w_in': nrm(ks[6], (DEPTH, D_MODEL, 3 * D_ATTN + 3 * D_CONV), D_MODEL ** -0.5),
        'conv_w': nrm(ks[7], (DEPTH, CONV_WIDTH, D_CONV), CONV_WIDTH ** -0.5),
        'norm_out_attn': gain(ks[8], (DEPTH, D_ATTN)),
        'norm_out_conv': gain(ks[9], (DEPTH, D_CONV)),
        'w_out': nrm(ks[10], (DEPTH, D_MODEL, D_MODEL), D_MODEL ** -0.5),
        'norm_ffn': gain(ks[11], (DEPTH, D_MODEL)),
        'w_router_group': nrm(ks[12], (DEPTH, D_MODEL, N_GROUPS), D_MODEL ** -0.5),
        'b_router_group': nrm(ks[13], (DEPTH, N_GROUPS), 0.01),
        'w_router_expert': nrm(ks[14], (DEPTH, D_MODEL, N_EXPERTS), D_MODEL ** -0.5),
        'b_router_expert': nrm(ks[15], (DEPTH, N_EXPERTS), 0.01),
        'w_gate': nrm(ks[16], (DEPTH, N_EXPERTS, D_MODEL, D_EXPERT), D_MODEL ** -0.5),
        'w_up': nrm(ks[17], (DEPTH, N_EXPERTS, D_MODEL, D_EXPERT), D_MODEL ** -0.5),
        'w_down': nrm(ks[18], (DEPTH, N_EXPERTS, D_EXPERT, D_MODEL), D_EXPERT ** -0.5),
        'norm_final': gain(ks[19], (D_MODEL,)),
    }

def reference(x_prompt, x_sample, cache_k, cache_v, state_conv, norm_mix, w_in, conv_w,
              norm_out_attn, norm_out_conv, w_out, norm_ffn, w_router_group, b_router_group,
              w_router_expert, b_router_expert, w_gate, w_up, w_down, norm_final):
    B, S, D = x_prompt.shape
    DB, DS, _ = x_sample.shape
    w_buf = cache_k.shape[2]
    w_keep = min(MAX_WINDOW, S)
    hp, hs = x_prompt, x_sample
    kp_l, vp_l, cp_l, ks_l, vs_l, cs_l = [], [], [], [], [], []
    for layer in range(DEPTH):
        qp, kp, vp, bp, up = _mix_in(_rmsnorm(hp, norm_mix[layer]), w_in[layer])
        qs, ks, vs, bs, us = _mix_in(_rmsnorm(hs, norm_mix[layer]), w_in[layer])

        attn_p = _combine([_branch_prompt(qp, kp, vp, d) for d in DILATIONS]).astype(qp.dtype)
        kk = jnp.concatenate([cache_k[layer].astype(ks.dtype), ks], axis=1)
        vv = jnp.concatenate([cache_v[layer].astype(vs.dtype), vs], axis=1)
        attn_s = _combine([_branch_sample(qs, kk, vv, d, w_buf) for d in DILATIONS]).astype(qs.dtype)

        conv_p, st_p = _short_conv(up, jnp.zeros((B, CONV_WIDTH - 1, D_CONV), up.dtype), conv_w[layer])
        conv_s, st_s = _short_conv(us, state_conv[layer], conv_w[layer])

        hp = hp + _mix_out(attn_p, bp * conv_p, norm_out_attn[layer], norm_out_conv[layer], w_out[layer])
        hs = hs + _mix_out(attn_s, bs * conv_s, norm_out_attn[layer], norm_out_conv[layer], w_out[layer])

        tok = jnp.concatenate([_rmsnorm(hp, norm_ffn[layer]).reshape(B * S, D),
                               _rmsnorm(hs, norm_ffn[layer]).reshape(DB * DS, D)], axis=0)
        f = _moe(tok, w_router_group[layer], b_router_group[layer], w_router_expert[layer],
                 b_router_expert[layer], w_gate[layer], w_up[layer], w_down[layer])
        hp = hp + f[:B * S].reshape(B, S, D)
        hs = hs + f[B * S:].reshape(DB, DS, D)

        kp_l.append(kp[:, S - w_keep:])
        vp_l.append(vp[:, S - w_keep:])
        cp_l.append(st_p)
        ks_l.append(ks)
        vs_l.append(vs)
        cs_l.append(st_s)
    y_prompt = _rmsnorm(hp, norm_final)
    y_sample = _rmsnorm(hs, norm_final)
    return (y_prompt, y_sample, jnp.stack(kp_l), jnp.stack(vp_l), jnp.stack(cp_l),
            jnp.stack(ks_l), jnp.stack(vs_l), jnp.stack(cs_l))


_drawn_inputs = setup_inputs


def setup_inputs(seed=0):
    import zlib

    import numpy as np

    out = dict(_drawn_inputs(seed))
    spreads = {}
    factors = {'norm_mix': 2.959,
     'norm_out_attn': 4.3,
     'norm_out_conv': 4.614,
     'norm_ffn': 3.223,
     'b_router_group': 8.0,
     'b_router_expert': 4.92,
     'norm_final': 5.648}
    for name, (base, spread) in spreads.items():
        noise = np.random.default_rng([zlib.crc32(name.encode()), seed]).standard_normal(out[name].shape)
        drawn = base * np.exp(spread * noise) if base else spread * noise
        out[name] = __import__('jax').numpy.asarray(drawn.astype(out[name].dtype))
    for name, factor in factors.items():
        out[name] = (out[name] * factor).astype(out[name].dtype)
    return out
```

```python
from contextlib import ExitStack

import numpy as np

import concourse.bass as bass
from concourse import mybir

F32 = mybir.dt.float32
I32 = mybir.dt.int32
ALU = mybir.AluOpType
ACT = mybir.ActivationFunctionType
X = mybir.AxisListType.X

P = 128
D = 1024
KD = D // P
SEQ = 1024
NS = 8
NTOK = SEQ + NS
NT = SEQ // P + 1
NQ = SEQ // P
H = 8
DH = 64
DA = H * DH
MA = DA // P
DIL = (1, 4, 16)
WIN = 128
WBUF = 2048
CONV = 3
NE = 32
NGRP = 4
EPG = NE // NGRP
DE = 512
SLOTS = 96
MORE = -(-NTOK // SLOTS) - 1
OVER = 2 * NTOK // SLOTS + 1
NBLK = NE + OVER
TC = NTOK // 3
EPS = 1e-6
NEG = -1e30
DROP = 8192.0


def rows(t):
    return P if t < NQ else NS


def constants():
    p = np.arange(P)[:, None]
    c = np.arange(P)[None, :]
    tok = 128 * np.arange(NT)[None, :] + p + 1
    const = np.concatenate([
        (p == c), np.broadcast_to(c, (P, P)), (p < c), np.ones((P, P)),
        tok, tok + NTOK, np.full((P, 1), EPS),
    ], axis=1).astype(np.float32)
    dist = p + (SEQ - P) - np.arange(SEQ)[None, :]
    count = sum(((dist >= 0) & (dist % d == 0) & (dist <= d * WIN)).astype(np.int32) for d in DIL)
    amask = np.where(count > 0, np.log(np.maximum(count, 1)), NEG).astype(np.float32)
    smask = np.full((NS, NS, H), NEG, np.float32)
    smask[np.arange(NS), np.arange(NS)] = np.log(len(DIL))
    return const, amask, smask.reshape(NS, NS * H)


def program(nc, a):
    with ExitStack() as ctx:
        def sb(name, shape, dt=F32):
            return ctx.enter_context(nc.sbuf_tensor(name, shape, dt))

        def sem(name):
            return ctx.enter_context(nc.semaphore(name))

        xres = sb("xres", [P, NT, D])
        wreg = sb("wreg", [P, 2 * 12288])
        hreg = sb("hreg", [P, KD * NTOK])
        ring = sb("ring", [P, 8192])
        cst = sb("cst", [P, 4 * P + 2 * NT + 1])
        gout = sb("gout", [P, KD])
        cw = sb("cw", [P, MA, CONV])
        cstate = sb("cstate", [P, MA, 2, NS])
        uout = sb("uout", [P, MA, NS + 2])
        srow = sb("srow", [NS, 3, DA])
        stat = sb("stat", [P, 96])
        gi_s = sb("gi_s", [SLOTS, 2], I32)
        si_s = sb("si_s", [SLOTS, 2], I32)
        gates = sb("gates", [P, 2, NT])
        gidx = sb("gidx", [SLOTS, NBLK], I32)
        sidx = sb("sidx", [SLOTS, NBLK], I32)
        oexp = sb("oexp", [1, OVER + 1], I32)

        ident, ramp = cst[:, 0:P], cst[:, P:2 * P]
        before, ones = cst[:, 2 * P:3 * P], cst[:, 3 * P:4 * P]
        tokv = cst[:, 4 * P:4 * P + NT]
        destv = cst[:, 4 * P + NT:4 * P + 2 * NT]
        eps = cst[:, 4 * P + 2 * NT:4 * P + 2 * NT + 1]
        epsn = eps[0:NS, :]
        ssq_x, std_x, rst_x = stat[:, 0:9], stat[:, 9:18], stat[:, 18:27]
        mx_n, neg_n = stat[:, 27:30], stat[:, 30:33]
        lsum, rl = stat[:, 33:49], stat[:, 49:65]
        smx, sneg, sl, srl = stat[0:64, 65:66], stat[0:64, 66:67], stat[0:64, 67:68], stat[0:64, 68:69]
        std_ac, rst_ac = stat[:, 70:72], stat[:, 72:74]
        ssq_f, std_f, rst_f = stat[:, 74:76], stat[:, 76:78], stat[:, 78:80]

        def region(r, at, *shape):
            n = int(np.prod(shape))
            v = r[:, at:at + n]
            if len(shape) == 2:
                v = v.rearrange("p (a b) -> p a b", a=shape[0])
            if len(shape) == 3:
                v = v.rearrange("p (a b c) -> p a b c", a=shape[0], b=shape[1])
            return v

        qT = region(wreg, 0, MA, NTOK)
        cT = region(wreg, 4128, MA, NTOK)
        xn = region(wreg, 4128, 2, D)
        gmix = region(wreg, 4128 + 2048, D)
        kn = region(wreg, 4128, NQ, DA)
        u = region(wreg, 8256, NTOK + 2)
        junk = region(wreg, 8256, D)
        cc = region(wreg, 9290, NTOK)
        z = region(wreg, 10322, NTOK)
        kT = region(wreg, 12288, MA, NTOK)
        v = region(wreg, 12288 + 4128, NQ, DA)
        kv = region(wreg, 12288 + 8224, 2, len(DIL) * DA)
        sscore = region(wreg, 12288 + 11296, len(DIL) + 1, NS * H)
        sprob = region(wreg, 12288 + 11552, 3 * P + NS)[0:64, :]
        sprobT = region(wreg, 11354, len(DIL) + 1, NS * H)
        ssm = region(wreg, 11610, NS * H)[0:NS, :]

        hT = region(hreg, 0, KD, NTOK)
        wo = region(hreg, 0, KD, D)
        win = [region(ring, 4096 * s, KD, 512) for s in range(2)]
        wcv = [region(ring, 4096 * s, 3, KD, P) for s in range(2)]
        sm = [region(ring, D * s, D) for s in range(3)]
        pt = [region(ring, 3072 + D * s, D) for s in range(2)]
        amask = region(ring, 5120, SEQ)
        an = [region(ring, 6144 + DA * s, DA) for s in range(2)]
        sq = [region(ring, 1024 * s, 2 * MA, P) for s in range(2)]
        h2 = [region(ring, 2048 + D * s, D) for s in range(2)]
        h2T = [region(ring, 4096 + D * s, KD, P) for s in range(2)]
        gffn = region(ring, 6144, D)
        wr = region(ring, 7168, KD, NGRP + NE)
        lg = region(ring, 7456, NT, NGRP + NE)
        rbias = region(ring, 7780, NGRP + NE)
        xg = [region(hreg, D * s, D)[0:SLOTS, :] for s in range(2)]
        xT = [region(hreg, 2048 + KD * SLOTS * s, KD, SLOTS) for s in range(2)]
        sg = [region(hreg, 3584 + 384 * s, 4, SLOTS) for s in range(2)]
        hid = [region(hreg, 4352 + 384 * s, 4, SLOTS) for s in range(2)]
        ysb = [region(hreg, 5120 + D * s, D)[0:SLOTS, :] for s in range(2)]
        wg = [region(wreg, 12288 * (1 - s), KD, DE) for s in range(2)]
        wu = [region(wreg, 12288 * (1 - s) + 4096, KD, DE) for s in range(2)]
        wd = [region(wreg, 12288 * (1 - s) + 8192, DE // P, D) for s in range(2)]
        yt = [region(ring, 2 * D * s, 2, D) for s in range(2)]
        ot = [region(ring, 4096 + D * s, D) for s in range(2)]
        gfin = region(ring, 6144, D)
        fjunk = region(ring, 7168, D)
        own = region(wreg, 11680, DA)[0:NS, :]

        def rt(at, *shape):
            return region(ring, at, *shape)

        r_gm, r_gi, r_sg, r_pg = (rt(9 * i, NT) for i in range(4))
        r_v1, r_v2, r_i1, r_i2 = (rt(36 + 9 * i, NT) for i in range(4))
        r_vd, r_den, r_t9, r_u9 = (rt(72 + 9 * i, NT) for i in range(4))
        r_e = rt(108, 2, NT)
        r_r = rt(126, 2, NT)
        r_so = rt(144, 2, NT)
        r_q = rt(162, 2, NT)
        r_j = rt(180, 2, NT)
        r_blk = rt(198, 2, NT)
        r_is = rt(216, 2, NT)
        r_ob, r_inc, r_exc = rt(240, NE), rt(272, NE), rt(304, NE)
        r_d, r_eq, r_goh = rt(340, NT, NGRP), rt(380, NT, NGRP), rt(420, NT, NGRP)
        r_le, r_eq8, r_oh, r_le2 = (rt(460 + 72 * i, NT, EPG) for i in range(4))
        r_big = rt(760, NT, NE)
        r_hot1, r_hot2, r_hot = rt(1050, NT, NE), rt(1340, NT, NE), rt(1630, NT, NE)
        r_sum = rt(4096, NT, NE)
        r_rank = rt(4400, NT + 1, NE)
        r_cmp = rt(4730, OVER, NE)
        r_tab = rt(5450, 2, NBLK)
        r_tab2 = rt(5570, NBLK)
        hot_slot = [rt(5640 + 96 * s, SLOTS) for s in range(2)]
        hot_blk = [rt(5840 + 2 * NBLK * s, 2 * NBLK) for s in range(2)]

        psum = ctx.enter_context(nc.psum_tensor("psum", [P, 8 * 512], F32))

        def bank(b, n=1):
            return psum[:, 512 * b:512 * (b + n)]

        h2_d = nc.dram_tensor("h2_rows", [NTOK, D], F32, kind="Internal").ap()
        y_d = nc.dram_tensor("y_rows", [2 * NTOK, D], F32, kind="Internal").ap()

        const_in = sem("const_in")
        gmix_in = sem("gmix_in")
        x_in = [sem(f"x_in{t}") for t in range(NT)]
        win_in = [sem(f"win_in{s}") for s in range(2)]
        kv_in = [sem(f"kv_in{s}") for s in range(2)]
        wo_in = sem("wo_in")
        mask_in = sem("mask_in")
        router_in = sem("router_in")
        act_step = sem("act_step")
        dve_step = sem("dve_step")
        std_ready = sem("std_ready")
        xn_ready = sem("xn_ready")
        group_done = sem("group_done")
        act_emptied = sem("act_emptied")
        dve_emptied = sem("dve_emptied")
        qb_ready = sem("qb_ready")
        scored = sem("scored")
        z_ready = sem("z_ready")
        kn_out = sem("kn_out")
        v_out = sem("v_out")
        u_ready = sem("u_ready")
        sT_ready = sem("sT_ready")
        smax_ready = sem("smax_ready")
        sexp_ready = sem("sexp_ready")
        sp_ready = sem("sp_ready")
        spT_ready = sem("spT_ready")
        spT_copied = sem("spT_copied")
        spv_used = sem("spv_used")
        spv_ready = sem("spv_ready")
        s_attn = sem("s_attn")
        s_ready = sem("s_ready")
        masked = sem("masked")
        exped = sem("exped")
        pT_ready = sem("pT_ready")
        pT_act = sem("pT_act")
        pT_dve = sem("pT_dve")
        pv_done = sem("pv_done")
        an_ready = sem("an_ready")
        aT_ready = sem("aT_ready")
        aT_copied = sem("aT_copied")
        wo_scaled = sem("wo_scaled")
        sq_ready = sem("sq_ready")
        ssq_ready = sem("ssq_ready")
        std_ac_ready = sem("std_ac_ready")
        o_ready = sem("o_ready")
        o_used = sem("o_used")
        std_f_ready = sem("std_f_ready")
        h2_ready = sem("h2_ready")
        h2_out = [sem(f"h2_out{s}") for s in range(2)]
        h2T_ready = sem("h2T_ready")
        h2T_copied = sem("h2T_copied")
        lg_ready = sem("lg_ready")
        lg_used = sem("lg_used")
        gd_ready = sem("gd_ready")
        gexp_ready = sem("gexp_ready")
        vd_ready = sem("vd_ready")
        vexp_ready = sem("vexp_ready")
        assigned = sem("assigned")
        ranked = sem("ranked")
        hot_ready = sem("hot_ready")
        hot_used = sem("hot_used")
        table_ready = sem("table_ready")
        routed = sem("routed")
        all_sent = sem("all_sent")

        class Flow:

            def __init__(self, tag, slots):
                self.gate_in = [sem(f"{tag}_gate_in{s}") for s in range(slots)]
                self.up_in = [sem(f"{tag}_up_in{s}") for s in range(slots)]
                self.down_in = [sem(f"{tag}_down_in{s}") for s in range(slots)]
                self.rows_in = [sem(f"{tag}_rows_in{s}") for s in range(slots)]
                self.sent = [sem(f"{tag}_sent{s}") for s in range(slots)]
                self.xT_ready = sem(f"{tag}_xT_ready")
                self.xT_act = sem(f"{tag}_xT_act")
                self.xT_dve = sem(f"{tag}_xT_dve")
                self.gate_done = sem(f"{tag}_gate_done")
                self.up_done = sem(f"{tag}_up_done")
                self.silu_done = sem(f"{tag}_silu_done")
                self.hid_done = sem(f"{tag}_hid_done")
                self.y_done = sem(f"{tag}_y_done")
                self.y_act = sem(f"{tag}_y_act")
                self.y_dve = sem(f"{tag}_y_dve")
                self.staged = sem(f"{tag}_staged")
                self.held = sem(f"{tag}_held")

        first, further = Flow("first", 2), Flow("further", 1)
        further.y_done = first.y_done
        y_in = [sem(f"y_in{s}") for s in range(2)]
        gfin_in = sem("gfin_in")
        fin_res = sem("fin_res")
        fin_std = sem("fin_std")
        fin_out = sem("fin_out")
        out_sent = [sem(f"out_sent{s}") for s in range(2)]
        out_misc = sem("out_misc")

        groups = []
        for n in range(3):
            groups += [("x", t, h) for t in range(3 * n, 3 * n + 3) for h in range(2)]
            groups += [("q", m, n) for m in range(MA)]
        groups += [("k", m, n) for n in range(3) for m in range(MA)]
        groups += [("rows", 0, 0), ("rows", 1, 0)]
        groups += [("v", i, 0) for i in range(NT)]
        groups += [("kn", i, 0) for i in range(NQ)]
        for m in range(MA):
            for n in range(3):
                groups += [("c", m, n), ("u", m, n)]
            groups += [("b", m, n) for n in range(3)]
        number = {g: i for i, g in enumerate(groups)}
        taker = []
        taken = {"act": 0, "dve": 0}
        for i, g in enumerate(groups):
            e = "act" if g[0] == "c" or (g[0] not in "ub" and i % 2 == 0) else "dve"
            taken[e] += 1
            taker.append((e, taken[e]))
        chunk_of = {"q": 0, "k": 1, "v": 2}
        last_of_chunk = [number["q", MA - 1, 2], number["k", MA - 1, 2], number["v", NQ, 0]] + [
            number["b", m, 2] for m in range(MA)]

        def wait_emptied(eng, g):
            e, n = taker[g]
            eng.wait_ge(act_emptied if e == "act" else dve_emptied, n)

        def group_psum(g):
            return bank(g % 4)

        NSTEP = NQ * H

        block = ctx.enter_context(nc.Block())

        @block.sync
        def _(sp):
            sp.dma_start(cst[:], a["const"]).then_inc(const_in, 16)
            sp.dma_start(xres[:, 0, :], a["x_prompt"][0:P, :]).then_inc(x_in[0], 16)
            sp.dma_start(gmix, a["norm_mix"].partition_broadcast(P)).then_inc(gmix_in, 16)
            for t in range(1, NQ):
                sp.dma_start(xres[:, t, :], a["x_prompt"][t * P:(t + 1) * P, :]).then_inc(x_in[t], 16)
                if t == 2:
                    sp.dma_start(win[0], a["w_in"][:, 0:512].rearrange("(k p) n -> p k n", p=P)).then_inc(win_in[0], 16)
            sp.dma_start(xres[0:NS, NQ, :], a["x_sample"]).then_inc(x_in[NQ], 16)
            sp.dma_start(gout[:], a["gain_out"]).then_inc(const_in, 16)
            sp.dma_start(cw[:], a["conv_w"]).then_inc(const_in, 16)
            sp.dma_start(cstate[:], a["conv_state"]).then_inc(const_in, 16)
            sp.dma_start(ssm, a["smask"]).then_inc(const_in, 16)
            sp.dma_start(a["conv_sample_old"], a["state_conv"][:, 1, :]).then_inc(out_misc, 16)

            def load_kv(n):
                b, src = n % NS, a["cache_k"] if n < NS else a["cache_v"]
                if 2 <= n < NS + 2:
                    sp.wait_ge(scored, n - 1)
                elif n >= NS + 2:
                    sp.wait_ge(spv_used, n - NS - 1)
                for r, d in enumerate(DIL):
                    at = WBUF - d * WIN
                    keys = src[b, at:WBUF, :].rearrange("(j d) c -> j d c", d=d)[:, 0, :]
                    sp.dma_start(kv[:, n % 2, r * DA:(r + 1) * DA], keys).then_inc(kv_in[n % 2], 16)

            def load_win(c):
                if c >= 2:
                    sp.wait_ge(group_done, last_of_chunk[c - 2] + 1)
                if c < 3:
                    sp.dma_start(win[c % 2], a["w_in"][:, 512 * c:512 * (c + 1)].rearrange("(k p) n -> p k n", p=P)
                                 ).then_inc(win_in[c % 2], 16)
                else:
                    for j in range(3):
                        at = (3 + j) * 512 + (c - 3) * P
                        sp.dma_start(wcv[c % 2][:, j], a["w_in"][:, at:at + P].rearrange("(k p) n -> p k n", p=P)
                                     ).then_inc(win_in[c % 2], 16)

            load_win(1)
            load_win(2)
            load_kv(0)
            load_kv(1)
            load_win(3)
            for n in range(2, NS):
                load_kv(n)
            load_kv(NS)
            load_kv(NS + 1)
            for i in range(NT):
                wait_emptied(sp, number["v", i, 0])
            sp.dma_start(a["v_prompt"].rearrange("(t p) c -> p t c", p=P), v).then_inc(v_out, 16)
            for i in range(2):
                wait_emptied(sp, number["rows", i, 0])
            sp.dma_start(a["k_sample"], srow[:, 1, :]).then_inc(out_misc, 16)
            sp.dma_start(a["v_sample"], srow[:, 2, :]).then_inc(out_misc, 16)
            load_win(4)
            for i in range(NQ):
                wait_emptied(sp, number["kn", i, 0])
            sp.dma_start(a["k_prompt"].rearrange("(t p) c -> p t c", p=P), kn).then_inc(kn_out, 16)
            load_win(5)
            load_win(6)
            for n in range(NS + 2, 2 * NS):
                load_kv(n)
            sp.wait_ge(group_done, len(groups))
            sp.dma_start(amask, a["amask"]).then_inc(mask_in, 16)
            sp.dma_start(wo, a["w_out"].rearrange("(k p) n -> p k n", p=P)).then_inc(wo_in, 16)
            sp.wait_ge(u_ready, MA)
            sp.dma_start(a["conv_u"], uout[:]).then_inc(out_misc, 16)
            sp.wait_ge(aT_ready, NQ)
            sp.wait_ge(masked, NSTEP)
            sp.dma_start(gffn, a["norm_ffn"].partition_broadcast(P)).then_inc(router_in, 16)
            sp.dma_start(wr, a["w_router"]).then_inc(router_in, 16)
            sp.dma_start(rbias, a["b_router"].partition_broadcast(P)).then_inc(router_in, 16)
            sp.wait_ge(v_out, 16)

            def load_gate(f, s, e):
                sp.dma_start(wg[s], a["w_gate"][e].rearrange("(k p) n -> p k n", p=P)).then_inc(f.gate_in[s], 16)

            def load_up(f, s, e):
                sp.dma_start(wu[s], a["w_up"][e].rearrange("(k p) n -> p k n", p=P)).then_inc(f.up_in[s], 16)

            def load_down(f, s, e):
                sp.dma_start(wd[s], a["w_down"][e].rearrange("(k p) n -> p k n", p=P)).then_inc(f.down_in[s], 16)

            load_gate(first, 0, 0)
            load_up(first, 0, 0)
            load_down(first, 0, 0)

            def store_h2(t):
                sp.wait_ge(h2_ready, t + 1)
                sp.dma_start(h2_d[P * t:P * t + rows(t), :], h2[t % 2][0:rows(t), :]).then_inc(h2_out[t % 2], 16)

            for t in range(NT):
                store_h2(t)
            sp.wait_ge(o_ready, 4 * NT)
            load_gate(first, 1, 1)
            load_up(first, 1, 1)
            load_down(first, 1, 1)

            with sp.Fori(0, NE // 2 - 1, 1) as j:
                for s in range(2):
                    e = sp.snap(2 * j + (s + 2))
                    sp.wait_ge(first.gate_done, 2 * j + (s + 1))
                    sp.dma_start(wg[s], a["w_gate_flat"][bass.ds(e * D, D), :].rearrange("(k p) n -> p k n", p=P)
                                 ).then_inc(first.gate_in[s], 16)
                    sp.wait_ge(first.up_done, 2 * j + (s + 1))
                    sp.dma_start(wu[s], a["w_up_flat"][bass.ds(e * D, D), :].rearrange("(k p) n -> p k n", p=P)
                                 ).then_inc(first.up_in[s], 16)
                    sp.wait_ge(first.y_done, 2 * j + (s + 1))
                    sp.dma_start(wd[s], a["w_down_flat"][bass.ds(e * DE, DE), :].rearrange("(k p) n -> p k n", p=P)
                                 ).then_inc(first.down_in[s], 16)
            sp.wait_ge(first.y_done, NE)
            more = sp.value_load(oexp[0:1, OVER:OVER + 1], min_val=0, max_val=OVER)
            with sp.If(more > 0):
                with sp.Fori(0, more, 1) as o:
                    e = sp.value_load(oexp[0:1, bass.ds(o, 1)], min_val=0, max_val=NE - 1)
                    sp.wait_ge(first.y_done, o + NE)
                    sp.dma_start(wg[0], a["w_gate_flat"][bass.ds(e * D, D), :].rearrange("(k p) n -> p k n", p=P)
                                 ).then_inc(further.gate_in[0], 16)
                    sp.dma_start(wu[0], a["w_up_flat"][bass.ds(e * D, D), :].rearrange("(k p) n -> p k n", p=P)
                                 ).then_inc(further.up_in[0], 16)
                    sp.dma_start(wd[0], a["w_down_flat"][bass.ds(e * DE, DE), :].rearrange("(k p) n -> p k n", p=P)
                                 ).then_inc(further.down_in[0], 16)
            sp.dma_start(gfin, a["norm_final"].partition_broadcast(P)).then_inc(gfin_in, 16)
            sp.wait_ge(all_sent, 1)

            def load_y(t):
                if t >= 2:
                    sp.wait_ge(fin_res, t - 1)
                n = rows(t)
                for c in range(2):
                    at = c * NTOK + P * t
                    sp.dma_start(yt[t % 2][0:n, c, :], y_d[at:at + n, :]).then_inc(y_in[t % 2], 16)

            load_y(0)
            load_y(1)
            for t in range(NT):
                if t + 2 < NT:
                    load_y(t + 2)
                sp.wait_ge(fin_out, t + 1)
                dst = a["y_prompt"][P * t:P * (t + 1), :] if t < NQ else a["y_sample"]
                sp.dma_start(dst, ot[t % 2][0:rows(t), :]).then_inc(out_sent[t % 2], 16)
            sp.wait_ge(out_sent[0], 16 * 5)
            sp.wait_ge(out_sent[1], 16 * 4)
            sp.wait_ge(out_misc, 16 * 4)
            sp.wait_ge(kn_out, 16)

        @block.tensor
        def _(pe):
            mm = nc.tensor.matmul
            pe.wait_ge(const_in, 16)

            def proj(g):
                kind, i, n = groups[g]
                if g >= 4:
                    wait_emptied(pe, g - 4)
                ps = group_psum(g)
                if kind == "x":
                    w = rows(i)
                    pe.wait_ge(xn_ready, i + 1)
                    for c in range(4):
                        k = 4 * n + c
                        ins = nc.tensor.transpose(ps[:, c * w:(c + 1) * w], xn[0:w, i % 2, k * P:(k + 1) * P],
                                                  ident[0:w, 0:w])
                elif kind in ("q", "k"):
                    c = chunk_of[kind]
                    if n == 0 and i == 0:
                        pe.wait_ge(win_in[c % 2], 16)
                    if kind == "q" and i == 0:
                        for t in range(3 * n, 3 * n + 3):
                            for h in range(2):
                                wait_emptied(pe, number["x", t, h])
                    for k in range(KD):
                        ins = mm(ps[:, 0:TC], win[c % 2][:, k, i * P:(i + 1) * P], hT[:, k, n * TC:(n + 1) * TC],
                                 start=(k == 0), stop=(k == KD - 1))
                elif kind == "rows":
                    for m in range(MA):
                        wait_emptied(pe, number["q" if i == 0 else "k", m, 2])
                    for m in range(MA):
                        ins = nc.tensor.transpose(ps[0:NS, m * P:(m + 1) * P],
                                                  (qT if i == 0 else kT)[:, m, SEQ:NTOK], ident)
                elif kind == "v":
                    w = rows(i)
                    if i == 0:
                        pe.wait_ge(win_in[0], 32)
                    for k in range(KD):
                        ins = mm(ps[0:w, :], hT[:, k, i * P:i * P + w], win[0][:, k, :],
                                 start=(k == 0), stop=(k == KD - 1))
                elif kind == "kn":
                    for m in range(MA):
                        ins = nc.tensor.transpose(ps[:, m * P:(m + 1) * P], kT[:, m, i * P:(i + 1) * P], ident)
                else:
                    c = 3 + i
                    if n == 0 and kind == "c":
                        pe.wait_ge(win_in[c % 2], (32 if c % 2 == 0 else 16) + 48 * ((i + 2 - c % 2) // 2 if c % 2 == 0 else i // 2 + 1))
                    j = {"b": 0, "c": 1, "u": 2}[kind]
                    for k in range(KD):
                        ins = mm(ps[:, 0:TC], wcv[c % 2][:, j, k, :], hT[:, k, n * TC:(n + 1) * TC],
                                 start=(k == 0), stop=(k == KD - 1))
                ins.then_inc(group_done, 1)

            def query_all_partitions(b):
                if b == 0:
                    wait_emptied(pe, number["rows", 0, 0])
                if b >= 2:
                    pe.wait_ge(scored, b - 1)
                mm(bank(4 + b % 2), ident[0:NS, b:b + 1].broadcast_to([NS, P]), srow[:, 0, :],
                   start=True, stop=True).then_inc(qb_ready, 1)

            def sample_scores_turned():
                pe.wait_ge(scored, NS)
                ps = bank(6)[0:64, :]
                for r in range(3):
                    nc.tensor.transpose(ps[:, r * P:(r + 1) * P], sscore[:, r, :], ident)
                nc.tensor.transpose(ps[:, 3 * P:3 * P + NS], sscore[0:NS, 3, :], ident[0:NS, 0:NS]
                                    ).then_inc(sT_ready, 1)

            def sample_probs_turned():
                pe.wait_ge(sp_ready, 1)
                ps = bank(7)
                for r in range(3):
                    nc.tensor.transpose(ps[:, r * 64:(r + 1) * 64], sprob[:, r * P:(r + 1) * P], ident[0:64, 0:64])
                nc.tensor.transpose(ps[0:NS, 192:256], sprob[:, 3 * P:3 * P + NS], ident[0:64, 0:64]
                                    ).then_inc(spT_ready, 1)

            def sample_values():
                pe.wait_ge(spT_copied, 1)
                out = bank(4).rearrange("p (m c) -> p m c", m=8)
                for m in range(MA):
                    mm(out[:, m, :], srow[:, 2, m * P:(m + 1) * P], sprobT[0:NS, 3, :],
                       start=(m == 0), stop=False, skip_group_check=True)
                for b in range(NS):
                    n = NS + b
                    pe.wait_ge(kv_in[n % 2], 48 * (n // 2 + 1))
                    for r in range(3):
                        for m in range(MA):
                            ins = mm(out[:, m, b * H:(b + 1) * H], kv[:, n % 2, r * DA + m * P:r * DA + (m + 1) * P],
                                     sprobT[:, r, b * H:(b + 1) * H], start=False, stop=(r == 2),
                                     skip_group_check=True)
                    if b < NS - 1:
                        ins.then_inc(spv_used, 1)
                    else:
                        ins.then_inc(spv_ready, 1)

            for g, (kind, i, n) in enumerate(groups):
                proj(g)
                if kind == "v" and i < NS:
                    query_all_partitions(i)
                if kind == "b" and n == 2:
                    if i == 0:
                        sample_scores_turned()
                    if i == 1:
                        sample_probs_turned()
                    if i == 2:
                        sample_values()

            def scores(n):
                i, h = divmod(n, H)
                m, lo = h // 2, DH * (h % 2)
                if n >= 2:
                    pe.wait_ge(masked, n - 1)
                ps = bank(2 * (n % 2), 2)
                width = (i + 1) * P
                for at in range(0, width, 512):
                    w = min(512, width - at)
                    ins = mm(ps[:, at:at + w], qT[lo:lo + DH, m, i * P:(i + 1) * P], kT[lo:lo + DH, m, at:at + w],
                             start=True, stop=True)
                ins.then_inc(s_ready, 1)

            def pT_wait(n):
                if n % 3 == 0:
                    pe.wait_ge(pT_dve, n // 3 + 1)
                else:
                    pe.wait_ge(pT_act, n - n // 3)

            def turn_probs(n):
                i = n // H
                pe.wait_ge(exped, n + 1)
                if n >= 1:
                    pT_wait(n - 1)
                ps = bank(4, 2)
                for j in range(i + 1):
                    ins = nc.tensor.transpose(ps[:, j * P:(j + 1) * P], sm[n % 3][:, j * P:(j + 1) * P], ident)
                ins.then_inc(pT_ready, 1)

            def weigh_values(n):
                i, h = divmod(n, H)
                pT_wait(n)
                if h == 0 and i >= 2:
                    pe.wait_ge(aT_copied, i - 1)
                acc = bank(6 + i % 2)
                for j in range(i + 1):
                    ins = mm(acc[:, h * DH:(h + 1) * DH], pt[n % 2][:, j * P:(j + 1) * P], v[:, j, h * DH:(h + 1) * DH],
                             start=(j == 0), stop=(j == i))
                ins.then_inc(pv_done, 1)

            def turn_attention(i):
                pe.wait_ge(an_ready, i + 1)
                ps = bank(6 + i % 2)
                for m in range(MA):
                    ins = nc.tensor.transpose(ps[:, m * P:(m + 1) * P], an[i % 2][:, m * P:(m + 1) * P], ident)
                ins.then_inc(aT_ready, 1)

            for g in range(len(groups) - 4, len(groups)):
                wait_emptied(pe, g)
            pe.wait_ge(s_attn, 1)
            for n in range(NSTEP + 6):
                if n < NSTEP:
                    scores(n)
                if 3 <= n < NSTEP + 3:
                    weigh_values(n - 3)
                if 2 <= n < NSTEP + 2:
                    turn_probs(n - 2)
                if n >= H + 5 and (n - 5) % H == 0:
                    turn_attention((n - 5) // H - 1)

            def project(t):
                w = rows(t)
                if t == 0:
                    pe.wait_ge(wo_scaled, 1)
                    pe.wait_ge(aT_copied, NQ)
                pe.wait_ge(sq_ready, t + 1)
                if t:
                    pe.wait_ge(std_ac_ready, t)
                for c in range(2):
                    for m in range(MA):
                        ins = mm(bank(6)[0:w, 2 * t + c:2 * t + c + 1], sq[t % 2][:, c * MA + m, 0:w],
                                 ones[:, 0:1], start=(m == 0), stop=(m == MA - 1))
                ins.then_inc(ssq_ready, 1)
                for half in range(2):
                    for c in range(2):
                        g = 4 * t + 2 * half + c
                        if g >= 4:
                            pe.wait_ge(o_used, g - 3)
                        for m in range(MA):
                            src = (qT, cT)[c]
                            ins = mm(bank(2 * half + c)[0:w, :], src[:, m, t * P:t * P + w],
                                     wo[:, c * MA + m, half * 512:(half + 1) * 512],
                                     start=(m == 0), stop=(m == MA - 1))
                        ins.then_inc(o_ready, 1)

            def route(t):
                w = rows(t)
                pe.wait_ge(h2_ready, t + 1)
                if t == 0:
                    pe.wait_ge(router_in, 48)
                for half in range(2):
                    if t >= 1:
                        pe.wait_ge(h2T_copied, 2 * t)
                    for c in range(4):
                        k = 4 * half + c
                        ins = nc.tensor.transpose(bank(4 + half)[:, c * w:(c + 1) * w],
                                                  h2[t % 2][0:w, k * P:(k + 1) * P], ident[0:w, 0:w])
                    ins.then_inc(h2T_ready, 1)
                pe.wait_ge(h2T_copied, 2 * t + 2)
                if t:
                    pe.wait_ge(lg_used, t)
                NR = NGRP + NE
                for k in range(KD):
                    ins = mm(bank(7)[0:w, t * NR:(t + 1) * NR], h2T[t % 2][:, k, 0:w], wr[:, k, :],
                             start=(k == 0), stop=(k == KD - 1))
                ins.then_inc(lg_ready, 1)

            for t in range(NT + 1):
                if t < NT:
                    project(t)
                if t >= 1:
                    route(t - 1)

            pe.wait_ge(assigned, 1)
            pe.wait_ge(o_used, 4 * NT)
            for t in range(NT):
                w = rows(t)
                if t:
                    mm(bank(0)[0:w, t * NE:(t + 1) * NE], ones[:, 0:w], r_sum[:, t, :], start=True, stop=False)
                mm(bank(0)[0:w, t * NE:(t + 1) * NE], before[0:w, 0:w], r_hot[0:w, t, :], start=(t == 0), stop=True)
            mm(bank(0)[:, NT * NE:(NT + 1) * NE], ones, r_sum[:, NQ, :], start=True, stop=False)
            mm(bank(0)[:, NT * NE:(NT + 1) * NE], ones[0:NS, :], r_hot[0:NS, NQ, :], start=False, stop=True
               ).then_inc(ranked, 1)
            for n in range(2 * NT):
                w = rows(n // 2)
                pe.wait_ge(hot_ready, n + 1)
                ins = mm(bank(1)[0:SLOTS, 0:2 * NBLK], hot_slot[n % 2][0:w, :], hot_blk[n % 2][0:w, :],
                         start=(n == 0), stop=(n == 2 * NT - 1))
                ins.then_inc(hot_used, 1)

            def turn_rows(f, s, n):
                for k in range(KD):
                    ins = nc.tensor.transpose(bank(4 + k // 4)[:, (k % 4) * SLOTS:(k % 4 + 1) * SLOTS],
                                              xg[s][:, k * P:(k + 1) * P], ident[0:SLOTS, 0:SLOTS])
                    if k % 4 == 3:
                        ins.then_inc(f.xT_ready, 1)

            def gate_or_up(w, s, b, done):
                for m in range(DE // P):
                    for k in range(KD):
                        ins = mm(bank(b)[:, m * SLOTS:(m + 1) * SLOTS], w[s][:, k, m * P:(m + 1) * P], xT[s][:, k, :],
                                 start=(k == 0), stop=(k == KD - 1))
                ins.then_inc(done, 1)

            def down(f, s):
                for half in range(2):
                    for m in range(DE // P):
                        ins = mm(bank(2 + half)[0:SLOTS, :], hid[s][:, m, :], wd[s][:, m, half * 512:(half + 1) * 512],
                                 start=(m == 0), stop=(m == DE // P - 1))
                ins.then_inc(f.y_done, 1)

            def expert(b, turns, s, turn_next, next_turns):
                pe.wait_ge(first.xT_act, b + 1)
                pe.wait_ge(first.xT_dve, b + 1)
                pe.wait_ge(first.gate_in[s], 16 * turns + 16)
                gate_or_up(wg, s, 0, first.gate_done)
                pe.wait_ge(first.up_in[s], 16 * turns + 16)
                gate_or_up(wu, s, 1, first.up_done)
                if turn_next:
                    pe.wait_ge(first.rows_in[1 - s], 16 * next_turns + 16)
                    turn_rows(first, 1 - s, b + 1)
                pe.wait_ge(first.down_in[s], 16 * turns + 16)
                pe.wait_ge(first.hid_done, b + 1)
                if not isinstance(b, int) or b > 0:
                    pe.wait_ge(first.y_act, b)
                    pe.wait_ge(first.y_dve, b)
                down(first, s)

            pe.wait_ge(routed, 1)
            pe.wait_ge(first.rows_in[0], 16)
            turn_rows(first, 0, 0)
            expert(0, 0, 0, True, 0)
            expert(1, 0, 1, True, 1)
            with pe.Fori(1, NE // 2 - 1, 1) as j:
                expert(2 * j, j, 0, True, j)
                expert(2 * j + 1, j, 1, True, j + 1)
            expert(NE - 2, NE // 2 - 1, 0, True, NE // 2 - 1)
            expert(NE - 1, NE // 2 - 1, 1, False, 0)
            pe.wait_ge(first.y_act, NE)
            pe.wait_ge(first.y_dve, NE)
            more = pe.value_load(oexp[0:1, OVER:OVER + 1], min_val=0, max_val=OVER)
            with pe.If(more > 0):
                with pe.Fori(0, more, 1) as o:
                    pe.wait_ge(further.rows_in[0], 16 * o + 16)
                    turn_rows(further, 0, o)
                    pe.wait_ge(further.xT_act, o + 1)
                    pe.wait_ge(further.xT_dve, o + 1)
                    pe.wait_ge(further.gate_in[0], 16 * o + 16)
                    gate_or_up(wg, 0, 0, further.gate_done)
                    pe.wait_ge(further.up_in[0], 16 * o + 16)
                    gate_or_up(wu, 0, 1, further.up_done)
                    pe.wait_ge(further.down_in[0], 16 * o + 16)
                    pe.wait_ge(further.hid_done, o + 1)
                    down(further, 0)
                    pe.wait_ge(further.y_act, o + 1)
                    pe.wait_ge(further.y_dve, o + 1)

        def unload_group(eng, copy, g):
            kind, i, n = groups[g]
            ps = group_psum(g)
            if kind == "x":
                w = rows(i)
                return copy(hT[:, 4 * n:4 * n + 4, i * P:i * P + w],
                            ps[:, 0:4 * w].rearrange("p (k t) -> p k t", k=4))
            if kind == "k":
                return copy(kT[:, i, n * TC:(n + 1) * TC], ps[:, 0:TC])
            if kind == "rows":
                return copy(srow[:, i, :], ps[0:NS, :])
            if kind == "v":
                return copy(v[:, i, :] if i < NQ else srow[:, 2, :], ps[0:rows(i), :])
            if kind == "kn":
                return copy(kn[:, i, :], ps[:, :])

        @block.scalar
        def _(act):
            steps = [0]

            def step(ins):
                steps[0] += 1
                ins.then_inc(act_step, 1)
                act.wait_ge(act_step, steps[0])

            def square_sum(t):
                w = rows(t)
                act.wait_ge(x_in[t], 16)
                step(nc.scalar.activation(junk[0:w, :], xres[0:w, t, :], ACT.Square, accum_out=ssq_x[0:w, t:t + 1]))
                nc.scalar.activation(std_x[0:w, t:t + 1], ssq_x[0:w, t:t + 1], ACT.Sqrt, bias=eps[0:w, :],
                                     scale=1.0 / D).then_inc(std_ready, 1)

            act.wait_ge(const_in, 16)
            square_sum(0)
            square_sum(1)
            for g, (kind, i, n) in enumerate(groups):
                if taker[g][0] != "act":
                    continue
                act.wait_ge(group_done, g + 1)
                if kind == "q":
                    ins = nc.scalar.mul(qT[:, i, n * TC:(n + 1) * TC], group_psum(g)[:, 0:TC], DH ** -0.5)
                elif kind == "c":
                    if i >= 1:
                        wait_emptied(act, number["u", i - 1, n])
                    ins = nc.scalar.copy(cc[:, n * TC:(n + 1) * TC], group_psum(g)[:, 0:TC])
                else:
                    if kind == "kn" and i < 2:
                        act.wait_ge(group_done, number["x", NT - 1, 1] + 1)
                    ins = unload_group(act, nc.scalar.copy, g)
                ins.then_inc(act_emptied, 1)
                if kind == "x" and i + 2 < NT:
                    square_sum(i + 2)
                if kind == "c" and i == 1 and n == 0:
                    act.wait_ge(smax_ready, 1)
                    nc.scalar.activation(sprob, bank(6)[0:64, 0:3 * P + NS], ACT.Exp, bias=sneg,
                                         accum_out=sl).then_inc(sexp_ready, 1)
                if kind == "c" and i == 2 and n == 0:
                    act.wait_ge(spT_ready, 1)
                    nc.scalar.copy(sprobT[0:NS, 3, :], bank(7)[0:NS, 192:256])
                    nc.scalar.copy(sprobT[:, 0:3, :], bank(7)[:, 0:192].rearrange("p (r c) -> p r c", r=3)
                                   ).then_inc(spT_copied, 1)

            def copy_pT(n):
                w = (n // H + 1) * P
                act.wait_ge(pT_ready, n + 1)
                if n >= 2:
                    act.wait_ge(pv_done, n - 1)
                nc.scalar.copy(pt[n % 2][:, 0:w], bank(4, 2)[:, 0:w]).then_inc(pT_act, 1)

            def exponent(n):
                i, h = divmod(n, H)
                w = (i + 1) * P
                act.wait_ge(masked, n + 1)
                if h == 0 and i >= 2:
                    act.wait_ge(an_ready, i - 1)
                c = (i % 2) * H + h
                nc.scalar.activation(sm[n % 3][:, 0:w], sm[n % 3][:, 0:w], ACT.Exp, bias=neg_n[:, n % 3:n % 3 + 1],
                                     accum_out=lsum[:, c:c + 1]).then_inc(exped, 1)

            def copy_aT(i):
                act.wait_ge(aT_ready, i + 1)
                nc.scalar.copy(qT[:, :, i * P:(i + 1) * P], bank(6 + i % 2).rearrange("p (m t) -> p m t", m=MA)
                               ).then_inc(aT_copied, 1)

            for n in range(NSTEP + 6):
                if 2 <= n < NSTEP + 2 and (n - 2) % 3:
                    copy_pT(n - 2)
                if n < NSTEP:
                    exponent(n)
                if n >= H + 5 and (n - 5) % H == 0:
                    copy_aT((n - 5) // H - 1)

            def squares(t):
                w = rows(t)
                if t == 0:
                    act.wait_ge(pT_ready, NSTEP)
                    act.wait_ge(pv_done, NSTEP)
                if t == NQ:
                    act.wait_ge(s_attn, 1)
                if t >= 2:
                    act.wait_ge(ssq_ready, t - 1)
                nc.scalar.activation(sq[t % 2][:, 0:MA, 0:w], qT[:, :, t * P:t * P + w], ACT.Square)
                nc.scalar.activation(sq[t % 2][:, MA:2 * MA, 0:w], cT[:, :, t * P:t * P + w], ACT.Square
                                     ).then_inc(sq_ready, 1)

            def roots(t):
                w = rows(t)
                act.wait_ge(ssq_ready, t + 1)
                if t >= 1:
                    act.wait_ge(o_used, 4 * t)
                nc.scalar.activation(std_ac[0:w, :], bank(6)[0:w, 2 * t:2 * t + 2], ACT.Sqrt, bias=eps[0:w, :],
                                     scale=1.0 / DA).then_inc(std_ac_ready, 1)

            def root_ffn(t):
                w = rows(t)
                act.wait_ge(o_used, 4 * t + 4)
                if t >= 2:
                    act.wait_ge(h2T_ready, 2 * (t - 1))
                    act.wait_ge(h2_out[t % 2], 16 * (t // 2))
                c = t % 2
                step(nc.scalar.activation(h2[c][0:w, :], xres[0:w, t, :], ACT.Square, accum_out=ssq_f[0:w, c:c + 1]))
                nc.scalar.activation(std_f[0:w, c:c + 1], ssq_f[0:w, c:c + 1], ACT.Sqrt, bias=eps[0:w, :],
                                     scale=1.0 / D).then_inc(std_f_ready, 1)

            def copy_h2T(t):
                w = rows(t)
                for half in range(2):
                    act.wait_ge(h2T_ready, 2 * t + half + 1)
                    if t >= 2:
                        act.wait_ge(lg_ready, t - 1)
                    nc.scalar.copy(h2T[t % 2][:, 4 * half:4 * half + 4, 0:w],
                                   bank(4 + half)[:, 0:4 * w].rearrange("p (k t) -> p k t", k=4)
                                   ).then_inc(h2T_copied, 1)

            squares(0)
            for t in range(NT):
                if t + 1 < NT:
                    squares(t + 1)
                roots(t)
                root_ffn(t)
                copy_h2T(t)
            act.wait_ge(gd_ready, 1)
            nc.scalar.activation(r_d, r_d, ACT.Exp).then_inc(gexp_ready, 1)
            act.wait_ge(vd_ready, 1)
            nc.scalar.activation(r_vd, r_vd, ACT.Exp).then_inc(vexp_ready, 1)

            def copy_xT(f, s, n):
                act.wait_ge(f.xT_ready, 2 * n + 1)
                nc.scalar.copy(xT[s][:, 0:4, :], bank(4)[:, 0:4 * SLOTS].rearrange("p (k t) -> p k t", k=4)
                               ).then_inc(f.xT_act, 1)

            def silu(f, s, n):
                act.wait_ge(f.gate_done, n + 1)
                nc.scalar.activation(sg[s], bank(0)[:, 0:4 * SLOTS].rearrange("p (m t) -> p m t", m=4), ACT.Silu
                                     ).then_inc(f.silu_done, 1)

            def copy_y(f, s, n, before=0):
                act.wait_ge(f.y_done, n + (before + 1))
                nc.scalar.copy(ysb[s][:, 0:512], bank(2)[0:SLOTS, :]).then_inc(f.y_act, 1)

            def expert(b, turns, s, turn_next, reused):
                silu(first, s, b)
                if turn_next:
                    copy_xT(first, 1 - s, b + 1)
                if reused:
                    act.wait_ge(first.sent[s], 16 * turns)
                copy_y(first, s, b)

            copy_xT(first, 0, 0)
            expert(0, 0, 0, True, False)
            expert(1, 0, 1, True, False)
            with act.Fori(1, NE // 2 - 1, 1) as j:
                expert(2 * j, j, 0, True, True)
                expert(2 * j + 1, j, 1, True, True)
            expert(NE - 2, NE // 2 - 1, 0, True, True)
            expert(NE - 1, NE // 2 - 1, 1, False, True)
            act.wait_ge(first.sent[0], 16 * (NE // 2))
            more = act.value_load(oexp[0:1, OVER:OVER + 1], min_val=0, max_val=OVER)
            with act.If(more > 0):
                with act.Fori(0, more, 1) as o:
                    copy_xT(further, 0, o)
                    silu(further, 0, o)
                    copy_y(further, 0, o, NE)
                    act.wait_ge(further.sent[0], 16 * o + 16)

            for t in range(NT):
                w = rows(t)
                act.wait_ge(fin_res, t + 1)
                c = t % 2
                step(nc.scalar.activation(fjunk[0:w, :], xres[0:w, t, :], ACT.Square, accum_out=ssq_f[0:w, c:c + 1]))
                if t >= 2:
                    act.wait_ge(fin_out, t - 1)
                nc.scalar.activation(std_f[0:w, c:c + 1], ssq_f[0:w, c:c + 1], ACT.Sqrt, bias=eps[0:w, :],
                                     scale=1.0 / D).then_inc(fin_std, 1)

        @block.vector
        def _(dve):
            vec = nc.vector
            steps = [0]

            def step(ins):
                steps[0] += 1
                ins.then_inc(dve_step, 1)
                dve.wait_ge(dve_step, steps[0])

            def normalise(t):
                w = rows(t)
                dve.wait_ge(std_ready, t + 1)
                step(vec.reciprocal(rst_x[0:w, t:t + 1], std_x[0:w, t:t + 1]))
                if t >= 2:
                    dve.wait_ge(group_done, number["x", t - 2, 1] + 1)
                vec.scalar_tensor_tensor(out=xn[0:w, t % 2, :], in0=xres[0:w, t, :], scalar=rst_x[0:w, t:t + 1],
                                         in1=gmix[0:w, :], op0=ALU.mult, op1=ALU.mult).then_inc(xn_ready, 1)

            def sample_scores(b):
                dve.wait_ge(kv_in[b % 2], 48 * (b // 2 + 1))
                dve.wait_ge(qb_ready, b + 1)
                q = bank(4 + b % 2)
                for r in range(3):
                    keys = kv[:, b % 2, r * DA:(r + 1) * DA]
                    step(vec.tensor_tensor(keys, keys, q, ALU.mult))
                    vec.tensor_reduce(sscore[:, r, b * H:(b + 1) * H], keys.rearrange("p (h d) -> p h d", h=H),
                                      X, ALU.add)
                step(vec.tensor_tensor(own, srow[:, 1, :], q[0:NS, :], ALU.mult))
                cols = slice(b * H, (b + 1) * H)
                step(vec.tensor_reduce(sscore[0:NS, 3, cols], own.rearrange("p (h d) -> p h d", h=H), X, ALU.add))
                vec.tensor_tensor(sscore[0:NS, 3, cols], sscore[0:NS, 3, cols], ssm[:, cols], ALU.add
                                  ).then_inc(scored, 1)

            def conv(m):
                step(vec.tensor_scalar(z[:, 0:SEQ], u[:, 0:SEQ], cw[:, m, 0:1], None, ALU.mult))
                for j in (1, 2):
                    step(vec.scalar_tensor_tensor(out=z[:, 0:SEQ], in0=u[:, j:j + SEQ], scalar=cw[:, m, j:j + 1],
                                                  in1=z[:, 0:SEQ], op0=ALU.mult, op1=ALU.add))
                zs = z[:, SEQ:NTOK]
                step(vec.tensor_scalar(zs, cstate[:, m, 0, :], cw[:, m, 0:1], None, ALU.mult))
                for j in (1, 2):
                    src = cstate[:, m, 1, :] if j == 1 else u[:, SEQ + 2:NTOK + 2]
                    step(vec.scalar_tensor_tensor(out=zs, in0=src, scalar=cw[:, m, j:j + 1], in1=zs,
                                                  op0=ALU.mult, op1=ALU.add))
                vec.tensor_copy(uout[:, m, :], u[:, SEQ:NTOK + 2]).then_inc(u_ready, 1)

            dve.wait_ge(const_in, 16 * 5)
            dve.wait_ge(gmix_in, 16)
            normalise(0)
            normalise(1)
            for g, (kind, i, n) in enumerate(groups):
                if taker[g][0] != "dve":
                    if kind == "v" and i < NS:
                        sample_scores(i)
                    continue
                dve.wait_ge(group_done, g + 1)
                ps = group_psum(g)
                if kind == "q":
                    ins = vec.tensor_scalar(qT[:, i, n * TC:(n + 1) * TC], ps[:, 0:TC], DH ** -0.5, None, ALU.mult)
                elif kind == "u":
                    if i == 0 and n == 0:
                        step(vec.memset(u[:, 0:2], 0.0))
                    wait_emptied(dve, number["c", i, n])
                    ins = vec.tensor_tensor(u[:, 2 + n * TC:2 + (n + 1) * TC], ps[:, 0:TC],
                                            cc[:, n * TC:(n + 1) * TC], ALU.mult)
                elif kind == "b":
                    if i == 0 and n == 0:
                        dve.wait_ge(kn_out, 16)
                    ins = vec.tensor_tensor(cT[:, i, n * TC:(n + 1) * TC], ps[:, 0:TC], z[:, n * TC:(n + 1) * TC],
                                            ALU.mult)
                else:
                    ins = unload_group(dve, vec.tensor_copy, g)
                ins.then_inc(dve_emptied, 1)
                if kind == "x" and i + 2 < NT:
                    normalise(i + 2)
                if kind == "v" and i < NS:
                    sample_scores(i)
                if kind == "u" and n == 2:
                    dve.wait_ge(dve_emptied, taker[g][1])
                    conv(i)
                if kind == "b" and n == 2 and i == 0:
                    dve.wait_ge(sT_ready, 1)
                    step(vec.tensor_reduce(smx, bank(6)[0:64, 0:3 * P + NS], X, ALU.max))
                    vec.tensor_scalar(sneg, smx, -1.0, None, ALU.mult).then_inc(smax_ready, 1)
                if kind == "b" and n == 2 and i == 1:
                    dve.wait_ge(sexp_ready, 1)
                    step(vec.reciprocal(srl, sl))
                    vec.tensor_scalar(sprob, sprob, srl, None, ALU.mult).then_inc(sp_ready, 1)
            dve.wait_ge(spv_ready, 1)
            out = bank(4).rearrange("p (m b h) -> p m b h", m=8, b=NS)
            for m in range(MA):
                for e in range(2):
                    part = slice(e * DH, (e + 1) * DH)
                    ins = vec.tensor_copy(qT[part, m, SEQ:NTOK], out[part, m, :, 2 * m + e])
            ins.then_inc(s_attn, 1)

            def mask(n):
                i = n // H
                w = (i + 1) * P
                if n == 0:
                    dve.wait_ge(mask_in, 16)
                dve.wait_ge(s_ready, n + 1)
                if n >= 3:
                    dve.wait_ge(pT_ready, n - 2)
                c = n % 3
                step(vec.tensor_tensor_reduce(sm[c][:, 0:w], bank(2 * (n % 2), 2)[:, 0:w], amask[:, SEQ - w:SEQ],
                                              1.0, NEG, ALU.add, ALU.max, mx_n[:, c:c + 1]))
                vec.tensor_scalar(neg_n[:, c:c + 1], mx_n[:, c:c + 1], -1.0, None, ALU.mult).then_inc(masked, 1)

            def copy_pT(n):
                w = (n // H + 1) * P
                dve.wait_ge(pT_ready, n + 1)
                if n >= 2:
                    dve.wait_ge(pv_done, n - 1)
                vec.tensor_copy(pt[n % 2][:, 0:w], bank(4, 2)[:, 0:w]).then_inc(pT_dve, 1)

            def divide(i):
                c = slice((i % 2) * H, (i % 2) * H + H)
                dve.wait_ge(pv_done, H * (i + 1))
                if i >= 2:
                    dve.wait_ge(aT_ready, i - 1)
                step(vec.reciprocal(rl[:, c], lsum[:, c]))
                vec.tensor_tensor(an[i % 2].rearrange("p (h d) -> p h d", h=H),
                                  bank(6 + i % 2).rearrange("p (h d) -> p h d", h=H),
                                  rl[:, c].unsqueeze(2).broadcast_to([P, H, DH]), ALU.mult).then_inc(an_ready, 1)

            for n in range(NSTEP + 6):
                if n < NSTEP:
                    mask(n)
                if 2 <= n < NSTEP + 2 and (n - 2) % 3 == 0:
                    copy_pT(n - 2)
                if n >= H + 3 and (n - 3) % H == 0:
                    divide((n - 3) // H - 1)

            dve.wait_ge(wo_in, 16)
            for k in range(KD):
                ins = vec.tensor_scalar(wo[:, k, :], wo[:, k, :], gout[:, k:k + 1], None, ALU.mult)
            ins.then_inc(wo_scaled, 1)

            def residual(t):
                w = rows(t)
                dve.wait_ge(std_ac_ready, t + 1)
                step(vec.reciprocal(rst_ac[0:w, :], std_ac[0:w, :]))
                for half in range(2):
                    x = xres[0:w, t, half * 512:(half + 1) * 512]
                    for c in range(2):
                        dve.wait_ge(o_ready, 4 * t + 2 * half + c + 1)
                        ins = vec.scalar_tensor_tensor(out=x, in0=bank(2 * half + c)[0:w, :], scalar=rst_ac[0:w, c:c + 1],
                                                       in1=x, op0=ALU.mult, op1=ALU.add)
                        ins.then_inc(o_used, 1)
                        dve.wait_ge(o_used, 4 * t + 2 * half + c + 1)

            def router_rows(t):
                w = rows(t)
                c = t % 2
                dve.wait_ge(std_f_ready, t + 1)
                step(vec.reciprocal(rst_f[0:w, c:c + 1], std_f[0:w, c:c + 1]))
                vec.scalar_tensor_tensor(out=h2[c][0:w, :], in0=xres[0:w, t, :], scalar=rst_f[0:w, c:c + 1],
                                         in1=gffn[0:w, :], op0=ALU.mult, op1=ALU.mult).then_inc(h2_ready, 1)

            dve.wait_ge(router_in, 48)
            step(vec.memset(lg, 0.0))
            for t in range(NT):
                residual(t)
                router_rows(t)
                w = rows(t)
                NR = NGRP + NE
                if t >= 1:
                    w = rows(t - 1)
                    dve.wait_ge(lg_ready, t)
                    vec.tensor_tensor(lg[0:w, t - 1, :], bank(7)[0:w, (t - 1) * NR:t * NR], rbias[0:w, :], ALU.add
                                      ).then_inc(lg_used, 1)
            dve.wait_ge(lg_ready, NT)
            vec.tensor_tensor(lg[0:NS, NQ, :], bank(7)[0:NS, NQ * NR:NT * NR], rbias[0:NS, :], ALU.add
                              ).then_inc(lg_used, 1)
            dve.wait_ge(lg_used, NT)
            dve.wait_ge(h2_out[0], 16 * 5)
            dve.wait_ge(h2_out[1], 16 * 4)

            def wide(x9, n):
                return x9.unsqueeze(2).broadcast_to([P, NT, n])

            def ramps(n):
                return ramp[:, 0:n].unsqueeze(1).broadcast_to([P, NT, n])

            def first_index(dst, eq, n):
                step(vec.scalar_tensor_tensor(out=eq, in0=eq, scalar=-float(n), in1=ramps(n), op0=ALU.mult,
                                              op1=ALU.add))
                step(vec.tensor_reduce(dst, eq, X, ALU.min))
                step(vec.tensor_scalar(dst, dst, float(n), None, ALU.add))

            gl = lg[:, :, 0:NGRP]
            step(vec.tensor_reduce(r_gm, gl, X, ALU.max))
            step(vec.tensor_tensor(r_eq, gl, wide(r_gm, NGRP), ALU.is_equal))
            vec.tensor_tensor(r_d, gl, wide(r_gm, NGRP), ALU.subtract).then_inc(gd_ready, 1)
            first_index(r_gi, r_eq, NGRP)
            step(vec.tensor_tensor(r_goh, ramps(NGRP), wide(r_gi, NGRP), ALU.is_equal))
            for g in range(NGRP):
                el = lg[:, :, NGRP + g * EPG:NGRP + (g + 1) * EPG]
                dst = r_le if g == 0 else r_eq8
                step(vec.tensor_tensor(dst, el, r_goh[:, :, g:g + 1].broadcast_to([P, NT, EPG]), ALU.mult))
                if g:
                    step(vec.tensor_tensor(r_le, r_le, r_eq8, ALU.add))
            step(vec.tensor_reduce(r_v1, r_le, X, ALU.max))
            step(vec.tensor_tensor(r_eq8, r_le, wide(r_v1, EPG), ALU.is_equal))
            first_index(r_i1, r_eq8, EPG)
            step(vec.tensor_tensor(r_oh, ramps(EPG), wide(r_i1, EPG), ALU.is_equal))
            step(vec.scalar_tensor_tensor(out=r_le2, in0=r_oh, scalar=-3e38, in1=r_le, op0=ALU.mult, op1=ALU.add))
            step(vec.tensor_reduce(r_v2, r_le2, X, ALU.max))
            step(vec.tensor_tensor(r_eq8, r_le2, wide(r_v2, EPG), ALU.is_equal))
            first_index(r_i2, r_eq8, EPG)
            vec.tensor_tensor(r_vd, r_v2, r_v1, ALU.subtract).then_inc(vd_ready, 1)
            for c, idx in enumerate((r_i1, r_i2)):
                step(vec.scalar_tensor_tensor(out=r_e[:, c, :], in0=r_gi, scalar=float(EPG), in1=idx, op0=ALU.mult,
                                              op1=ALU.add))
            step(vec.tensor_tensor(r_hot1, ramps(NE), wide(r_e[:, 0, :], NE), ALU.is_equal))
            step(vec.tensor_tensor(r_hot2, ramps(NE), wide(r_e[:, 1, :], NE), ALU.is_equal))
            step(vec.tensor_tensor(r_hot, r_hot1, r_hot2, ALU.add))
            step(vec.memset(r_sum[:, 0, :], 0.0))
            for t in range(1, NT):
                ins = vec.tensor_tensor(r_sum[:, t, :], r_sum[:, t - 1, :], r_hot[:, t - 1, :], ALU.add)
                if t < NT - 1:
                    step(ins)
            ins.then_inc(assigned, 1)
            dve.wait_ge(gexp_ready, 1)
            step(vec.tensor_reduce(r_sg, r_d, X, ALU.add))
            step(vec.reciprocal(r_pg, r_sg))
            dve.wait_ge(vexp_ready, 1)
            step(vec.tensor_scalar(r_den, r_vd, 1.0, None, ALU.add))
            step(vec.reciprocal(r_t9, r_den))
            step(vec.tensor_tensor(gates[:, 0, :], r_t9, r_pg, ALU.mult))
            step(vec.tensor_tensor(gates[:, 1, :], gates[:, 0, :], r_vd, ALU.mult))
            step(vec.memset(r_rank, 0.0))
            dve.wait_ge(ranked, 1)
            vec.tensor_copy(r_rank[0:NS, NQ, :], bank(0)[0:NS, NQ * NE:NT * NE])
            vec.tensor_copy(r_rank[:, 0:NQ, :], bank(0)[:, 0:NQ * NE].rearrange("p (t e) -> p t e", t=NQ))
            step(vec.tensor_copy(r_rank[:, NT, :], bank(0)[:, NT * NE:(NT + 1) * NE]))
            count = r_rank[:, NT, :]
            step(vec.tensor_scalar(r_ob, count, float(SLOTS), None, ALU.is_gt))
            for m in range(2, MORE + 1):
                step(vec.scalar_tensor_tensor(out=r_ob, in0=count, scalar=float(m * SLOTS), in1=r_ob, op0=ALU.is_gt,
                                              op1=ALU.add))
            step(vec.tensor_tensor_scan(r_inc, ones[:, 0:NE], r_ob, 0.0, ALU.mult, ALU.add))
            step(vec.tensor_tensor(r_exc, r_inc, r_ob, ALU.subtract))
            for c, hot in enumerate((r_hot1, r_hot2)):
                step(vec.tensor_tensor(r_big, hot, r_rank[:, 0:NT, :], ALU.mult))
                step(vec.tensor_reduce(r_r[:, c, :], r_big, X, ALU.add))
                step(vec.tensor_tensor(r_big, hot, r_exc.unsqueeze(1).broadcast_to([P, NT, NE]), ALU.mult))
                step(vec.tensor_reduce(r_so[:, c, :], r_big, X, ALU.add))
            step(vec.tensor_scalar(r_q, r_r, float(SLOTS), None, ALU.is_ge))
            step(vec.tensor_copy(r_is, r_q))
            for m in range(2, MORE + 1):
                step(vec.scalar_tensor_tensor(out=r_q, in0=r_r, scalar=float(m * SLOTS), in1=r_q, op0=ALU.is_ge,
                                              op1=ALU.add))
            step(vec.scalar_tensor_tensor(out=r_j, in0=r_q, scalar=-float(SLOTS), in1=r_r, op0=ALU.mult, op1=ALU.add))
            step(vec.tensor_tensor(r_blk, r_so, r_q, ALU.add))
            step(vec.tensor_tensor(r_blk, r_blk, r_e, ALU.subtract))
            step(vec.scalar_tensor_tensor(out=r_blk, in0=r_blk, scalar=float(NE - 1), in1=r_is, op0=ALU.add,
                                          op1=ALU.mult))
            step(vec.tensor_tensor(r_blk, r_blk, r_e, ALU.add))
            for n in range(2 * NT):
                t, c = divmod(n, 2)
                w = rows(t)
                if n >= 2:
                    dve.wait_ge(hot_used, n - 1)
                vec.tensor_scalar(hot_slot[c][0:w, :], ramp[0:w, 0:SLOTS], r_j[0:w, c, t:t + 1], None, ALU.is_equal)
                vec.tensor_scalar(hot_blk[c][0:w, 0:NBLK], ramp[0:w, 0:NBLK], r_blk[0:w, c, t:t + 1],
                                  tokv[0:w, t:t + 1], ALU.is_equal, ALU.mult)
                vec.tensor_scalar(hot_blk[c][0:w, NBLK:2 * NBLK], ramp[0:w, 0:NBLK], r_blk[0:w, c, t:t + 1],
                                  (tokv, destv)[c][0:w, t:t + 1], ALU.is_equal, ALU.mult).then_inc(hot_ready, 1)
            step(vec.tensor_tensor(r_cmp[0:1], r_inc[0:1].unsqueeze(1).broadcast_to([1, OVER, NE]),
                                   ramp[0:1, 0:OVER].unsqueeze(2).broadcast_to([1, OVER, NE]), ALU.is_le))
            step(vec.tensor_reduce(r_tab2[0:1, 0:OVER], r_cmp[0:1], X, ALU.add))
            step(vec.tensor_scalar(r_tab2[0:1, 0:OVER], r_tab2[0:1, 0:OVER], float(NE - 1), None, ALU.min))
            vec.tensor_copy(oexp[0:1, 0:OVER], r_tab2[0:1, 0:OVER])
            vec.tensor_copy(oexp[0:1, OVER:OVER + 1], r_inc[0:1, NE - 1:NE])
            dve.wait_ge(hot_used, 2 * NT)
            tab = bank(1)[0:SLOTS, 0:2 * NBLK]
            step(vec.tensor_scalar(r_tab[0:SLOTS, 0, :], tab[:, 0:NBLK], -1.0, 0.0, ALU.add, ALU.max))
            step(vec.tensor_scalar(r_tab2[0:SLOTS], tab[:, NBLK:2 * NBLK], 0.0, DROP, ALU.is_equal, ALU.mult))
            step(vec.scalar_tensor_tensor(out=r_tab[0:SLOTS, 1, :], in0=tab[:, NBLK:2 * NBLK], scalar=-1.0,
                                          in1=r_tab2[0:SLOTS], op0=ALU.add, op1=ALU.add))
            vec.tensor_copy(gi_s[:], r_tab[0:SLOTS, 0, 0:2])
            step(vec.tensor_copy(gidx[:], r_tab[0:SLOTS, 0, :]))
            vec.tensor_copy(sidx[:], r_tab[0:SLOTS, 1, :]).then_inc(routed, 1)

            def copy_xT(f, s, n):
                dve.wait_ge(f.xT_ready, 2 * n + 2)
                vec.tensor_copy(xT[s][:, 4:8, :], bank(5)[:, 0:4 * SLOTS].rearrange("p (k t) -> p k t", k=4)
                                ).then_inc(f.xT_dve, 1)

            def hidden(f, s, n):
                dve.wait_ge(f.silu_done, n + 1)
                dve.wait_ge(f.up_done, n + 1)
                vec.tensor_tensor(hid[s], bank(1)[:, 0:4 * SLOTS].rearrange("p (m t) -> p m t", m=4), sg[s], ALU.mult
                                  ).then_inc(f.hid_done, 1)

            def copy_y(f, s, n, before=0):
                dve.wait_ge(f.y_done, n + (before + 1))
                vec.tensor_copy(ysb[s][:, 512:1024], bank(3)[0:SLOTS, :]).then_inc(f.y_dve, 1)

            def stage(dst, s, src, blk):
                return vec.tensor_scalar(dst[:, s:s + 1], src[:, bass.ds(blk, 1)], 0.0, None, ALU.add)

            def expert(b, turns, s, turn_next, reused, fetch_next=True):
                hidden(first, s, b)
                if turn_next:
                    copy_xT(first, 1 - s, b + 1)
                if reused:
                    dve.wait_ge(first.sent[s], 16 * turns)
                stage(si_s, s, sidx, b)
                if fetch_next:
                    stage(gi_s, s, gidx, b + 2)
                if reused or s == 1:
                    dve.wait_ge(first.held, b)
                copy_y(first, s, b)

            copy_xT(first, 0, 0)
            expert(0, 0, 0, True, False)
            expert(1, 0, 1, True, False)
            with dve.Fori(1, NE // 2 - 1, 1) as j:
                expert(2 * j, j, 0, True, True)
                expert(2 * j + 1, j, 1, True, True)
            expert(NE - 2, NE // 2 - 1, 0, True, True, False)
            expert(NE - 1, NE // 2 - 1, 1, False, True, False)
            dve.wait_ge(first.sent[0], 16 * (NE // 2))
            dve.wait_ge(first.held, NE)
            more = dve.value_load(oexp[0:1, OVER:OVER + 1], min_val=0, max_val=OVER)
            with dve.If(more > 0):
                with dve.Fori(0, more, 1) as o:
                    stage(si_s, 0, sidx, o + NE)
                    stage(gi_s, 0, gidx, o + NE).then_inc(further.staged, 1)
                    copy_xT(further, 0, o)
                    hidden(further, 0, o)
                    dve.wait_ge(further.held, 2 * o + 1)
                    copy_y(further, 0, o, NE)
                    dve.wait_ge(further.sent[0], 16 * o + 16)
                    dve.wait_ge(further.held, 2 * o + 2)

            def add_experts(t):
                w = rows(t)
                dve.wait_ge(y_in[t % 2], 32 * (t // 2 + 1))
                x = xres[0:w, t, :]
                for c in range(2):
                    ins = vec.scalar_tensor_tensor(out=x, in0=yt[t % 2][0:w, c, :], scalar=gates[0:w, c, t:t + 1], in1=x,
                                                   op0=ALU.mult, op1=ALU.add)
                    if c == 0:
                        step(ins)
                ins.then_inc(fin_res, 1)

            def finish(t):
                w = rows(t)
                c = t % 2
                dve.wait_ge(fin_std, t + 1)
                step(vec.reciprocal(rst_f[0:w, c:c + 1], std_f[0:w, c:c + 1]))
                if t >= 2:
                    dve.wait_ge(out_sent[c], 16 * (t // 2))
                vec.scalar_tensor_tensor(out=ot[c][0:w, :], in0=xres[0:w, t, :], scalar=rst_f[0:w, c:c + 1],
                                         in1=gfin[0:w, :], op0=ALU.mult, op1=ALU.mult).then_inc(fin_out, 1)

            dve.wait_ge(gfin_in, 16)
            add_experts(0)
            for t in range(NT):
                if t + 1 < NT:
                    add_experts(t + 1)
                finish(t)

        @block.gpsimd
        def _(pool):
            gp = nc.gpsimd

            def hold(f, cell):
                gp.tensor_tensor(stat[0:1, cell:cell + 1], ones[0:1, 0:1], ones[0:1, 0:1], ALU.mult
                                 ).then_inc(f.held, 1)

            def fetch(f, s):
                gp.indirect_dma_start(xg[s], None, h2_d[:, :], bass.IndirectOffsetOnAxis(ap=gi_s[:, s:s + 1], axis=0)
                                      ).then_inc(f.rows_in[s], 16)

            def send(f, s):
                gp.indirect_dma_start(y_d[:, :], bass.IndirectOffsetOnAxis(ap=si_s[:, s:s + 1], axis=0), ysb[s], None,
                                      bounds_check=2 * NTOK - 1, oob_is_err=False).then_inc(f.sent[s], 16)

            pool.wait_ge(h2_out[0], 16 * 5)
            pool.wait_ge(h2_out[1], 16 * 4)
            pool.wait_ge(routed, 1)
            fetch(first, 0)
            fetch(first, 1)

            def expert(b, s, fetch_next):
                pool.wait_ge(first.y_act, b + 1)
                pool.wait_ge(first.y_dve, b + 1)
                hold(first, 93 + s)
                send(first, s)
                if fetch_next:
                    fetch(first, s)

            with pool.Fori(0, NE // 2 - 1, 1) as j:
                expert(2 * j, 0, True)
                expert(2 * j + 1, 1, True)
            expert(NE - 2, 0, False)
            expert(NE - 1, 1, False)
            pool.wait_ge(first.sent[0], 16 * (NE // 2))
            pool.wait_ge(first.sent[1], 16 * (NE // 2))
            more = pool.value_load(oexp[0:1, OVER:OVER + 1], min_val=0, max_val=OVER)
            with pool.If(more > 0):
                with pool.Fori(0, more, 1) as o:
                    pool.wait_ge(further.staged, o + 1)
                    hold(further, 93)
                    fetch(further, 0)
                    pool.wait_ge(further.y_act, o + 1)
                    pool.wait_ge(further.y_dve, o + 1)
                    hold(further, 94)
                    send(further, 0)
                    pool.wait_ge(further.sent[0], 16 * o + 16)
            gp.memset(stat[0:1, 95:96], 0.0).then_inc(all_sent, 1)


_OUT = {
    "y_prompt": (SEQ, D), "y_sample": (NS, D), "k_prompt": (SEQ, DA), "v_prompt": (SEQ, DA),
    "conv_u": (P, MA, NS + 2), "k_sample": (NS, DA), "v_sample": (NS, DA), "conv_sample_old": (NS, DA),
}


def kernel(**inputs):
    import concourse.bacc as _bacc
    from concourse.bass_utils import run_bass_kernel_spmd as _run

    x = {n: np.ascontiguousarray(v) for n, v in inputs.items()}
    const, amask, smask = constants()
    gain_out = np.concatenate([x["norm_out_attn"][0], x["norm_out_conv"][0]]).reshape(KD, P).T
    arrays = {
        "x_prompt": x["x_prompt"][0], "x_sample": x["x_sample"][:, 0], "w_in": x["w_in"][0],
        "cache_k": x["cache_k"][0].reshape(NS, WBUF, DA), "cache_v": x["cache_v"][0].reshape(NS, WBUF, DA),
        "state_conv": x["state_conv"][0],
        "conv_state": x["state_conv"][0].reshape(NS, 2, MA, P).transpose(3, 2, 1, 0),
        "conv_w": x["conv_w"][0].reshape(CONV, MA, P).transpose(2, 1, 0),
        "gain_out": gain_out, "norm_mix": x["norm_mix"][0], "norm_ffn": x["norm_ffn"][0],
        "norm_final": x["norm_final"], "w_out": x["w_out"][0],
        "w_router": np.concatenate([x["w_router_group"][0], x["w_router_expert"][0]], axis=1)
        .reshape(KD, P, NGRP + NE).transpose(1, 0, 2),
        "b_router": np.concatenate([x["b_router_group"][0], x["b_router_expert"][0]]),
        "w_gate": x["w_gate"][0], "w_up": x["w_up"][0], "w_down": x["w_down"][0],
        "const": const, "amask": amask, "smask": smask,
    }
    nc = _bacc.Bacc("TRN2", target_bir_lowering=False, num_devices=1)
    feed, aps = {}, {}
    for name, arr in arrays.items():
        arr = np.ascontiguousarray(arr)
        feed[f"in_{name}"] = arr
        aps[name] = nc.dram_tensor(f"in_{name}", arr.shape, mybir.dt.from_np(arr.dtype), kind="ExternalInput").ap()
    for name in ("w_gate", "w_up", "w_down"):
        aps[name + "_flat"] = aps[name].rearrange("e d n -> (e d) n")
    for name, shape in _OUT.items():
        aps[name] = nc.dram_tensor(f"out_{name}", shape, F32, kind="ExternalOutput").ap()
    program(nc, aps)
    r = _run(nc, [feed], core_ids=[0]).results[0]
    got = {n: r[f"out_{n}"] for n in _OUT}
    u = got["conv_u"].transpose(2, 1, 0).reshape(NS + 2, DA)
    conv_sample = np.stack([got["conv_sample_old"], u[2:]], axis=1)
    return (got["y_prompt"][None], got["y_sample"][:, None], got["k_prompt"].reshape(1, 1, SEQ, H, DH),
            got["v_prompt"].reshape(1, 1, SEQ, H, DH), u[None, None, 0:2],
            got["k_sample"].reshape(1, NS, 1, H, DH), got["v_sample"].reshape(1, NS, 1, H, DH), conv_sample[None])
```

```python
from contextlib import ExitStack

import numpy as np

import concourse.bass as bass
from concourse import mybir

F32 = mybir.dt.float32
F32R = mybir.dt.float32r
I32 = mybir.dt.int32
ALU = mybir.AluOpType
ACT = mybir.ActivationFunctionType
X = mybir.AxisListType.X

P = 128
D = 1024
KD = D // P
SEQ = 1024
NS = 8
NTOK = SEQ + NS
NT = SEQ // P + 1
NQ = SEQ // P
H = 8
DH = 64
DA = H * DH
MA = DA // P
DIL = (1, 4, 16)
WIN = 128
WBUF = 2048
CONV = 3
NE = 32
NGRP = 4
EPG = NE // NGRP
DE = 512
SLOTS = 96
MORE = -(-NTOK // SLOTS) - 1
OVER = 2 * NTOK // SLOTS + 1
NBLK = NE + OVER
TC = NTOK // 3
EPS = 1e-6
NEG = -1e30
DROP = 8192.0


def rows(t):
    return P if t < NQ else NS


def constants():
    p = np.arange(P)[:, None]
    c = np.arange(P)[None, :]
    tok = 128 * np.arange(NT)[None, :] + p + 1
    const = np.concatenate([
        (p == c), np.broadcast_to(c, (P, P)), (p < c), np.ones((P, P)),
        tok, tok + NTOK, np.full((P, 1), EPS),
    ], axis=1).astype(np.float32)
    dist = p + (SEQ - P) - np.arange(SEQ)[None, :]
    count = sum(((dist >= 0) & (dist % d == 0) & (dist <= d * WIN)).astype(np.int32) for d in DIL)
    amask = np.where(count > 0, np.log(np.maximum(count, 1)), NEG).astype(np.float32)
    smask = np.full((NS, NS, H), NEG, np.float32)
    smask[np.arange(NS), np.arange(NS)] = np.log(len(DIL))
    return const, amask, smask.reshape(NS, NS * H)


def program(nc, a):
    with ExitStack() as ctx:
        def sb(name, shape, dt=F32):
            return ctx.enter_context(nc.sbuf_tensor(name, shape, dt))

        def sem(name):
            return ctx.enter_context(nc.semaphore(name))

        base = -(-nc.sbuf_base // 32) * 32

        def at(name, offset, shape, dt=F32):
            return nc.alloc_sbuf_tensor_at(name, [P] + list(shape), dt, offset=base + offset)[:]

        class Pack:

            def __init__(self, start, end):
                self.next, self.end = start, end

            def __call__(self, name, shape, dt=F32):
                t = at(name, self.next, shape, dt)
                self.next += -(-4 * int(np.prod(shape)) // 32) * 32
                assert self.next <= self.end, name
                return t

        XRES, WEI, TMP, END = 10240, 47104, 194560, 212832
        WSLOT = 49152
        QT, CT, MISC, WOUT = 145408, 161920, 178432, 79872

        keep = Pack(0, XRES)
        cst = keep("cst", [4 * P + 2 * NT + 1])
        gout = keep("gout", [KD])
        cw = keep("cw", [MA, CONV])
        cstate = keep("cstate", [MA, 2, NS])
        uout = keep("uout", [MA, NS + 2])
        srow = keep("srow", [3, DA])[0:NS]
        stat = keep("stat", [96])
        gates = keep("gates", [2, NT])
        gidx = keep("gidx", [NBLK], I32)[0:SLOTS]
        sidx = keep("sidx", [NBLK], I32)[0:SLOTS]
        oexp = keep("oexp", [OVER + 1], I32)
        gi_s = keep("gi_s", [1], I32)[0:SLOTS]
        si_s = keep("si_s", [1], I32)[0:SLOTS]

        ident, ramp = cst[:, 0:P], cst[:, P:2 * P]
        before, ones = cst[:, 2 * P:3 * P], cst[:, 3 * P:4 * P]
        tokv = cst[:, 4 * P:4 * P + NT]
        destv = cst[:, 4 * P + NT:4 * P + 2 * NT]
        eps = cst[:, 4 * P + 2 * NT:4 * P + 2 * NT + 1]
        ssq_x, std_x, rst_x = stat[:, 0:9], stat[:, 9:18], stat[:, 18:27]
        mx_n, neg_n = stat[:, 27:30], stat[:, 30:33]
        lsum, rl = stat[:, 33:49], stat[:, 49:65]
        smx, sneg, sl, srl = stat[0:64, 65:66], stat[0:64, 66:67], stat[0:64, 67:68], stat[0:64, 68:69]
        std_ac, rst_ac = stat[:, 70:72], stat[:, 72:74]
        ssq_f, std_f, rst_f = stat[:, 74:76], stat[:, 76:78], stat[:, 78:80]

        NXT = 5
        pack = Pack(XRES, WEI)
        xt = [pack(f"x_tile{s}", [D]) for s in range(NXT)]
        xn = [pack(f"xn{s}", [D]) for s in range(2)]
        gmix = pack("gmix", [D])
        junk = pack("junk", [D])
        pack = Pack(XRES, WEI)
        kT = pack("kT", [MA, NTOK])
        v = pack("v", [NQ, DA])
        pack = Pack(WEI, QT)
        h_hi = pack("h_hi", [KD, NTOK], F32R)
        h_lo = pack("h_lo", [KD, NTOK], F32R)
        w_raw = [pack(f"w_raw{s}", [KD, P]) for s in range(3)]
        w_hi = [pack(f"w_hi{s}", [KD, P], F32R) for s in range(2)]
        w_lo = [pack(f"w_lo{s}", [KD, P], F32R) for s in range(2)]
        own = pack("own", [DA])[0:NS]
        qT = at("qT", QT, [MA, NTOK])
        cT = at("cT", CT, [MA, NTOK])
        kn = at("kn", CT, [NQ, DA])
        pack = Pack(MISC, END)
        u = pack("u", [NTOK + 2])
        cc_at = pack.next
        cc = pack("cc", [NTOK])
        z = pack("z", [NTOK])
        vT = [pack("vT0", [NTOK]), at("vT1", cc_at, [NTOK])]
        kv = pack("kv", [2, len(DIL) * DA])
        sscore = pack("sscore", [len(DIL) + 1, NS * H])
        sprob = pack("sprob", [3 * P + NS])[0:64]
        sprobT = pack("sprobT", [len(DIL) + 1, NS * H])
        ssm = pack("ssm", [NS * H])[0:NS]
        pack = Pack(WEI, WOUT)
        sm = [pack(f"scores{s}", [D]) for s in range(3)]
        pt = [pack(f"probsT{s}", [D]) for s in range(2)]
        amask = pack("amask", [SEQ])
        an = [pack(f"attn{s}", [DA]) for s in range(2)]
        wo_raw = [at(f"wo_raw{s}", MISC + 4096 * s, [D]) for s in range(4)]
        wo_hi = at("wo_hi", WOUT, [KD, D], F32R)
        wo_lo = at("wo_lo", WOUT + 32768, [KD, D], F32R)
        xres = at("xres", XRES, [NT, D])
        pack = Pack(WEI + 16384, WOUT)
        a_hi = [pack(f"a_hi{s}", [2 * MA, P], F32R) for s in range(2)]
        a_lo = [pack(f"a_lo{s}", [2 * MA, P], F32R) for s in range(2)]
        pack = Pack(MISC, END)
        sq = [pack(f"sq{s}", [2 * MA, P]) for s in range(2)]
        h2 = [pack(f"h2_{s}", [D]) for s in range(2)]
        h2T = [pack(f"h2T{s}", [KD, P]) for s in range(2)]
        gffn = pack("gffn", [D])
        wr = pack("wr", [KD, NGRP + NE])
        rbias = pack("rbias", [NGRP + NE])
        lg = pack("lg", [NT, NGRP + NE])
        rt = Pack(MISC, TMP)
        r_gm, r_gi, r_sg, r_pg, r_v1, r_v2, r_i1, r_i2, r_vd, r_den, r_t9 = (
            rt(f"r{i}", [NT]) for i in range(11))
        r_e, r_r, r_so, r_q, r_j, r_blk, r_is = (rt(f"rc{i}", [2, NT]) for i in range(7))
        r_ob, r_inc, r_exc = (rt(f"re{i}", [NE]) for i in range(3))
        r_d, r_eq, r_goh = (rt(f"rg{i}", [NT, NGRP]) for i in range(3))
        r_le, r_eq8, r_oh, r_le2 = (rt(f"rl{i}", [NT, EPG]) for i in range(4))
        r_big, r_hot1, r_hot2, r_hot, r_sum = (rt(f"rh{i}", [NT, NE]) for i in range(5))
        r_rank = rt("r_rank", [NT + 1, NE])
        r_cmp = rt("r_cmp", [OVER, NE])
        r_tab = rt("r_tab", [2, NBLK])
        r_tab2 = rt("r_tab2", [NBLK])
        hot_slot = [rt(f"hot_slot{s}", [SLOTS]) for s in range(2)]
        hot_blk = [rt(f"hot_blk{s}", [2 * NBLK]) for s in range(2)]
        wg = [at(f"w_gate{s}", WEI + WSLOT * s, [KD, DE]) for s in range(3)]
        wu = [at(f"w_up{s}", WEI + WSLOT * s + 16384, [KD, DE]) for s in range(3)]
        wd = [at(f"w_down{s}", WEI + WSLOT * s + 32768, [DE // P, D]) for s in range(3)]
        pack = Pack(TMP, END)
        xg = pack("x_rows", [D])[0:SLOTS]
        xT = pack("x_turned", [KD, SLOTS])
        sg = pack("silu_gate", [4, SLOTS])
        hid = pack("hid", [4, SLOTS])
        ysb = pack("y_rows", [D])[0:SLOTS]
        NY, NO = 4, 3
        pack = Pack(WEI, QT)
        yt = [pack(f"y_tile{s}", [2, D]) for s in range(NY)]
        ot = [pack(f"out_tile{s}", [D]) for s in range(NO)]
        gfin = pack("gfin", [D])
        fjunk = pack("fjunk", [D])

        psum = ctx.enter_context(nc.psum_tensor("psum", [P, 8 * 512], F32))

        def bank(b, n=1):
            return psum[:, 512 * b:512 * (b + n)]

        h2_d = nc.dram_tensor("h2_rows", [NTOK, D], F32, kind="Internal").ap()
        y_d = nc.dram_tensor("y_rows", [2 * NTOK, D], F32, kind="Internal").ap()

        const_in = sem("const_in")
        small_in = sem("small_in")
        gmix_in = sem("gmix_in")
        x_in = [sem(f"x_in{t}") for t in range(NT)]
        win_in = [sem(f"win_in{s}") for s in range(3)]
        w_hi_ready = sem("w_hi_ready")
        w_ready = sem("w_ready")
        h_hi_ready = sem("h_hi_ready")
        kv_in = [sem(f"kv_in{s}") for s in range(2)]
        wo_in = [sem(f"wo_in{s}") for s in range(4)]
        xres_in = [sem(f"xres_in{t}") for t in range(NT)]
        mask_in = sem("mask_in")
        router_in = sem("router_in")
        act_step = sem("act_step")
        dve_step = sem("dve_step")
        std_ready = sem("std_ready")
        xn_ready = sem("xn_ready")
        group_done = sem("group_done")
        act_emptied = sem("act_emptied")
        dve_emptied = sem("dve_emptied")
        qb_ready = sem("qb_ready")
        scored = sem("scored")
        z_ready = sem("z_ready")
        kn_out = sem("kn_out")
        v_out = sem("v_out")
        u_ready = sem("u_ready")
        sT_ready = sem("sT_ready")
        smax_ready = sem("smax_ready")
        sexp_ready = sem("sexp_ready")
        sp_ready = sem("sp_ready")
        spT_ready = sem("spT_ready")
        spT_copied = sem("spT_copied")
        spv_used = sem("spv_used")
        spv_ready = sem("spv_ready")
        s_attn = sem("s_attn")
        s_ready = sem("s_ready")
        masked = sem("masked")
        exped = sem("exped")
        pT_ready = sem("pT_ready")
        pT_act = sem("pT_act")
        pT_dve = sem("pT_dve")
        pv_done = sem("pv_done")
        an_ready = sem("an_ready")
        aT_ready = sem("aT_ready")
        aT_copied = sem("aT_copied")
        wo_hi_ready = sem("wo_hi_ready")
        wo_ready = sem("wo_ready")
        a_hi_ready = sem("a_hi_ready")
        a_ready = sem("a_ready")
        sq_ready = sem("sq_ready")
        ssq_ready = sem("ssq_ready")
        std_ac_ready = sem("std_ac_ready")
        o_ready = sem("o_ready")
        o_used = sem("o_used")
        std_f_ready = sem("std_f_ready")
        h2_ready = sem("h2_ready")
        h2_out = [sem(f"h2_out{s}") for s in range(2)]
        h2T_ready = sem("h2T_ready")
        h2T_copied = sem("h2T_copied")
        lg_ready = sem("lg_ready")
        lg_used = sem("lg_used")
        gd_ready = sem("gd_ready")
        gexp_ready = sem("gexp_ready")
        vd_ready = sem("vd_ready")
        vexp_ready = sem("vexp_ready")
        assigned = sem("assigned")
        ranked = sem("ranked")
        hot_ready = sem("hot_ready")
        hot_used = sem("hot_used")
        table_ready = sem("table_ready")
        routed = sem("routed")
        all_sent = sem("all_sent")

        class Flow:

            def __init__(self, tag, slots):
                self.gate_in = [sem(f"{tag}_gate_in{s}") for s in range(slots)]
                self.up_in = [sem(f"{tag}_up_in{s}") for s in range(slots)]
                self.down_in = [sem(f"{tag}_down_in{s}") for s in range(slots)]
                self.rows_in = sem(f"{tag}_rows_in")
                self.sent = sem(f"{tag}_sent")
                self.xT_ready = sem(f"{tag}_xT_ready")
                self.xT_act = sem(f"{tag}_xT_act")
                self.xT_dve = sem(f"{tag}_xT_dve")
                self.gate_done = sem(f"{tag}_gate_done")
                self.up_done = sem(f"{tag}_up_done")
                self.silu_done = sem(f"{tag}_silu_done")
                self.hid_done = sem(f"{tag}_hid_done")
                self.y_done = sem(f"{tag}_y_done")
                self.y_act = sem(f"{tag}_y_act")
                self.y_dve = sem(f"{tag}_y_dve")
                self.staged = sem(f"{tag}_staged")
                self.held = sem(f"{tag}_held")

        first, further = Flow("first", 3), Flow("further", 1)
        further.y_done = first.y_done
        y_in = [sem(f"y_in{s}") for s in range(NY)]
        gfin_in = sem("gfin_in")
        fin_res = sem("fin_res")
        fin_std = sem("fin_std")
        fin_out = sem("fin_out")
        out_sent = [sem(f"out_sent{s}") for s in range(NO)]
        out_misc = sem("out_misc")

        tiles = [("q", m) for m in range(MA)] + [("k", m) for m in range(MA)] + [("v", m) for m in range(MA)]
        for m in range(MA):
            tiles += [("c", m), ("u", m), ("b", m)]
        column = {"q": 0, "k": DA, "v": 2 * DA, "b": 3 * DA, "c": 3 * DA + 512, "u": 3 * DA + 1024}
        groups = []
        for n in range(3):
            groups += [("x", t, h) for t in range(3 * n, 3 * n + 3) for h in range(2)]
            groups += [("q", 0, n)]
        for kind, m in tiles[1:]:
            for n in range(3):
                groups += [(kind, m, n)]
                if n == 0 and kind == "v" and m >= 1:
                    groups += [("vn", m - 1, j) for j in range(3)]
            if (kind, m) == ("k", MA - 1):
                groups += [("rows", 0, 0), ("rows", 1, 0)]
            if (kind, m) == ("v", MA - 1):
                groups += [("kn", i, 0) for i in range(NQ)] + [("vn", MA - 1, j) for j in range(3)]
        number = {g: i for i, g in enumerate(groups)}
        taker = []
        taken = {"act": 0, "dve": 0}
        for i, g in enumerate(groups):
            e = "act" if g[0] == "c" or (g[0] not in "ubx" and i % 2 == 0) else "dve"
            taken[e] += 1
            taker.append((e, taken[e]))

        def wait_emptied(eng, g):
            e, n = taker[g]
            eng.wait_ge(act_emptied if e == "act" else dve_emptied, n)

        def group_psum(g):
            return bank(g % 4)

        NSTEP = NQ * H
        WO_AT = 24

        block = ctx.enter_context(nc.Block())

        @block.sync
        def _(sp):
            def load_win(t):
                kind, m = tiles[t]
                c = column[kind] + m * P
                if t >= 3:
                    sp.wait_ge(w_ready, t - 2)
                sp.dma_start(w_raw[t % 3], a["w_in"][:, c:c + P].rearrange("(k p) n -> p k n", p=P)
                             ).then_inc(win_in[t % 3], 16)

            def load_x(t):
                if t >= NXT:
                    sp.wait_ge(xn_ready, t - NXT + 1)
                src = a["x_prompt"][t * P:(t + 1) * P, :] if t < NQ else a["x_sample"]
                sp.dma_start(xt[t % NXT][0:rows(t), :], src).then_inc(x_in[t], 16)

            load_x(0)
            sp.dma_start(cst[:], a["const"]).then_inc(const_in, 16)
            sp.dma_start(gmix, a["norm_mix"].partition_broadcast(P)).then_inc(gmix_in, 16)
            load_win(0)
            load_x(1)
            load_x(2)
            load_win(1)
            for t in range(3, NT):
                load_x(t)
            load_win(2)
            for src, dst in (("gain_out", gout), ("conv_w", cw), ("conv_state", cstate), ("smask", ssm)):
                sp.dma_start(dst, a[src]).then_inc(small_in, 16)
            sp.dma_start(a["conv_sample_old"], a["state_conv"][:, 1, :]).then_inc(out_misc, 16)
            for t in range(3, len(tiles)):
                load_win(t)
                if tiles[t] == ("b", 1):
                    for m in range(MA):
                        for j in range(3):
                            wait_emptied(sp, number["vn", m, j])
                    for i in range(2):
                        wait_emptied(sp, number["rows", i, 0])
                    for i in range(NQ):
                        wait_emptied(sp, number["kn", i, 0])
                    sp.dma_start(a["k_prompt"].rearrange("(t p) c -> p t c", p=P), kn).then_inc(kn_out, 16)
                    sp.dma_start(a["v_prompt"].rearrange("(t p) c -> p t c", p=P), v).then_inc(v_out, 16)
                    sp.dma_start(a["k_sample"], srow[:, 1, :]).then_inc(out_misc, 16)
                    sp.dma_start(a["v_sample"], srow[:, 2, :]).then_inc(out_misc, 16)
            sp.wait_ge(group_done, len(groups))
            sp.dma_start(amask, a["amask"]).then_inc(mask_in, 16)
            sp.wait_ge(u_ready, MA)
            sp.dma_start(a["conv_u"], uout[:]).then_inc(out_misc, 16)
            sp.wait_ge(s_attn, 1)
            for emptied, last in ((act_emptied, taken["act"]), (dve_emptied, taken["dve"])):
                sp.wait_ge(emptied, last)
            for k in range(KD):
                if k >= 4:
                    sp.wait_ge(wo_ready, k - 3)
                sp.dma_start(wo_raw[k % 4], a["w_out"][k * P:(k + 1) * P, :]).then_inc(wo_in[k % 4], 16)
            sp.dma_start(gffn, a["norm_ffn"].partition_broadcast(P)).then_inc(router_in, 16)
            sp.dma_start(wr, a["w_router"]).then_inc(router_in, 16)
            sp.dma_start(rbias, a["b_router"].partition_broadcast(P)).then_inc(router_in, 16)
            sp.wait_ge(v_out, 16)
            sp.wait_ge(pv_done, NSTEP)
            for t in range(NT):
                src = a["x_prompt"][t * P:(t + 1) * P, :] if t < NQ else a["x_sample"]
                sp.dma_start(xres[0:rows(t), t, :], src).then_inc(xres_in[t], 16)
            sp.wait_ge(aT_ready, NQ)

            def load_gate(f, s, e):
                sp.dma_start(wg[s], a["w_gate"][e].rearrange("(k p) n -> p k n", p=P)).then_inc(f.gate_in[s], 16)

            def load_up(f, s, e):
                sp.dma_start(wu[s], a["w_up"][e].rearrange("(k p) n -> p k n", p=P)).then_inc(f.up_in[s], 16)

            def load_down(f, s, e):
                sp.dma_start(wd[s], a["w_down"][e].rearrange("(k p) n -> p k n", p=P)).then_inc(f.down_in[s], 16)

            load_gate(first, 0, 0)

            def store_h2(t):
                sp.wait_ge(h2_ready, t + 1)
                sp.dma_start(h2_d[P * t:P * t + rows(t), :], h2[t % 2][0:rows(t), :]).then_inc(h2_out[t % 2], 16)

            for t in range(NT):
                store_h2(t)
            sp.wait_ge(o_ready, 4 * NT)
            load_up(first, 0, 0)
            load_down(first, 0, 0)
            for load in (load_gate, load_up, load_down):
                load(first, 1, 1)
            load_gate(first, 2, 2)
            sp.wait_ge(aT_copied, NQ)
            load_up(first, 2, 2)
            sp.wait_ge(routed, 1)
            load_down(first, 2, 2)

            def refill(e, s):
                sp.wait_ge(first.gate_done, e - 2)
                sp.dma_start(wg[s], a["w_gate_flat"][bass.ds(e * D, D), :].rearrange("(k p) n -> p k n", p=P)
                             ).then_inc(first.gate_in[s], 16)
                sp.wait_ge(first.up_done, e - 2)
                sp.dma_start(wu[s], a["w_up_flat"][bass.ds(e * D, D), :].rearrange("(k p) n -> p k n", p=P)
                             ).then_inc(first.up_in[s], 16)
                sp.wait_ge(first.y_done, e - 2)
                sp.dma_start(wd[s], a["w_down_flat"][bass.ds(e * DE, DE), :].rearrange("(k p) n -> p k n", p=P)
                             ).then_inc(first.down_in[s], 16)

            with sp.Fori(1, NE // 3, 1) as j:
                for s in range(3):
                    refill(sp.snap(3 * j + s), s)
            refill(NE - 2, 0)
            refill(NE - 1, 1)
            sp.wait_ge(first.y_done, NE)
            more = sp.value_load(oexp[0:1, OVER:OVER + 1], min_val=0, max_val=OVER)
            with sp.If(more > 0):
                with sp.Fori(0, more, 1) as o:
                    e = sp.value_load(oexp[0:1, bass.ds(o, 1)], min_val=0, max_val=NE - 1)
                    sp.wait_ge(first.y_done, o + NE)
                    sp.dma_start(wg[0], a["w_gate_flat"][bass.ds(e * D, D), :].rearrange("(k p) n -> p k n", p=P)
                                 ).then_inc(further.gate_in[0], 16)
                    sp.dma_start(wu[0], a["w_up_flat"][bass.ds(e * D, D), :].rearrange("(k p) n -> p k n", p=P)
                                 ).then_inc(further.up_in[0], 16)
                    sp.dma_start(wd[0], a["w_down_flat"][bass.ds(e * DE, DE), :].rearrange("(k p) n -> p k n", p=P)
                                 ).then_inc(further.down_in[0], 16)
            sp.dma_start(gfin, a["norm_final"].partition_broadcast(P)).then_inc(gfin_in, 16)
            sp.wait_ge(all_sent, 1)

            def load_y(t):
                if t >= NY:
                    sp.wait_ge(fin_res, t - NY + 1)
                n = rows(t)
                for c in range(2):
                    row = c * NTOK + P * t
                    sp.dma_start(yt[t % NY][0:n, c, :], y_d[row:row + n, :]).then_inc(y_in[t % NY], 16)

            for t in range(NY):
                load_y(t)
            for t in range(NT):
                if t + NY < NT:
                    load_y(t + NY)
                sp.wait_ge(fin_out, t + 1)
                dst = a["y_prompt"][P * t:P * (t + 1), :] if t < NQ else a["y_sample"]
                sp.dma_start(dst, ot[t % NO][0:rows(t), :]).then_inc(out_sent[t % NO], 16)
            for o in out_sent:
                sp.wait_ge(o, 16 * (NT // NO))
            sp.wait_ge(out_misc, 16 * 4)
            sp.wait_ge(kn_out, 16)

        @block.tensor
        def _(pe):
            mm = nc.tensor.matmul
            pe.wait_ge(const_in, 16)

            def proj(g):
                kind, i, n = groups[g]
                if g >= 4:
                    wait_emptied(pe, g - 4)
                ps = group_psum(g)
                if kind == "x":
                    w = rows(i)
                    pe.wait_ge(xn_ready, i + 1)
                    for c in range(4):
                        k = 4 * n + c
                        ins = nc.tensor.transpose(ps[:, c * w:(c + 1) * w], xn[i % 2][0:w, k * P:(k + 1) * P],
                                                  ident[0:w, 0:w])
                elif kind == "rows":
                    for m in range(MA):
                        wait_emptied(pe, number["q" if i == 0 else "k", m, 2])
                    for m in range(MA):
                        ins = nc.tensor.transpose(ps[0:NS, m * P:(m + 1) * P],
                                                  (qT if i == 0 else kT)[:, m, SEQ:NTOK], ident)
                elif kind == "vn":
                    for c in range(3):
                        wait_emptied(pe, number["v", i, c])
                    for c in range(4 if n < 2 else 1):
                        t = 4 * n + c
                        w = rows(t)
                        ins = nc.tensor.transpose(ps[0:w, c * P:(c + 1) * P], vT[i % 2][:, t * P:t * P + w], ident)
                elif kind == "kn":
                    for m in range(MA):
                        ins = nc.tensor.transpose(ps[:, m * P:(m + 1) * P], kT[:, m, i * P:(i + 1) * P], ident)
                else:
                    t = tiles.index((kind, i))
                    if n == 0:
                        pe.wait_ge(w_ready, t + 1)
                    if t == 0:
                        for x in range(3 * n, 3 * n + 3):
                            for h in range(2):
                                wait_emptied(pe, number["x", x, h])
                    cols = slice(n * TC, (n + 1) * TC)
                    wh, wl = w_hi[t % 2], w_lo[t % 2]
                    for k in range(KD):
                        mm(ps[:, 0:TC], wh[:, k, :], h_hi[:, k, cols], start=(k == 0), stop=False)
                        mm(ps[:, 0:TC], wh[:, k, :], h_lo[:, k, cols], start=False, stop=False)
                        ins = mm(ps[:, 0:TC], wl[:, k, :], h_hi[:, k, cols], start=False, stop=(k == KD - 1))
                ins.then_inc(group_done, 1)

            def query_all_partitions(b):
                if b == 0:
                    wait_emptied(pe, number["rows", 0, 0])
                if b >= 2:
                    pe.wait_ge(scored, b - 1)
                mm(bank(4 + b % 2), ident[0:NS, b:b + 1].broadcast_to([NS, P]), srow[:, 0, :],
                   start=True, stop=True).then_inc(qb_ready, 1)

            def sample_scores_turned():
                pe.wait_ge(scored, NS)
                ps = bank(6)[0:64, :]
                for r in range(3):
                    nc.tensor.transpose(ps[:, r * P:(r + 1) * P], sscore[:, r, :], ident)
                nc.tensor.transpose(ps[:, 3 * P:3 * P + NS], sscore[0:NS, 3, :], ident[0:NS, 0:NS]
                                    ).then_inc(sT_ready, 1)

            def sample_probs_turned():
                pe.wait_ge(sp_ready, 1)
                ps = bank(7)
                for r in range(3):
                    nc.tensor.transpose(ps[:, r * 64:(r + 1) * 64], sprob[:, r * P:(r + 1) * P], ident[0:64, 0:64])
                nc.tensor.transpose(ps[0:NS, 192:256], sprob[:, 3 * P:3 * P + NS], ident[0:64, 0:64]
                                    ).then_inc(spT_ready, 1)

            def sample_values():
                pe.wait_ge(spT_copied, 1)
                out = bank(4).rearrange("p (m c) -> p m c", m=8)
                for m in range(MA):
                    mm(out[:, m, :], srow[:, 2, m * P:(m + 1) * P], sprobT[0:NS, 3, :],
                       start=(m == 0), stop=False, skip_group_check=True)
                for b in range(NS):
                    n = NS + b
                    pe.wait_ge(kv_in[n % 2], 48 * (n // 2 + 1))
                    for r in range(3):
                        for m in range(MA):
                            ins = mm(out[:, m, b * H:(b + 1) * H], kv[:, n % 2, r * DA + m * P:r * DA + (m + 1) * P],
                                     sprobT[:, r, b * H:(b + 1) * H], start=False, stop=(r == 2),
                                     skip_group_check=True)
                    if b < NS - 1:
                        ins.then_inc(spv_used, 1)
                    else:
                        ins.then_inc(spv_ready, 1)

            for g, (kind, i, n) in enumerate(groups):
                proj(g)
                if n < 2 or (kind, i) not in tiles:
                    continue
                t = tiles.index((kind, i))
                if 8 <= t < 8 + NS:
                    query_all_partitions(t - 8)
                if t == 16:
                    sample_scores_turned()
                if t == 20:
                    sample_probs_turned()
                if t == 21:
                    sample_values()

            def scores(n):
                i, h = divmod(n, H)
                m, lo = h // 2, DH * (h % 2)
                if n >= 2:
                    pe.wait_ge(masked, n - 1)
                ps = bank(2 * (n % 2), 2)
                width = (i + 1) * P
                for at in range(0, width, 512):
                    w = min(512, width - at)
                    ins = mm(ps[:, at:at + w], qT[lo:lo + DH, m, i * P:(i + 1) * P], kT[lo:lo + DH, m, at:at + w],
                             start=True, stop=True)
                ins.then_inc(s_ready, 1)

            def pT_wait(n):
                if n % 3 == 0:
                    pe.wait_ge(pT_dve, n // 3 + 1)
                else:
                    pe.wait_ge(pT_act, n - n // 3)

            def turn_probs(n):
                i = n // H
                pe.wait_ge(exped, n + 1)
                if n >= 1:
                    pT_wait(n - 1)
                ps = bank(4, 2)
                for j in range(i + 1):
                    ins = nc.tensor.transpose(ps[:, j * P:(j + 1) * P], sm[n % 3][:, j * P:(j + 1) * P], ident)
                ins.then_inc(pT_ready, 1)

            def weigh_values(n):
                i, h = divmod(n, H)
                pT_wait(n)
                if h == 0 and i >= 2:
                    pe.wait_ge(aT_copied, i - 1)
                acc = bank(6 + i % 2)
                for j in range(i + 1):
                    ins = mm(acc[:, h * DH:(h + 1) * DH], pt[n % 2][:, j * P:(j + 1) * P], v[:, j, h * DH:(h + 1) * DH],
                             start=(j == 0), stop=(j == i))
                ins.then_inc(pv_done, 1)

            def turn_attention(i):
                pe.wait_ge(an_ready, i + 1)
                ps = bank(6 + i % 2)
                for m in range(MA):
                    ins = nc.tensor.transpose(ps[:, m * P:(m + 1) * P], an[i % 2][:, m * P:(m + 1) * P], ident)
                ins.then_inc(aT_ready, 1)

            for g in range(len(groups) - 4, len(groups)):
                wait_emptied(pe, g)
            pe.wait_ge(s_attn, 1)
            for n in range(NSTEP + 6):
                if n < NSTEP:
                    scores(n)
                if 3 <= n < NSTEP + 3:
                    weigh_values(n - 3)
                if 2 <= n < NSTEP + 2:
                    turn_probs(n - 2)
                if n >= H + 5 and (n - 5) % H == 0:
                    turn_attention((n - 5) // H - 1)

            def project(t):
                w = rows(t)
                if t == 0:
                    pe.wait_ge(wo_ready, KD)
                pe.wait_ge(sq_ready, t + 1)
                if t:
                    pe.wait_ge(std_ac_ready, t)
                for c in range(2):
                    for m in range(MA):
                        ins = mm(bank(6)[0:w, 2 * t + c:2 * t + c + 1], sq[t % 2][:, c * MA + m, 0:w],
                                 ones[:, 0:1], start=(m == 0), stop=(m == MA - 1))
                ins.then_inc(ssq_ready, 1)
                pe.wait_ge(a_ready, t + 1)
                for half in range(2):
                    for c in range(2):
                        g = 4 * t + 2 * half + c
                        if g >= 4:
                            pe.wait_ge(o_used, g - 3)
                        out = bank(2 * half + c)[0:w, :]
                        cols = slice(half * 512, (half + 1) * 512)
                        for m in range(c * MA, (c + 1) * MA):
                            first_m, last_m = m == c * MA, m == (c + 1) * MA - 1
                            hi, lo = a_hi[t % 2][:, m, :], a_lo[t % 2][:, m, :]
                            if w < P:
                                out = bank(2 * half + c)
                            mm(out, hi, wo_hi[:, m, cols], start=first_m, stop=False)
                            mm(out, lo, wo_hi[:, m, cols], start=False, stop=False)
                            ins = mm(out, hi, wo_lo[:, m, cols], start=False, stop=last_m)
                        ins.then_inc(o_ready, 1)

            def route(t):
                w = rows(t)
                pe.wait_ge(h2_ready, t + 1)
                if t == 0:
                    pe.wait_ge(router_in, 48)
                for half in range(2):
                    if t >= 1:
                        pe.wait_ge(h2T_copied, 2 * t)
                    for c in range(4):
                        k = 4 * half + c
                        ins = nc.tensor.transpose(bank(4 + half)[:, c * w:(c + 1) * w],
                                                  h2[t % 2][0:w, k * P:(k + 1) * P], ident[0:w, 0:w])
                    ins.then_inc(h2T_ready, 1)
                pe.wait_ge(h2T_copied, 2 * t + 2)
                if t:
                    pe.wait_ge(lg_used, t)
                NR = NGRP + NE
                for k in range(KD):
                    ins = mm(bank(7)[0:w, t * NR:(t + 1) * NR], h2T[t % 2][:, k, 0:w], wr[:, k, :],
                             start=(k == 0), stop=(k == KD - 1))
                ins.then_inc(lg_ready, 1)

            for t in range(NT + 1):
                if t < NT:
                    project(t)
                if t >= 1:
                    route(t - 1)

            pe.wait_ge(assigned, 1)
            pe.wait_ge(o_used, 4 * NT)
            for t in range(NT):
                w = rows(t)
                if t:
                    mm(bank(0)[0:w, t * NE:(t + 1) * NE], ones[:, 0:w], r_sum[:, t, :], start=True, stop=False)
                mm(bank(0)[0:w, t * NE:(t + 1) * NE], before[0:w, 0:w], r_hot[0:w, t, :], start=(t == 0), stop=True)
            mm(bank(0)[:, NT * NE:(NT + 1) * NE], ones, r_sum[:, NQ, :], start=True, stop=False)
            mm(bank(0)[:, NT * NE:(NT + 1) * NE], ones[0:NS, :], r_hot[0:NS, NQ, :], start=False, stop=True
               ).then_inc(ranked, 1)
            for n in range(2 * NT):
                w = rows(n // 2)
                pe.wait_ge(hot_ready, n + 1)
                ins = mm(bank(1)[0:SLOTS, 0:2 * NBLK], hot_slot[n % 2][0:w, :], hot_blk[n % 2][0:w, :],
                         start=(n == 0), stop=(n == 2 * NT - 1))
                ins.then_inc(hot_used, 1)

            def turn_rows(f):
                for k in range(KD):
                    ins = nc.tensor.transpose(bank(4 + k // 4)[:, (k % 4) * SLOTS:(k % 4 + 1) * SLOTS],
                                              xg[:, k * P:(k + 1) * P], ident[0:SLOTS, 0:SLOTS])
                    if k % 4 == 3:
                        ins.then_inc(f.xT_ready, 1)

            def gate_or_up(w, s, b, done):
                for m in range(DE // P):
                    for k in range(KD):
                        ins = mm(bank(b)[:, m * SLOTS:(m + 1) * SLOTS], w[s][:, k, m * P:(m + 1) * P], xT[:, k, :],
                                 start=(k == 0), stop=(k == KD - 1))
                ins.then_inc(done, 1)

            def down(f, s):
                for half in range(2):
                    for m in range(DE // P):
                        ins = mm(bank(2 + half)[0:SLOTS, :], hid[:, m, :], wd[s][:, m, half * 512:(half + 1) * 512],
                                 start=(m == 0), stop=(m == DE // P - 1))
                ins.then_inc(f.y_done, 1)

            def expert(b, turns, s, turn_next=True):
                pe.wait_ge(first.xT_act, b + 1)
                pe.wait_ge(first.xT_dve, b + 1)
                pe.wait_ge(first.gate_in[s], 16 * turns + 16)
                gate_or_up(wg, s, 0, first.gate_done)
                pe.wait_ge(first.up_in[s], 16 * turns + 16)
                gate_or_up(wu, s, 1, first.up_done)
                if turn_next:
                    pe.wait_ge(first.rows_in, 16 * b + 32)
                    turn_rows(first)
                pe.wait_ge(first.down_in[s], 16 * turns + 16)
                pe.wait_ge(first.hid_done, b + 1)
                if not isinstance(b, int) or b > 0:
                    pe.wait_ge(first.y_act, b)
                    pe.wait_ge(first.y_dve, b)
                down(first, s)

            pe.wait_ge(routed, 1)
            pe.wait_ge(first.rows_in, 16)
            turn_rows(first)
            expert(0, 0, 0)
            expert(1, 0, 1)
            with pe.Fori(0, NE // 3 - 1, 1) as j:
                expert(3 * j + 2, j, 2)
                expert(3 * j + 3, j + 1, 0)
                expert(3 * j + 4, j + 1, 1)
            expert(NE - 3, NE // 3 - 1, 2)
            expert(NE - 2, NE // 3, 0)
            expert(NE - 1, NE // 3, 1, False)
            pe.wait_ge(first.y_act, NE)
            pe.wait_ge(first.y_dve, NE)
            more = pe.value_load(oexp[0:1, OVER:OVER + 1], min_val=0, max_val=OVER)
            with pe.If(more > 0):
                with pe.Fori(0, more, 1) as o:
                    pe.wait_ge(further.rows_in, 16 * o + 16)
                    turn_rows(further)
                    pe.wait_ge(further.xT_act, o + 1)
                    pe.wait_ge(further.xT_dve, o + 1)
                    pe.wait_ge(further.gate_in[0], 16 * o + 16)
                    gate_or_up(wg, 0, 0, further.gate_done)
                    pe.wait_ge(further.up_in[0], 16 * o + 16)
                    gate_or_up(wu, 0, 1, further.up_done)
                    pe.wait_ge(further.down_in[0], 16 * o + 16)
                    pe.wait_ge(further.hid_done, o + 1)
                    down(further, 0)
                    pe.wait_ge(further.y_act, o + 1)
                    pe.wait_ge(further.y_dve, o + 1)

        def unload_group(eng, copy, g):
            kind, i, n = groups[g]
            ps = group_psum(g)
            if kind == "k":
                return copy(kT[:, i, n * TC:(n + 1) * TC], ps[:, 0:TC])
            if kind == "rows":
                return copy(srow[:, i, :], ps[0:NS, :])
            if kind == "v":
                return copy(vT[i % 2][:, n * TC:(n + 1) * TC], ps[:, 0:TC])
            if kind == "vn":
                cols = slice(i * P, (i + 1) * P)
                if n == 2:
                    return copy(srow[:, 2, cols], ps[0:NS, 0:P])
                return copy(v[:, 4 * n:4 * n + 4, cols], ps[:, :].rearrange("p (t c) -> p t c", t=4))
            if kind == "kn":
                return copy(kn[:, i, :], ps[:, :])

        @block.scalar
        def _(act):
            steps = [0]

            def step(ins):
                steps[0] += 1
                ins.then_inc(act_step, 1)
                act.wait_ge(act_step, steps[0])

            def square_sum(t):
                w = rows(t)
                act.wait_ge(x_in[t], 16)
                step(nc.scalar.activation(junk[0:w, :], xt[t % NXT][0:w, :], ACT.Square, accum_out=ssq_x[0:w, t:t + 1]))
                nc.scalar.activation(std_x[0:w, t:t + 1], ssq_x[0:w, t:t + 1], ACT.Sqrt, bias=eps[0:w, :],
                                     scale=1.0 / D).then_inc(std_ready, 1)

            def upper_weights(t):
                act.wait_ge(win_in[t % 3], 16 * (t // 3 + 1))
                if t >= 2:
                    kind, m = tiles[t - 2]
                    act.wait_ge(group_done, number[kind, m, 2] + 1)
                nc.scalar.copy(w_hi[t % 2], w_raw[t % 3]).then_inc(w_hi_ready, 1)

            act.wait_ge(const_in, 16)
            square_sum(0)
            square_sum(1)
            upper_weights(0)
            for g, (kind, i, n) in enumerate(groups):
                if n == 0 and (kind, i) in tiles and tiles.index((kind, i)) + 1 < len(tiles):
                    upper_weights(tiles.index((kind, i)) + 1)
                if kind == "x":
                    w = rows(i)
                    act.wait_ge(group_done, g + 1)
                    nc.scalar.copy(h_hi[:, 4 * n:4 * n + 4, i * P:i * P + w],
                                   group_psum(g)[:, 0:4 * w].rearrange("p (k t) -> p k t", k=4)
                                   ).then_inc(h_hi_ready, 1)
                    if n == 0 and i + 2 < NT:
                        square_sum(i + 2)
                if taker[g][0] == "act":
                    act.wait_ge(group_done, g + 1)
                    if kind == "q":
                        ins = nc.scalar.mul(qT[:, i, n * TC:(n + 1) * TC], group_psum(g)[:, 0:TC], DH ** -0.5)
                    elif kind == "c":
                        if i >= 1:
                            wait_emptied(act, number["u", i - 1, n])
                        else:
                            act.wait_ge(group_done, number["vn", MA - 1, 2] + 1)
                        ins = nc.scalar.copy(cc[:, n * TC:(n + 1) * TC], group_psum(g)[:, 0:TC])
                    else:
                        if kind == "v" and i >= 2:
                            act.wait_ge(group_done, number["vn", i - 2, 2] + 1)
                        ins = unload_group(act, nc.scalar.copy, g)
                    ins.then_inc(act_emptied, 1)
                if n < 2 or (kind, i) not in tiles:
                    continue
                if tiles.index((kind, i)) == 18:
                    act.wait_ge(smax_ready, 1)
                    nc.scalar.activation(sprob, bank(6)[0:64, 0:3 * P + NS], ACT.Exp, bias=sneg,
                                         accum_out=sl).then_inc(sexp_ready, 1)
                if tiles.index((kind, i)) == 20:
                    act.wait_ge(spT_ready, 1)
                    nc.scalar.copy(sprobT[0:NS, 3, :], bank(7)[0:NS, 192:256])
                    nc.scalar.copy(sprobT[:, 0:3, :], bank(7)[:, 0:192].rearrange("p (r c) -> p r c", r=3)
                                   ).then_inc(spT_copied, 1)

            def copy_pT(n):
                w = (n // H + 1) * P
                act.wait_ge(pT_ready, n + 1)
                if n >= 2:
                    act.wait_ge(pv_done, n - 1)
                nc.scalar.copy(pt[n % 2][:, 0:w], bank(4, 2)[:, 0:w]).then_inc(pT_act, 1)

            def exponent(n):
                i, h = divmod(n, H)
                w = (i + 1) * P
                act.wait_ge(masked, n + 1)
                if h == 0 and i >= 2:
                    act.wait_ge(an_ready, i - 1)
                c = (i % 2) * H + h
                nc.scalar.activation(sm[n % 3][:, 0:w], sm[n % 3][:, 0:w], ACT.Exp, bias=neg_n[:, n % 3:n % 3 + 1],
                                     accum_out=lsum[:, c:c + 1]).then_inc(exped, 1)

            def copy_aT(i):
                act.wait_ge(aT_ready, i + 1)
                nc.scalar.copy(qT[:, :, i * P:(i + 1) * P], bank(6 + i % 2).rearrange("p (m t) -> p m t", m=MA)
                               ).then_inc(aT_copied, 1)

            def upper_wo(k):
                act.wait_ge(wo_in[k % 4], 16 * (k // 4 + 1))
                nc.scalar.activation(wo_hi[:, k, :], wo_raw[k % 4], ACT.Copy, scale=gout[:, k:k + 1]
                                     ).then_inc(wo_hi_ready, 1)

            for n in range(NSTEP + 6):
                if 2 <= n < NSTEP + 2 and (n - 2) % 3:
                    copy_pT(n - 2)
                if n < NSTEP:
                    exponent(n)
                if n >= H + 5 and (n - 5) % H == 0:
                    copy_aT((n - 5) // H - 1)
                if WO_AT <= n < WO_AT + KD:
                    upper_wo(n - WO_AT)

            def squares(t):
                w = rows(t)
                if t == 0:
                    act.wait_ge(wo_ready, KD)
                    act.wait_ge(pT_ready, NSTEP)
                    act.wait_ge(pv_done, NSTEP)
                if t >= 2:
                    act.wait_ge(o_ready, 4 * (t - 1))
                cols = slice(t * P, t * P + w)
                nc.scalar.activation(sq[t % 2][:, 0:MA, 0:w], qT[:, :, cols], ACT.Square)
                nc.scalar.activation(sq[t % 2][:, MA:2 * MA, 0:w], cT[:, :, cols], ACT.Square).then_inc(sq_ready, 1)
                nc.scalar.copy(a_hi[t % 2][:, 0:MA, 0:w], qT[:, :, cols])
                nc.scalar.copy(a_hi[t % 2][:, MA:2 * MA, 0:w], cT[:, :, cols]).then_inc(a_hi_ready, 1)

            def roots(t):
                w = rows(t)
                act.wait_ge(ssq_ready, t + 1)
                if t >= 1:
                    act.wait_ge(o_used, 4 * t)
                nc.scalar.activation(std_ac[0:w, :], bank(6)[0:w, 2 * t:2 * t + 2], ACT.Sqrt, bias=eps[0:w, :],
                                     scale=1.0 / DA).then_inc(std_ac_ready, 1)

            def root_ffn(t):
                w = rows(t)
                act.wait_ge(o_used, 4 * t + 4)
                if t >= 2:
                    act.wait_ge(h2T_ready, 2 * (t - 1))
                    act.wait_ge(h2_out[t % 2], 16 * (t // 2))
                c = t % 2
                step(nc.scalar.activation(h2[c][0:w, :], xres[0:w, t, :], ACT.Square, accum_out=ssq_f[0:w, c:c + 1]))
                nc.scalar.activation(std_f[0:w, c:c + 1], ssq_f[0:w, c:c + 1], ACT.Sqrt, bias=eps[0:w, :],
                                     scale=1.0 / D).then_inc(std_f_ready, 1)

            def copy_h2T(t):
                w = rows(t)
                for half in range(2):
                    act.wait_ge(h2T_ready, 2 * t + half + 1)
                    if t >= 2:
                        act.wait_ge(lg_ready, t - 1)
                    nc.scalar.copy(h2T[t % 2][:, 4 * half:4 * half + 4, 0:w],
                                   bank(4 + half)[:, 0:4 * w].rearrange("p (k t) -> p k t", k=4)
                                   ).then_inc(h2T_copied, 1)

            squares(0)
            for t in range(NT):
                if t + 1 < NT:
                    squares(t + 1)
                roots(t)
                root_ffn(t)
                copy_h2T(t)
            act.wait_ge(gd_ready, 1)
            nc.scalar.activation(r_d, r_d, ACT.Exp).then_inc(gexp_ready, 1)
            act.wait_ge(vd_ready, 1)
            nc.scalar.activation(r_vd, r_vd, ACT.Exp).then_inc(vexp_ready, 1)

            def copy_xT(f, n):
                act.wait_ge(f.xT_ready, 2 * n + 1)
                nc.scalar.copy(xT[:, 0:4, :], bank(4)[:, 0:4 * SLOTS].rearrange("p (k t) -> p k t", k=4)
                               ).then_inc(f.xT_act, 1)

            def silu(f, n):
                act.wait_ge(f.gate_done, n + 1)
                nc.scalar.activation(sg, bank(0)[:, 0:4 * SLOTS].rearrange("p (m t) -> p m t", m=4), ACT.Silu
                                     ).then_inc(f.silu_done, 1)

            def copy_y(f, n, before=0):
                act.wait_ge(f.y_done, n + (before + 1))
                nc.scalar.copy(ysb[:, 0:512], bank(2)[0:SLOTS, :]).then_inc(f.y_act, 1)

            def expert(b, turn_next=True):
                silu(first, b)
                if turn_next:
                    copy_xT(first, b + 1)
                if not isinstance(b, int) or b > 0:
                    act.wait_ge(first.sent, 16 * b)
                copy_y(first, b)

            copy_xT(first, 0)
            expert(0)
            with act.Fori(1, NE - 1, 1) as b:
                expert(b)
            expert(NE - 1, False)
            act.wait_ge(first.sent, 16 * NE)
            more = act.value_load(oexp[0:1, OVER:OVER + 1], min_val=0, max_val=OVER)
            with act.If(more > 0):
                with act.Fori(0, more, 1) as o:
                    copy_xT(further, o)
                    silu(further, o)
                    copy_y(further, o, NE)
                    act.wait_ge(further.sent, 16 * o + 16)

            for t in range(NT):
                w = rows(t)
                act.wait_ge(fin_res, t + 1)
                c = t % 2
                step(nc.scalar.activation(fjunk[0:w, :], xres[0:w, t, :], ACT.Square, accum_out=ssq_f[0:w, c:c + 1]))
                if t >= 2:
                    act.wait_ge(fin_out, t - 1)
                nc.scalar.activation(std_f[0:w, c:c + 1], ssq_f[0:w, c:c + 1], ACT.Sqrt, bias=eps[0:w, :],
                                     scale=1.0 / D).then_inc(fin_std, 1)

        @block.vector
        def _(dve):
            vec = nc.vector
            steps = [0]

            def step(ins):
                steps[0] += 1
                ins.then_inc(dve_step, 1)
                dve.wait_ge(dve_step, steps[0])

            def normalise(t):
                w = rows(t)
                dve.wait_ge(std_ready, t + 1)
                step(vec.reciprocal(rst_x[0:w, t:t + 1], std_x[0:w, t:t + 1]))
                if t >= 2:
                    dve.wait_ge(group_done, number["x", t - 2, 1] + 1)
                vec.scalar_tensor_tensor(out=xn[t % 2][0:w, :], in0=xt[t % NXT][0:w, :], scalar=rst_x[0:w, t:t + 1],
                                         in1=gmix[0:w, :], op0=ALU.mult, op1=ALU.mult).then_inc(xn_ready, 1)

            def lower_weights(t):
                dve.wait_ge(w_hi_ready, t + 1)
                vec.tensor_tensor(w_lo[t % 2], w_raw[t % 3], w_hi[t % 2].bitcast(F32), ALU.subtract
                                  ).then_inc(w_ready, 1)

            def sample_scores(b):
                if b == 0:
                    dve.wait_ge(small_in, 16 * 4)
                dve.wait_ge(kv_in[b % 2], 48 * (b // 2 + 1))
                dve.wait_ge(qb_ready, b + 1)
                q = bank(4 + b % 2)
                for r in range(3):
                    keys = kv[:, b % 2, r * DA:(r + 1) * DA]
                    step(vec.tensor_tensor(keys, keys, q, ALU.mult))
                    vec.tensor_reduce(sscore[:, r, b * H:(b + 1) * H], keys.rearrange("p (h d) -> p h d", h=H),
                                      X, ALU.add)
                step(vec.tensor_tensor(own, srow[:, 1, :], q[0:NS, :], ALU.mult))
                cols = slice(b * H, (b + 1) * H)
                step(vec.tensor_reduce(sscore[0:NS, 3, cols], own.rearrange("p (h d) -> p h d", h=H), X, ALU.add))
                vec.tensor_tensor(sscore[0:NS, 3, cols], sscore[0:NS, 3, cols], ssm[:, cols], ALU.add
                                  ).then_inc(scored, 1)

            def conv(m):
                step(vec.tensor_scalar(z[:, 0:SEQ], u[:, 0:SEQ], cw[:, m, 0:1], None, ALU.mult))
                for j in (1, 2):
                    step(vec.scalar_tensor_tensor(out=z[:, 0:SEQ], in0=u[:, j:j + SEQ], scalar=cw[:, m, j:j + 1],
                                                  in1=z[:, 0:SEQ], op0=ALU.mult, op1=ALU.add))
                zs = z[:, SEQ:NTOK]
                step(vec.tensor_scalar(zs, cstate[:, m, 0, :], cw[:, m, 0:1], None, ALU.mult))
                for j in (1, 2):
                    src = cstate[:, m, 1, :] if j == 1 else u[:, SEQ + 2:NTOK + 2]
                    step(vec.scalar_tensor_tensor(out=zs, in0=src, scalar=cw[:, m, j:j + 1], in1=zs,
                                                  op0=ALU.mult, op1=ALU.add))
                vec.tensor_copy(uout[:, m, :], u[:, SEQ:NTOK + 2]).then_inc(u_ready, 1)

            dve.wait_ge(const_in, 16)
            dve.wait_ge(gmix_in, 16)
            normalise(0)
            normalise(1)
            lower_weights(0)
            for g, (kind, i, n) in enumerate(groups):
                if n == 0 and (kind, i) in tiles and tiles.index((kind, i)) + 1 < len(tiles):
                    lower_weights(tiles.index((kind, i)) + 1)
                if taker[g][0] == "dve":
                    dve.wait_ge(group_done, g + 1)
                    ps = group_psum(g)
                    if kind == "x":
                        w = rows(i)
                        dve.wait_ge(h_hi_ready, 2 * i + n + 1)
                        there = slice(i * P, i * P + w)
                        ins = vec.tensor_tensor(h_lo[:, 4 * n:4 * n + 4, there],
                                                ps[:, 0:4 * w].rearrange("p (k t) -> p k t", k=4),
                                                h_hi[:, 4 * n:4 * n + 4, there].bitcast(F32), ALU.subtract)
                    elif kind == "q":
                        ins = vec.tensor_scalar(qT[:, i, n * TC:(n + 1) * TC], ps[:, 0:TC], DH ** -0.5, None, ALU.mult)
                    elif kind == "u":
                        if i == 0 and n == 0:
                            step(vec.memset(u[:, 0:2], 0.0))
                        wait_emptied(dve, number["c", i, n])
                        ins = vec.tensor_tensor(u[:, 2 + n * TC:2 + (n + 1) * TC], ps[:, 0:TC],
                                                cc[:, n * TC:(n + 1) * TC], ALU.mult)
                    elif kind == "b":
                        if i == 0 and n == 0:
                            dve.wait_ge(kn_out, 16)
                        ins = vec.tensor_tensor(cT[:, i, n * TC:(n + 1) * TC], ps[:, 0:TC],
                                                z[:, n * TC:(n + 1) * TC], ALU.mult)
                    else:
                        if kind == "v" and i >= 2:
                            dve.wait_ge(group_done, number["vn", i - 2, 2] + 1)
                        ins = unload_group(dve, vec.tensor_copy, g)
                    ins.then_inc(dve_emptied, 1)
                    if kind == "x" and n == 1 and i + 2 < NT:
                        normalise(i + 2)
                if n < 2 or (kind, i) not in tiles:
                    continue
                t = tiles.index((kind, i))
                if kind == "u":
                    if i == 0:
                        dve.wait_ge(small_in, 16 * 4)
                    dve.wait_ge(dve_emptied, taker[g][1])
                    conv(i)
                if 8 <= t < 8 + NS:
                    sample_scores(t - 8)
                if t == 17:
                    dve.wait_ge(sT_ready, 1)
                    step(vec.tensor_reduce(smx, bank(6)[0:64, 0:3 * P + NS], X, ALU.max))
                    vec.tensor_scalar(sneg, smx, -1.0, None, ALU.mult).then_inc(smax_ready, 1)
                if t == 19:
                    dve.wait_ge(sexp_ready, 1)
                    step(vec.reciprocal(srl, sl))
                    vec.tensor_scalar(sprob, sprob, srl, None, ALU.mult).then_inc(sp_ready, 1)
            dve.wait_ge(spv_ready, 1)
            out = bank(4).rearrange("p (m b h) -> p m b h", m=8, b=NS)
            for m in range(MA):
                for e in range(2):
                    part = slice(e * DH, (e + 1) * DH)
                    ins = vec.tensor_copy(qT[part, m, SEQ:NTOK], out[part, m, :, 2 * m + e])
            ins.then_inc(s_attn, 1)

            def mask(n):
                i = n // H
                w = (i + 1) * P
                if n == 0:
                    dve.wait_ge(mask_in, 16)
                dve.wait_ge(s_ready, n + 1)
                if n >= 3:
                    dve.wait_ge(pT_ready, n - 2)
                c = n % 3
                step(vec.tensor_tensor_reduce(sm[c][:, 0:w], bank(2 * (n % 2), 2)[:, 0:w], amask[:, SEQ - w:SEQ],
                                              1.0, NEG, ALU.add, ALU.max, mx_n[:, c:c + 1]))
                vec.tensor_scalar(neg_n[:, c:c + 1], mx_n[:, c:c + 1], -1.0, None, ALU.mult).then_inc(masked, 1)

            def copy_pT(n):
                w = (n // H + 1) * P
                dve.wait_ge(pT_ready, n + 1)
                if n >= 2:
                    dve.wait_ge(pv_done, n - 1)
                vec.tensor_copy(pt[n % 2][:, 0:w], bank(4, 2)[:, 0:w]).then_inc(pT_dve, 1)

            def divide(i):
                c = slice((i % 2) * H, (i % 2) * H + H)
                dve.wait_ge(pv_done, H * (i + 1))
                if i >= 2:
                    dve.wait_ge(aT_ready, i - 1)
                step(vec.reciprocal(rl[:, c], lsum[:, c]))
                vec.tensor_tensor(an[i % 2].rearrange("p (h d) -> p h d", h=H),
                                  bank(6 + i % 2).rearrange("p (h d) -> p h d", h=H),
                                  rl[:, c].unsqueeze(2).broadcast_to([P, H, DH]), ALU.mult).then_inc(an_ready, 1)

            def lower_wo(k):
                dve.wait_ge(wo_hi_ready, k + 1)
                vec.scalar_tensor_tensor(out=wo_lo[:, k, :], in0=wo_raw[k % 4], scalar=gout[:, k:k + 1],
                                         in1=wo_hi[:, k, :].bitcast(F32), op0=ALU.mult, op1=ALU.subtract
                                         ).then_inc(wo_ready, 1)

            for n in range(NSTEP + 6):
                if n < NSTEP:
                    mask(n)
                if 2 <= n < NSTEP + 2 and (n - 2) % 3 == 0:
                    copy_pT(n - 2)
                if n >= H + 3 and (n - 3) % H == 0:
                    divide((n - 3) // H - 1)
                if WO_AT <= n < WO_AT + KD:
                    lower_wo(n - WO_AT)

            def lower_attention(t):
                w = rows(t)
                dve.wait_ge(a_hi_ready, t + 1)
                for c, src in enumerate((qT, cT)):
                    m = slice(c * MA, (c + 1) * MA)
                    ins = vec.tensor_tensor(a_lo[t % 2][:, m, 0:w], src[:, :, t * P:t * P + w],
                                            a_hi[t % 2][:, m, 0:w].bitcast(F32), ALU.subtract)
                ins.then_inc(a_ready, 1)

            def residual(t):
                w = rows(t)
                dve.wait_ge(xres_in[t], 16)
                dve.wait_ge(std_ac_ready, t + 1)
                step(vec.reciprocal(rst_ac[0:w, :], std_ac[0:w, :]))
                for half in range(2):
                    x = xres[0:w, t, half * 512:(half + 1) * 512]
                    for c in range(2):
                        dve.wait_ge(o_ready, 4 * t + 2 * half + c + 1)
                        ins = vec.scalar_tensor_tensor(out=x, in0=bank(2 * half + c)[0:w, :], scalar=rst_ac[0:w, c:c + 1],
                                                       in1=x, op0=ALU.mult, op1=ALU.add)
                        ins.then_inc(o_used, 1)
                        dve.wait_ge(o_used, 4 * t + 2 * half + c + 1)

            def router_rows(t):
                w = rows(t)
                c = t % 2
                dve.wait_ge(std_f_ready, t + 1)
                step(vec.reciprocal(rst_f[0:w, c:c + 1], std_f[0:w, c:c + 1]))
                vec.scalar_tensor_tensor(out=h2[c][0:w, :], in0=xres[0:w, t, :], scalar=rst_f[0:w, c:c + 1],
                                         in1=gffn[0:w, :], op0=ALU.mult, op1=ALU.mult).then_inc(h2_ready, 1)

            dve.wait_ge(router_in, 48)
            step(vec.memset(lg, 0.0))
            lower_attention(0)
            for t in range(NT):
                if t + 1 < NT:
                    lower_attention(t + 1)
                residual(t)
                router_rows(t)
                w = rows(t)
                NR = NGRP + NE
                if t >= 1:
                    w = rows(t - 1)
                    dve.wait_ge(lg_ready, t)
                    vec.tensor_tensor(lg[0:w, t - 1, :], bank(7)[0:w, (t - 1) * NR:t * NR], rbias[0:w, :], ALU.add
                                      ).then_inc(lg_used, 1)
            dve.wait_ge(lg_ready, NT)
            vec.tensor_tensor(lg[0:NS, NQ, :], bank(7)[0:NS, NQ * NR:NT * NR], rbias[0:NS, :], ALU.add
                              ).then_inc(lg_used, 1)
            dve.wait_ge(lg_used, NT)
            dve.wait_ge(h2_out[0], 16 * 5)
            dve.wait_ge(h2_out[1], 16 * 4)

            def wide(x9, n):
                return x9.unsqueeze(2).broadcast_to([P, NT, n])

            def ramps(n):
                return ramp[:, 0:n].unsqueeze(1).broadcast_to([P, NT, n])

            def first_index(dst, eq, n):
                step(vec.scalar_tensor_tensor(out=eq, in0=eq, scalar=-float(n), in1=ramps(n), op0=ALU.mult,
                                              op1=ALU.add))
                step(vec.tensor_reduce(dst, eq, X, ALU.min))
                step(vec.tensor_scalar(dst, dst, float(n), None, ALU.add))

            gl = lg[:, :, 0:NGRP]
            step(vec.tensor_reduce(r_gm, gl, X, ALU.max))
            step(vec.tensor_tensor(r_eq, gl, wide(r_gm, NGRP), ALU.is_equal))
            vec.tensor_tensor(r_d, gl, wide(r_gm, NGRP), ALU.subtract).then_inc(gd_ready, 1)
            first_index(r_gi, r_eq, NGRP)
            step(vec.tensor_tensor(r_goh, ramps(NGRP), wide(r_gi, NGRP), ALU.is_equal))
            for g in range(NGRP):
                el = lg[:, :, NGRP + g * EPG:NGRP + (g + 1) * EPG]
                dst = r_le if g == 0 else r_eq8
                step(vec.tensor_tensor(dst, el, r_goh[:, :, g:g + 1].broadcast_to([P, NT, EPG]), ALU.mult))
                if g:
                    step(vec.tensor_tensor(r_le, r_le, r_eq8, ALU.add))
            step(vec.tensor_reduce(r_v1, r_le, X, ALU.max))
            step(vec.tensor_tensor(r_eq8, r_le, wide(r_v1, EPG), ALU.is_equal))
            first_index(r_i1, r_eq8, EPG)
            step(vec.tensor_tensor(r_oh, ramps(EPG), wide(r_i1, EPG), ALU.is_equal))
            step(vec.scalar_tensor_tensor(out=r_le2, in0=r_oh, scalar=-3e38, in1=r_le, op0=ALU.mult, op1=ALU.add))
            step(vec.tensor_reduce(r_v2, r_le2, X, ALU.max))
            step(vec.tensor_tensor(r_eq8, r_le2, wide(r_v2, EPG), ALU.is_equal))
            first_index(r_i2, r_eq8, EPG)
            vec.tensor_tensor(r_vd, r_v2, r_v1, ALU.subtract).then_inc(vd_ready, 1)
            for c, idx in enumerate((r_i1, r_i2)):
                step(vec.scalar_tensor_tensor(out=r_e[:, c, :], in0=r_gi, scalar=float(EPG), in1=idx, op0=ALU.mult,
                                              op1=ALU.add))
            step(vec.tensor_tensor(r_hot1, ramps(NE), wide(r_e[:, 0, :], NE), ALU.is_equal))
            step(vec.tensor_tensor(r_hot2, ramps(NE), wide(r_e[:, 1, :], NE), ALU.is_equal))
            step(vec.tensor_tensor(r_hot, r_hot1, r_hot2, ALU.add))
            step(vec.memset(r_sum[:, 0, :], 0.0))
            for t in range(1, NT):
                ins = vec.tensor_tensor(r_sum[:, t, :], r_sum[:, t - 1, :], r_hot[:, t - 1, :], ALU.add)
                if t < NT - 1:
                    step(ins)
            ins.then_inc(assigned, 1)
            dve.wait_ge(gexp_ready, 1)
            step(vec.tensor_reduce(r_sg, r_d, X, ALU.add))
            step(vec.reciprocal(r_pg, r_sg))
            dve.wait_ge(vexp_ready, 1)
            step(vec.tensor_scalar(r_den, r_vd, 1.0, None, ALU.add))
            step(vec.reciprocal(r_t9, r_den))
            step(vec.tensor_tensor(gates[:, 0, :], r_t9, r_pg, ALU.mult))
            step(vec.tensor_tensor(gates[:, 1, :], gates[:, 0, :], r_vd, ALU.mult))
            step(vec.memset(r_rank, 0.0))
            dve.wait_ge(ranked, 1)
            vec.tensor_copy(r_rank[0:NS, NQ, :], bank(0)[0:NS, NQ * NE:NT * NE])
            vec.tensor_copy(r_rank[:, 0:NQ, :], bank(0)[:, 0:NQ * NE].rearrange("p (t e) -> p t e", t=NQ))
            step(vec.tensor_copy(r_rank[:, NT, :], bank(0)[:, NT * NE:(NT + 1) * NE]))
            count = r_rank[:, NT, :]
            step(vec.tensor_scalar(r_ob, count, float(SLOTS), None, ALU.is_gt))
            for m in range(2, MORE + 1):
                step(vec.scalar_tensor_tensor(out=r_ob, in0=count, scalar=float(m * SLOTS), in1=r_ob, op0=ALU.is_gt,
                                              op1=ALU.add))
            step(vec.tensor_tensor_scan(r_inc, ones[:, 0:NE], r_ob, 0.0, ALU.mult, ALU.add))
            step(vec.tensor_tensor(r_exc, r_inc, r_ob, ALU.subtract))
            for c, hot in enumerate((r_hot1, r_hot2)):
                step(vec.tensor_tensor(r_big, hot, r_rank[:, 0:NT, :], ALU.mult))
                step(vec.tensor_reduce(r_r[:, c, :], r_big, X, ALU.add))
                step(vec.tensor_tensor(r_big, hot, r_exc.unsqueeze(1).broadcast_to([P, NT, NE]), ALU.mult))
                step(vec.tensor_reduce(r_so[:, c, :], r_big, X, ALU.add))
            step(vec.tensor_scalar(r_q, r_r, float(SLOTS), None, ALU.is_ge))
            step(vec.tensor_copy(r_is, r_q))
            for m in range(2, MORE + 1):
                step(vec.scalar_tensor_tensor(out=r_q, in0=r_r, scalar=float(m * SLOTS), in1=r_q, op0=ALU.is_ge,
                                              op1=ALU.add))
            step(vec.scalar_tensor_tensor(out=r_j, in0=r_q, scalar=-float(SLOTS), in1=r_r, op0=ALU.mult, op1=ALU.add))
            step(vec.tensor_tensor(r_blk, r_so, r_q, ALU.add))
            step(vec.tensor_tensor(r_blk, r_blk, r_e, ALU.subtract))
            step(vec.scalar_tensor_tensor(out=r_blk, in0=r_blk, scalar=float(NE - 1), in1=r_is, op0=ALU.add,
                                          op1=ALU.mult))
            step(vec.tensor_tensor(r_blk, r_blk, r_e, ALU.add))
            for n in range(2 * NT):
                t, c = divmod(n, 2)
                w = rows(t)
                if n >= 2:
                    dve.wait_ge(hot_used, n - 1)
                vec.tensor_scalar(hot_slot[c][0:w, :], ramp[0:w, 0:SLOTS], r_j[0:w, c, t:t + 1], None, ALU.is_equal)
                vec.tensor_scalar(hot_blk[c][0:w, 0:NBLK], ramp[0:w, 0:NBLK], r_blk[0:w, c, t:t + 1],
                                  tokv[0:w, t:t + 1], ALU.is_equal, ALU.mult)
                vec.tensor_scalar(hot_blk[c][0:w, NBLK:2 * NBLK], ramp[0:w, 0:NBLK], r_blk[0:w, c, t:t + 1],
                                  (tokv, destv)[c][0:w, t:t + 1], ALU.is_equal, ALU.mult).then_inc(hot_ready, 1)
            step(vec.tensor_tensor(r_cmp[0:1], r_inc[0:1].unsqueeze(1).broadcast_to([1, OVER, NE]),
                                   ramp[0:1, 0:OVER].unsqueeze(2).broadcast_to([1, OVER, NE]), ALU.is_le))
            step(vec.tensor_reduce(r_tab2[0:1, 0:OVER], r_cmp[0:1], X, ALU.add))
            step(vec.tensor_scalar(r_tab2[0:1, 0:OVER], r_tab2[0:1, 0:OVER], float(NE - 1), None, ALU.min))
            vec.tensor_copy(oexp[0:1, 0:OVER], r_tab2[0:1, 0:OVER])
            vec.tensor_copy(oexp[0:1, OVER:OVER + 1], r_inc[0:1, NE - 1:NE])
            dve.wait_ge(hot_used, 2 * NT)
            tab = bank(1)[0:SLOTS, 0:2 * NBLK]
            step(vec.tensor_scalar(r_tab[0:SLOTS, 0, :], tab[:, 0:NBLK], -1.0, 0.0, ALU.add, ALU.max))
            step(vec.tensor_scalar(r_tab2[0:SLOTS], tab[:, NBLK:2 * NBLK], 0.0, DROP, ALU.is_equal, ALU.mult))
            step(vec.scalar_tensor_tensor(out=r_tab[0:SLOTS, 1, :], in0=tab[:, NBLK:2 * NBLK], scalar=-1.0,
                                          in1=r_tab2[0:SLOTS], op0=ALU.add, op1=ALU.add))
            vec.tensor_copy(gi_s, r_tab[0:SLOTS, 0, 0:1])
            step(vec.tensor_copy(gidx[:], r_tab[0:SLOTS, 0, :]))
            vec.tensor_copy(sidx[:], r_tab[0:SLOTS, 1, :]).then_inc(routed, 1)

            def copy_xT(f, n):
                dve.wait_ge(f.xT_ready, 2 * n + 2)
                vec.tensor_copy(xT[:, 4:8, :], bank(5)[:, 0:4 * SLOTS].rearrange("p (k t) -> p k t", k=4)
                                ).then_inc(f.xT_dve, 1)

            def hidden(f, n):
                dve.wait_ge(f.silu_done, n + 1)
                dve.wait_ge(f.up_done, n + 1)
                vec.tensor_tensor(hid, bank(1)[:, 0:4 * SLOTS].rearrange("p (m t) -> p m t", m=4), sg, ALU.mult
                                  ).then_inc(f.hid_done, 1)

            def copy_y(f, n, before=0):
                dve.wait_ge(f.y_done, n + (before + 1))
                vec.tensor_copy(ysb[:, 512:1024], bank(3)[0:SLOTS, :]).then_inc(f.y_dve, 1)

            def stage(dst, src, blk):
                return vec.tensor_scalar(dst, src[:, bass.ds(blk, 1)], 0.0, None, ALU.add)

            def expert(b, turn_next=True, fetch_next=True):
                hidden(first, b)
                if turn_next:
                    copy_xT(first, b + 1)
                if not isinstance(b, int) or b > 0:
                    dve.wait_ge(first.sent, 16 * b)
                stage(si_s, sidx, b)
                if fetch_next:
                    stage(gi_s, gidx, b + 2)
                if not isinstance(b, int) or b > 0:
                    dve.wait_ge(first.held, b)
                copy_y(first, b)

            copy_xT(first, 0)
            stage(gi_s, gidx, 1).then_inc(first.staged, 1)
            expert(0)
            with dve.Fori(1, NE - 2, 1) as b:
                expert(b)
            expert(NE - 2, True, False)
            expert(NE - 1, False, False)
            dve.wait_ge(first.sent, 16 * NE)
            dve.wait_ge(first.held, NE)
            more = dve.value_load(oexp[0:1, OVER:OVER + 1], min_val=0, max_val=OVER)
            with dve.If(more > 0):
                with dve.Fori(0, more, 1) as o:
                    stage(si_s, sidx, o + NE)
                    stage(gi_s, gidx, o + NE).then_inc(further.staged, 1)
                    copy_xT(further, o)
                    hidden(further, o)
                    dve.wait_ge(further.held, 2 * o + 1)
                    copy_y(further, o, NE)
                    dve.wait_ge(further.sent, 16 * o + 16)
                    dve.wait_ge(further.held, 2 * o + 2)

            def add_experts(t):
                w = rows(t)
                dve.wait_ge(y_in[t % NY], 32 * (t // NY + 1))
                x = xres[0:w, t, :]
                for c in range(2):
                    ins = vec.scalar_tensor_tensor(out=x, in0=yt[t % NY][0:w, c, :], scalar=gates[0:w, c, t:t + 1], in1=x,
                                                   op0=ALU.mult, op1=ALU.add)
                    if c == 0:
                        step(ins)
                ins.then_inc(fin_res, 1)

            def finish(t):
                w = rows(t)
                c = t % 2
                dve.wait_ge(fin_std, t + 1)
                step(vec.reciprocal(rst_f[0:w, c:c + 1], std_f[0:w, c:c + 1]))
                if t >= NO:
                    dve.wait_ge(out_sent[t % NO], 16 * (t // NO))
                vec.scalar_tensor_tensor(out=ot[t % NO][0:w, :], in0=xres[0:w, t, :], scalar=rst_f[0:w, c:c + 1],
                                         in1=gfin[0:w, :], op0=ALU.mult, op1=ALU.mult).then_inc(fin_out, 1)

            dve.wait_ge(gfin_in, 16)
            add_experts(0)
            for t in range(NT):
                if t + 1 < NT:
                    add_experts(t + 1)
                finish(t)

        @block.gpsimd
        def _(pool):
            gp = nc.gpsimd

            def hold(f, cell):
                gp.tensor_tensor(stat[0:1, cell:cell + 1], ones[0:1, 0:1], ones[0:1, 0:1], ALU.mult
                                 ).then_inc(f.held, 1)

            def fetch(f):
                gp.indirect_dma_start(xg, None, h2_d[:, :], bass.IndirectOffsetOnAxis(ap=gi_s, axis=0)
                                      ).then_inc(f.rows_in, 16)

            def send(f):
                gp.indirect_dma_start(y_d[:, :], bass.IndirectOffsetOnAxis(ap=si_s, axis=0), ysb, None,
                                      bounds_check=2 * NTOK - 1, oob_is_err=False).then_inc(f.sent, 16)

            for n in range(2 * NS):
                b, src = n % NS, a["cache_k"] if n < NS else a["cache_v"]
                if 2 <= n < NS + 2:
                    pool.wait_ge(scored, n - 1)
                elif n >= NS + 2:
                    pool.wait_ge(spv_used, n - NS - 1)
                for r, d in enumerate(DIL):
                    keys = src[b, WBUF - d * WIN:WBUF, :].rearrange("(j d) c -> j d c", d=d)[:, 0, :]
                    gp.dma_start(kv[:, n % 2, r * DA:(r + 1) * DA], keys).then_inc(kv_in[n % 2], 16)

            pool.wait_ge(h2_out[0], 16 * 5)
            pool.wait_ge(h2_out[1], 16 * 4)
            pool.wait_ge(routed, 1)
            fetch(first)
            pool.wait_ge(first.xT_ready, 2)
            pool.wait_ge(first.staged, 1)
            fetch(first)

            def expert(b, s, fetch_next=True):
                pool.wait_ge(first.y_act, b + 1)
                pool.wait_ge(first.y_dve, b + 1)
                hold(first, 93 + s)
                send(first)
                if fetch_next:
                    fetch(first)

            with pool.Fori(0, NE // 2 - 1, 1) as j:
                expert(2 * j, 0)
                expert(2 * j + 1, 1)
            expert(NE - 2, 0, False)
            expert(NE - 1, 1, False)
            pool.wait_ge(first.sent, 16 * NE)
            more = pool.value_load(oexp[0:1, OVER:OVER + 1], min_val=0, max_val=OVER)
            with pool.If(more > 0):
                with pool.Fori(0, more, 1) as o:
                    pool.wait_ge(further.staged, o + 1)
                    hold(further, 93)
                    fetch(further)
                    pool.wait_ge(further.y_act, o + 1)
                    pool.wait_ge(further.y_dve, o + 1)
                    hold(further, 94)
                    send(further)
                    pool.wait_ge(further.sent, 16 * o + 16)
            gp.memset(stat[0:1, 95:96], 0.0).then_inc(all_sent, 1)


_OUT = {
    "y_prompt": (SEQ, D), "y_sample": (NS, D), "k_prompt": (SEQ, DA), "v_prompt": (SEQ, DA),
    "conv_u": (P, MA, NS + 2), "k_sample": (NS, DA), "v_sample": (NS, DA), "conv_sample_old": (NS, DA),
}


def kernel(**inputs):
    import concourse.bacc as _bacc
    from concourse.bass_utils import run_bass_kernel_spmd as _run

    x = {n: np.ascontiguousarray(v) for n, v in inputs.items()}
    const, amask, smask = constants()
    gain_out = np.concatenate([x["norm_out_attn"][0], x["norm_out_conv"][0]]).reshape(KD, P).T
    arrays = {
        "x_prompt": x["x_prompt"][0], "x_sample": x["x_sample"][:, 0], "w_in": x["w_in"][0],
        "cache_k": x["cache_k"][0].reshape(NS, WBUF, DA), "cache_v": x["cache_v"][0].reshape(NS, WBUF, DA),
        "state_conv": x["state_conv"][0],
        "conv_state": x["state_conv"][0].reshape(NS, 2, MA, P).transpose(3, 2, 1, 0),
        "conv_w": x["conv_w"][0].reshape(CONV, MA, P).transpose(2, 1, 0),
        "gain_out": gain_out, "norm_mix": x["norm_mix"][0], "norm_ffn": x["norm_ffn"][0],
        "norm_final": x["norm_final"], "w_out": x["w_out"][0],
        "w_router": np.concatenate([x["w_router_group"][0], x["w_router_expert"][0]], axis=1)
        .reshape(KD, P, NGRP + NE).transpose(1, 0, 2),
        "b_router": np.concatenate([x["b_router_group"][0], x["b_router_expert"][0]]),
        "w_gate": x["w_gate"][0], "w_up": x["w_up"][0], "w_down": x["w_down"][0],
        "const": const, "amask": amask, "smask": smask,
    }
    nc = _bacc.Bacc("TRN2", target_bir_lowering=False, num_devices=1)
    feed, aps = {}, {}
    for name, arr in arrays.items():
        arr = np.ascontiguousarray(arr)
        feed[f"in_{name}"] = arr
        aps[name] = nc.dram_tensor(f"in_{name}", arr.shape, mybir.dt.from_np(arr.dtype), kind="ExternalInput").ap()
    for name in ("w_gate", "w_up", "w_down"):
        aps[name + "_flat"] = aps[name].rearrange("e d n -> (e d) n")
    for name, shape in _OUT.items():
        aps[name] = nc.dram_tensor(f"out_{name}", shape, F32, kind="ExternalOutput").ap()
    program(nc, aps)
    r = _run(nc, [feed], core_ids=[0]).results[0]
    got = {n: r[f"out_{n}"] for n in _OUT}
    u = got["conv_u"].transpose(2, 1, 0).reshape(NS + 2, DA)
    conv_sample = np.stack([got["conv_sample_old"], u[2:]], axis=1)
    return (got["y_prompt"][None], got["y_sample"][:, None], got["k_prompt"].reshape(1, 1, SEQ, H, DH),
            got["v_prompt"].reshape(1, 1, SEQ, H, DH), u[None, None, 0:2],
            got["k_sample"].reshape(1, NS, 1, H, DH), got["v_sample"].reshape(1, NS, 1, H, DH), conv_sample[None])
```

```python
from contextlib import ExitStack

import numpy as np

import concourse.bass as bass
from concourse import mybir

F32 = mybir.dt.float32
F32R = mybir.dt.float32r
I32 = mybir.dt.int32
ALU = mybir.AluOpType
ACT = mybir.ActivationFunctionType
X = mybir.AxisListType.X

P = 128
D = 1024
KD = D // P
SEQ = 1024
NS = 8
NTOK = SEQ + NS
NT = SEQ // P + 1
NQ = SEQ // P
H = 8
DH = 64
DA = H * DH
MA = DA // P
DIL = (1, 4, 16)
WIN = 128
WBUF = 2048
CONV = 3
NE = 32
NGRP = 4
EPG = NE // NGRP
DE = 512
SLOTS = 96
MORE = -(-NTOK // SLOTS) - 1
OVER = 2 * NTOK // SLOTS + 1
NBLK = NE + OVER
TC = NTOK // 3
EPS = 1e-6
NEG = -1e30
DROP = 8192.0


def rows(t):
    return P if t < NQ else NS


def constants():
    p = np.arange(P)[:, None]
    c = np.arange(P)[None, :]
    tok = 128 * np.arange(NT)[None, :] + p + 1
    const = np.concatenate([
        (p == c), np.broadcast_to(c, (P, P)), (p < c), np.ones((P, P)),
        tok, tok + NTOK, np.full((P, 1), EPS),
    ], axis=1).astype(np.float32)
    dist = p + (SEQ - P) - np.arange(SEQ)[None, :]
    count = sum(((dist >= 0) & (dist % d == 0) & (dist <= d * WIN)).astype(np.int32) for d in DIL)
    amask = np.where(count > 0, np.log(np.maximum(count, 1)), NEG).astype(np.float32)
    smask = np.full((NS, NS, H), NEG, np.float32)
    smask[np.arange(NS), np.arange(NS)] = np.log(len(DIL))
    return const, amask, smask.reshape(NS, NS * H)


def program(nc, a):
    with ExitStack() as ctx:
        def sb(name, shape, dt=F32):
            return ctx.enter_context(nc.sbuf_tensor(name, shape, dt))

        def sem(name):
            return ctx.enter_context(nc.semaphore(name))

        base = -(-nc.sbuf_base // 32) * 32

        def at(name, offset, shape, dt=F32):
            return nc.alloc_sbuf_tensor_at(name, [P] + list(shape), dt, offset=base + offset)[:]

        class Pack:

            def __init__(self, start, end):
                self.next, self.end = start, end

            def __call__(self, name, shape, dt=F32):
                t = at(name, self.next, shape, dt)
                self.next += -(-4 * int(np.prod(shape)) // 32) * 32
                assert self.next <= self.end, name
                return t

        XRES, WEI, TMP, END = 10240, 47104, 194560, 212832
        WSLOT = 49152
        QT, CT, MISC, WOUT = 145408, 161920, 178432, 79872

        keep = Pack(0, XRES)
        cst = keep("cst", [4 * P + 2 * NT + 1])
        gout = keep("gout", [KD])
        cw = keep("cw", [MA, CONV])
        cstate = keep("cstate", [MA, 2, NS])
        uout = keep("uout", [MA, NS + 2])
        srow = keep("srow", [3, DA])[0:NS]
        stat = keep("stat", [96])
        gates = keep("gates", [2, NT])
        gidx = keep("gidx", [NBLK], I32)[0:SLOTS]
        sidx = keep("sidx", [NBLK], I32)[0:SLOTS]
        oexp = keep("oexp", [OVER + 1], I32)
        gi_s = keep("gi_s", [1], I32)[0:SLOTS]
        si_s = keep("si_s", [1], I32)[0:SLOTS]

        ident, ramp = cst[:, 0:P], cst[:, P:2 * P]
        before, ones = cst[:, 2 * P:3 * P], cst[:, 3 * P:4 * P]
        tokv = cst[:, 4 * P:4 * P + NT]
        destv = cst[:, 4 * P + NT:4 * P + 2 * NT]
        eps = cst[:, 4 * P + 2 * NT:4 * P + 2 * NT + 1]
        ssq_x, std_x, rst_x = stat[:, 0:9], stat[:, 9:18], stat[:, 18:27]
        mx_n, neg_n = stat[:, 27:30], stat[:, 30:33]
        lsum, rl = stat[:, 33:65], stat[:, 80:82]
        smx, sneg, sl, srl = stat[0:64, 65:66], stat[0:64, 66:67], stat[0:64, 67:68], stat[0:64, 68:69]
        std_ac, rst_ac = stat[:, 70:72], stat[:, 72:74]
        ssq_f, std_f, rst_f = stat[:, 74:76], stat[:, 76:78], stat[:, 78:80]

        NXT, NXN = 4, 3
        pack = Pack(XRES, WEI)
        xt = [pack(f"x_tile{s}", [D]) for s in range(NXT)]
        xn = [pack(f"xn{s}", [D]) for s in range(NXN)]
        gmix = pack("gmix", [D])
        junk = pack("junk", [D])
        pack = Pack(XRES, WEI)
        kT = pack("kT", [MA, NTOK])
        v = pack("v", [NQ, DA])
        pack = Pack(WEI, QT)
        h_hi = pack("h_hi", [KD, NTOK], F32R)
        h_lo = pack("h_lo", [KD, NTOK], F32R)
        w_raw = [pack(f"w_raw{s}", [KD, P]) for s in range(3)]
        w_hi = [pack(f"w_hi{s}", [KD, P], F32R) for s in range(2)]
        w_lo = [pack(f"w_lo{s}", [KD, P], F32R) for s in range(2)]
        own = pack("own", [DA])[0:NS]
        own_sum = pack("own_sum", [H])[0:NS]
        qT = at("qT", QT, [MA, NTOK])
        cT = at("cT", CT, [MA, NTOK])
        kn = at("kn", CT, [NQ, DA])
        pack = Pack(MISC, END)
        u = pack("u", [NTOK + 2])
        cc_at = pack.next
        cc = pack("cc", [NTOK])
        z = pack("z", [NTOK])
        vT = [pack("vT0", [NTOK]), at("vT1", cc_at, [NTOK])]
        kv = pack("kv", [2, len(DIL) * DA])
        sscore = pack("sscore", [len(DIL) + 1, NS * H])
        sprob = pack("sprob", [3 * P + NS])[0:64]
        sprobT = pack("sprobT", [len(DIL) + 1, NS * H])
        ssm = pack("ssm", [NS * H])[0:NS]
        pack = Pack(WEI, WOUT)
        sm = [pack(f"scores{s}", [D]) for s in range(3)]
        pt = [pack(f"probsT{s}", [D]) for s in range(2)]
        amask = pack("amask", [SEQ])
        an = [pack(f"attn{s}", [DA]) for s in range(4)]
        wo_raw = [at(f"wo_raw{s}", MISC + 4096 * s, [D]) for s in range(4)]
        wo_hi = at("wo_hi", WOUT, [KD, D], F32R)
        wo_lo = at("wo_lo", WOUT + 32768, [KD, D], F32R)
        xres = at("xres", XRES, [NT, D])
        pack = Pack(WEI + 16384, WOUT)
        a_hi = [pack(f"a_hi{s}", [2 * MA, P], F32R) for s in range(2)]
        a_lo = [pack(f"a_lo{s}", [2 * MA, P], F32R) for s in range(2)]
        pack = Pack(MISC, END)
        sq = [pack(f"sq{s}", [2 * MA, P]) for s in range(2)]
        sqs = [pack(f"sq_sum{s}", [2, P]) for s in range(2)]
        h2 = [pack(f"h2_{s}", [D]) for s in range(2)]
        h2T = [pack(f"h2T{s}", [KD, P]) for s in range(2)]
        gffn = pack("gffn", [D])
        wr = pack("wr", [KD, NGRP + NE])
        rbias = pack("rbias", [NGRP + NE])
        lg = pack("lg", [NT, NGRP + NE])
        rt = Pack(MISC, TMP)
        r_gm, r_gi, r_sg, r_pg, r_v1, r_v2, r_i1, r_i2, r_vd, r_den, r_t9 = (
            rt(f"r{i}", [NT]) for i in range(11))
        r_e, r_r, r_so, r_q, r_j, r_blk, r_is = (rt(f"rc{i}", [2, NT]) for i in range(7))
        r_ob, r_inc, r_exc = (rt(f"re{i}", [NE]) for i in range(3))
        r_d, r_eq, r_goh = (rt(f"rg{i}", [NT, NGRP]) for i in range(3))
        r_le, r_eq8, r_oh, r_le2 = (rt(f"rl{i}", [NT, EPG]) for i in range(4))
        r_big, r_hot1, r_hot2, r_hot, r_sum = (rt(f"rh{i}", [NT, NE]) for i in range(5))
        r_rank = rt("r_rank", [NT + 1, NE])
        r_mul = rt("r_mul", [MORE])
        flat = rt("r_comparisons", [OVER * NE])
        r_cmp = flat.rearrange("p (o e) -> p o e", o=OVER)
        r_gt = flat[:, 0:NE * MORE].rearrange("p (e m) -> p e m", e=NE)
        r_ge = flat[:, 0:2 * NT * MORE].rearrange("p (n m) -> p n m", n=2 * NT)
        r_tab = rt("r_tab", [2, NBLK])
        r_tab2 = rt("r_tab2", [NBLK])
        hot_slot = [rt(f"hot_slot{s}", [SLOTS]) for s in range(2)]
        hot_blk = [rt(f"hot_blk{s}", [NBLK]) for s in range(2)]
        wg = [at(f"w_gate{s}", WEI + WSLOT * s, [KD, DE]) for s in range(3)]
        wu = [at(f"w_up{s}", WEI + WSLOT * s + 16384, [KD, DE]) for s in range(3)]
        wd = [at(f"w_down{s}", WEI + WSLOT * s + 32768, [DE // P, D]) for s in range(2)]
        wd_lo = [at(f"w_down_lo{s}", WEI + WSLOT * s + 32768, [DE // P, D], F32R) for s in range(2)]
        wd_hi = at("w_down_hi", WEI + WSLOT * 2 + 32768, [DE // P, D], F32R)
        pack = Pack(TMP, END)
        xg = pack("x_rows", [D])[0:SLOTS]
        xT = pack("x_turned", [KD, SLOTS])
        sg = pack("silu_gate", [4, SLOTS])
        hid = pack("hid", [4, SLOTS])
        hid_hi = pack("hid_hi", [4, SLOTS], F32R)
        hid_lo = pack("hid_lo", [4, SLOTS], F32R)
        ysb = pack("y_rows", [D])[0:SLOTS]
        NY, NO = 4, 3
        pack = Pack(WEI, QT)
        yt = [pack(f"y_tile{s}", [2, D]) for s in range(NY)]
        ot = [pack(f"out_tile{s}", [D]) for s in range(NO)]
        gfin = pack("gfin", [D])
        fjunk = pack("fjunk", [D])

        psum = ctx.enter_context(nc.psum_tensor("psum", [P, 8 * 512], F32))

        def bank(b, n=1):
            return psum[:, 512 * b:512 * (b + n)]

        h2_d = nc.dram_tensor("h2_rows", [NTOK, D], F32, kind="Internal").ap()
        y_d = nc.dram_tensor("y_rows", [2 * NTOK, D], F32, kind="Internal").ap()

        const_in = sem("const_in")
        small_in = sem("small_in")
        gmix_in = sem("gmix_in")
        x_in = [sem(f"x_in{t}") for t in range(NT)]
        win_in = [sem(f"win_in{s}") for s in range(3)]
        w_hi_ready = sem("w_hi_ready")
        w_ready = sem("w_ready")
        h_hi_ready = sem("h_hi_ready")
        kv_in = [sem(f"kv_in{s}") for s in range(2)]
        wo_in = [sem(f"wo_in{s}") for s in range(4)]
        xres_in = [sem(f"xres_in{t}") for t in range(NT)]
        mask_in = sem("mask_in")
        router_in = sem("router_in")
        act_step = sem("act_step")
        dve_step = sem("dve_step")
        std_ready = sem("std_ready")
        xn_ready = sem("xn_ready")
        group_done = sem("group_done")
        act_emptied = sem("act_emptied")
        dve_emptied = sem("dve_emptied")
        qb_ready = sem("qb_ready")
        scored = sem("scored")
        z_ready = sem("z_ready")
        kn_out = sem("kn_out")
        v_out = sem("v_out")
        u_ready = sem("u_ready")
        sT_ready = sem("sT_ready")
        smax_ready = sem("smax_ready")
        sexp_ready = sem("sexp_ready")
        sp_ready = sem("sp_ready")
        spT_ready = sem("spT_ready")
        spT_copied = sem("spT_copied")
        spv_used = sem("spv_used")
        spv_ready = sem("spv_ready")
        s_attn = sem("s_attn")
        s_ready = sem("s_ready")
        masked = sem("masked")
        exped = sem("exped")
        pT_ready = sem("pT_ready")
        pT_act = sem("pT_act")
        pT_dve = sem("pT_dve")
        pv_done = sem("pv_done")
        an_ready = sem("an_ready")
        aT_ready = sem("aT_ready")
        aT_copied = sem("aT_copied")
        wo_hi_ready = sem("wo_hi_ready")
        wo_ready = sem("wo_ready")
        a_hi_ready = sem("a_hi_ready")
        a_ready = sem("a_ready")
        sq_ready = sem("sq_ready")
        sq_summed = sem("sq_summed")
        ssq_ready = sem("ssq_ready")
        std_ac_ready = sem("std_ac_ready")
        o_ready = sem("o_ready")
        o_used = sem("o_used")
        std_f_ready = sem("std_f_ready")
        h2_ready = sem("h2_ready")
        h2_out = [sem(f"h2_out{s}") for s in range(2)]
        h2T_ready = sem("h2T_ready")
        h2T_copied = sem("h2T_copied")
        lg_ready = sem("lg_ready")
        lg_used = sem("lg_used")
        gd_ready = sem("gd_ready")
        gexp_ready = sem("gexp_ready")
        vd_ready = sem("vd_ready")
        vexp_ready = sem("vexp_ready")
        assigned = sem("assigned")
        ranked = sem("ranked")
        hot_ready = sem("hot_ready")
        hot_used = sem("hot_used")
        table_ready = sem("table_ready")
        routed = sem("routed")
        all_sent = sem("all_sent")

        class Flow:

            def __init__(self, tag, slots):
                self.gate_in = [sem(f"{tag}_gate_in{s}") for s in range(slots)]
                self.up_in = [sem(f"{tag}_up_in{s}") for s in range(slots)]
                self.down_in = [sem(f"{tag}_down_in{s}") for s in range(min(slots, 2))]
                self.down_hi = sem(f"{tag}_down_hi")
                self.down_split = sem(f"{tag}_down_split")
                self.rows_in = sem(f"{tag}_rows_in")
                self.sent = sem(f"{tag}_sent")
                self.xT_ready = sem(f"{tag}_xT_ready")
                self.xT_act = sem(f"{tag}_xT_act")
                self.xT_dve = sem(f"{tag}_xT_dve")
                self.gate_done = sem(f"{tag}_gate_done")
                self.up_done = sem(f"{tag}_up_done")
                self.silu_done = sem(f"{tag}_silu_done")
                self.pieces = sem(f"{tag}_pieces")
                self.hid_hi_done = sem(f"{tag}_hid_hi_done")
                self.hid_done = sem(f"{tag}_hid_done")
                self.y_done = sem(f"{tag}_y_done")
                self.y_act = sem(f"{tag}_y_act")
                self.y_dve = sem(f"{tag}_y_dve")
                self.staged = sem(f"{tag}_staged")
                self.held = sem(f"{tag}_held")

        first, further = Flow("first", 3), Flow("further", 1)
        further.y_done = first.y_done
        y_in = [sem(f"y_in{s}") for s in range(NY)]
        gfin_in = sem("gfin_in")
        fin_res = sem("fin_res")
        fin_std = sem("fin_std")
        fin_out = sem("fin_out")
        out_sent = [sem(f"out_sent{s}") for s in range(NO)]
        out_misc = sem("out_misc")

        tiles = [("q", m) for m in range(MA)] + [("k", m) for m in range(MA)] + [("v", m) for m in range(MA)]
        for m in range(MA):
            tiles += [("c", m), ("u", m), ("b", m)]
        column = {"q": 0, "k": DA, "v": 2 * DA, "b": 3 * DA, "c": 3 * DA + 512, "u": 3 * DA + 1024}
        groups = []
        for n in range(3):
            groups += [("x", t, h) for t in range(3 * n, 3 * n + 3) for h in range(2)]
            groups += [("q", 0, n)]
        for kind, m in tiles[1:]:
            for n in range(3):
                groups += [(kind, m, n)]
                if n == 0 and kind == "v" and m >= 1:
                    groups += [("vn", m - 1, j) for j in range(3)]
            if (kind, m) == ("k", 0):
                groups += [("rows", 0, 0)]
            if (kind, m) == ("v", 0):
                groups += [("rows", 1, 0)]
            if (kind, m) == ("v", MA - 1):
                groups += [("kn", i, 0) for i in range(NQ)] + [("vn", MA - 1, j) for j in range(3)]
        number = {g: i for i, g in enumerate(groups)}
        taker = []
        taken = {"act": 0, "dve": 0}
        for i, g in enumerate(groups):
            e = "dve" if g[0] in "ubx" or (g[0] == "q" and i % 2) else "act"
            taken[e] += 1
            taker.append((e, taken[e]))

        def wait_emptied(eng, g):
            e, n = taker[g]
            eng.wait_ge(act_emptied if e == "act" else dve_emptied, n)

        def group_psum(g):
            return bank(g % 4)

        SCORE_AT = 5
        TURN_AT = SCORE_AT + NS
        VALUES_AT = len(tiles) - 6

        def values_after(t):
            n = t - VALUES_AT
            return [] if n < 0 else [0, 1] if n == 0 else [NS - 2, NS - 1] if n == 5 else [n + 1]

        steps_of = [(b, h) for b in range(NQ) for h in range(H)]
        NSTEP = len(steps_of)
        PAIR = 2 * H

        def sum_column(n):
            i, h = steps_of[n]
            return H * (2 * (n // PAIR % 2) + (i % 2)) + h

        def turned(k):
            return k, 2 * (k // 2 % 2) + k % 2

        turn_step = {H * (k + 1) + 5: k for k in range(NQ)}
        split_step = {36 + 3 * k: k for k in range(KD)}

        block = ctx.enter_context(nc.Block())

        @block.sync
        def _(sp):
            def load_win(t):
                kind, m = tiles[t]
                c = column[kind] + m * P
                if t >= 3:
                    sp.wait_ge(w_ready, t - 2)
                sp.dma_start(w_raw[t % 3], a["w_in"][:, c:c + P].rearrange("(k p) n -> p k n", p=P)
                             ).then_inc(win_in[t % 3], 16)

            def load_x(t):
                if t >= NXT:
                    sp.wait_ge(xn_ready, t - NXT + 1)
                src = a["x_prompt"][t * P:(t + 1) * P, :] if t < NQ else a["x_sample"]
                sp.dma_start(xt[t % NXT][0:rows(t), :], src).then_inc(x_in[t], 16)

            load_x(0)
            sp.dma_start(cst[:], a["const"]).then_inc(const_in, 16)
            sp.dma_start(gmix, a["norm_mix"].partition_broadcast(P)).then_inc(gmix_in, 16)
            load_win(0)
            load_x(1)
            load_x(2)
            load_win(1)
            for t in range(3, NT):
                load_x(t)
            load_win(2)
            for src, dst in (("gain_out", gout), ("conv_w", cw), ("conv_state", cstate), ("smask", ssm)):
                sp.dma_start(dst, a[src]).then_inc(small_in, 16)
            sp.dma_start(a["conv_sample_old"], a["state_conv"][:, 1, :]).then_inc(out_misc, 16)
            for t in range(3, len(tiles)):
                load_win(t)
                if tiles[t] == ("b", 1):
                    for m in range(MA):
                        for j in range(3):
                            wait_emptied(sp, number["vn", m, j])
                    for i in range(2):
                        wait_emptied(sp, number["rows", i, 0])
                    for i in range(NQ):
                        wait_emptied(sp, number["kn", i, 0])
                    sp.dma_start(a["k_prompt"].rearrange("(t p) c -> p t c", p=P), kn).then_inc(kn_out, 16)
                    sp.dma_start(a["v_prompt"].rearrange("(t p) c -> p t c", p=P), v).then_inc(v_out, 16)
                    sp.dma_start(a["k_sample"], srow[:, 1, :]).then_inc(out_misc, 16)
                    sp.dma_start(a["v_sample"], srow[:, 2, :]).then_inc(out_misc, 16)
            sp.wait_ge(group_done, len(groups))
            sp.dma_start(amask, a["amask"]).then_inc(mask_in, 16)
            sp.wait_ge(u_ready, MA)
            sp.dma_start(a["conv_u"], uout[:]).then_inc(out_misc, 16)
            sp.wait_ge(s_attn, 1)
            for emptied, last in ((act_emptied, taken["act"]), (dve_emptied, taken["dve"])):
                sp.wait_ge(emptied, last)
            for k in range(KD):
                if k >= 4:
                    sp.wait_ge(wo_ready, k - 3)
                sp.dma_start(wo_raw[k % 4], a["w_out"][k * P:(k + 1) * P, :]).then_inc(wo_in[k % 4], 16)
            sp.dma_start(gffn, a["norm_ffn"].partition_broadcast(P)).then_inc(router_in, 16)
            sp.dma_start(wr, a["w_router"]).then_inc(router_in, 16)
            sp.dma_start(rbias, a["b_router"].partition_broadcast(P)).then_inc(router_in, 16)
            sp.wait_ge(v_out, 16)
            sp.wait_ge(pv_done, NSTEP)
            for t in range(NT):
                src = a["x_prompt"][t * P:(t + 1) * P, :] if t < NQ else a["x_sample"]
                sp.dma_start(xres[0:rows(t), t, :], src).then_inc(xres_in[t], 16)
            sp.wait_ge(aT_ready, NQ)

            def load_gate(f, s, e):
                sp.dma_start(wg[s], a["w_gate"][e].rearrange("(k p) n -> p k n", p=P)).then_inc(f.gate_in[s], 16)

            def load_up(f, s, e):
                sp.dma_start(wu[s], a["w_up"][e].rearrange("(k p) n -> p k n", p=P)).then_inc(f.up_in[s], 16)

            def load_down(f, s, e):
                sp.dma_start(wd[s], a["w_down"][e].rearrange("(k p) n -> p k n", p=P)).then_inc(f.down_in[s], 16)

            load_gate(first, 0, 0)

            def store_h2(t):
                sp.wait_ge(h2_ready, t + 1)
                sp.dma_start(h2_d[P * t:P * t + rows(t), :], h2[t % 2][0:rows(t), :]).then_inc(h2_out[t % 2], 16)

            for t in range(NT):
                store_h2(t)
            sp.wait_ge(o_ready, 4 * NT)
            load_up(first, 0, 0)
            load_down(first, 0, 0)
            for load in (load_gate, load_up, load_down):
                load(first, 1, 1)
            load_gate(first, 2, 2)
            sp.wait_ge(aT_copied, NQ)
            load_up(first, 2, 2)

            def refill_down(e, s):
                sp.wait_ge(first.y_done, e - 1)
                sp.dma_start(wd[s], a["w_down_flat"][bass.ds(e * DE, DE), :].rearrange("(k p) n -> p k n", p=P)
                             ).then_inc(first.down_in[s], 16)

            def refill(e, s, sd):
                sp.wait_ge(first.gate_done, e - 2)
                sp.dma_start(wg[s], a["w_gate_flat"][bass.ds(e * D, D), :].rearrange("(k p) n -> p k n", p=P)
                             ).then_inc(first.gate_in[s], 16)
                sp.wait_ge(first.up_done, e - 2)
                sp.dma_start(wu[s], a["w_up_flat"][bass.ds(e * D, D), :].rearrange("(k p) n -> p k n", p=P)
                             ).then_inc(first.up_in[s], 16)
                refill_down(e - 1, sd)

            with sp.Fori(0, (NE - 3) // 6, 1) as j:
                for k in range(6):
                    refill(sp.snap(6 * j + (3 + k)), k % 3, k % 2)
            for e in range(3 + (NE - 3) // 6 * 6, NE):
                refill(e, e % 3, (e - 1) % 2)
            refill_down(NE - 1, (NE - 1) % 2)
            sp.wait_ge(first.y_done, NE)
            more = sp.value_load(oexp[0:1, OVER:OVER + 1], min_val=0, max_val=OVER)
            with sp.If(more > 0):
                with sp.Fori(0, more, 1) as o:
                    e = sp.value_load(oexp[0:1, bass.ds(o, 1)], min_val=0, max_val=NE - 1)
                    sp.wait_ge(first.y_done, o + NE)
                    sp.dma_start(wg[0], a["w_gate_flat"][bass.ds(e * D, D), :].rearrange("(k p) n -> p k n", p=P)
                                 ).then_inc(further.gate_in[0], 16)
                    sp.dma_start(wu[0], a["w_up_flat"][bass.ds(e * D, D), :].rearrange("(k p) n -> p k n", p=P)
                                 ).then_inc(further.up_in[0], 16)
                    sp.dma_start(wd[0], a["w_down_flat"][bass.ds(e * DE, DE), :].rearrange("(k p) n -> p k n", p=P)
                                 ).then_inc(further.down_in[0], 16)
            sp.wait_ge(all_sent, 1)
            sp.dma_start(gfin, a["norm_final"].partition_broadcast(P)).then_inc(gfin_in, 16)

            def load_y(t):
                if t >= NY:
                    sp.wait_ge(fin_res, t - NY + 1)
                n = rows(t)
                for c in range(2):
                    row = c * NTOK + P * t
                    sp.dma_start(yt[t % NY][0:n, c, :], y_d[row:row + n, :]).then_inc(y_in[t % NY], 16)

            for t in range(NY):
                load_y(t)
            for t in range(NT):
                if t + NY < NT:
                    load_y(t + NY)
                sp.wait_ge(fin_out, t + 1)
                dst = a["y_prompt"][P * t:P * (t + 1), :] if t < NQ else a["y_sample"]
                sp.dma_start(dst, ot[t % NO][0:rows(t), :]).then_inc(out_sent[t % NO], 16)
            for o in out_sent:
                sp.wait_ge(o, 16 * (NT // NO))
            sp.wait_ge(out_misc, 16 * 4)
            sp.wait_ge(kn_out, 16)

        @block.tensor
        def _(pe):
            mm = nc.tensor.matmul
            pe.wait_ge(const_in, 16)

            def proj(g):
                kind, i, n = groups[g]
                if g >= 4:
                    wait_emptied(pe, g - 4)
                ps = group_psum(g)
                if kind == "x":
                    w = rows(i)
                    pe.wait_ge(xn_ready, i + 1)
                    for c in range(4):
                        k = 4 * n + c
                        ins = nc.tensor.transpose(ps[:, c * w:(c + 1) * w], xn[i % NXN][0:w, k * P:(k + 1) * P],
                                                  ident[0:w, 0:w])
                elif kind == "rows":
                    for m in range(MA):
                        wait_emptied(pe, number["q" if i == 0 else "k", m, 2])
                    for m in range(MA):
                        ins = nc.tensor.transpose(ps[0:NS, m * P:(m + 1) * P],
                                                  (qT if i == 0 else kT)[:, m, SEQ:NTOK], ident)
                elif kind == "vn":
                    for c in range(3):
                        wait_emptied(pe, number["v", i, c])
                    for c in range(4 if n < 2 else 1):
                        t = 4 * n + c
                        w = rows(t)
                        ins = nc.tensor.transpose(ps[0:w, c * P:(c + 1) * P], vT[i % 2][:, t * P:t * P + w], ident)
                elif kind == "kn":
                    for m in range(MA):
                        ins = nc.tensor.transpose(ps[:, m * P:(m + 1) * P], kT[:, m, i * P:(i + 1) * P], ident)
                else:
                    t = tiles.index((kind, i))
                    if n == 0:
                        pe.wait_ge(w_ready, t + 1)
                    if t == 0:
                        for x in range(3 * n, 3 * n + 3):
                            for h in range(2):
                                wait_emptied(pe, number["x", x, h])
                    cols = slice(n * TC, (n + 1) * TC)
                    wh, wl = w_hi[t % 2], w_lo[t % 2]
                    for k in range(KD):
                        mm(ps[:, 0:TC], wh[:, k, :], h_hi[:, k, cols], start=(k == 0), stop=False)
                        mm(ps[:, 0:TC], wh[:, k, :], h_lo[:, k, cols], start=False, stop=False)
                        ins = mm(ps[:, 0:TC], wl[:, k, :], h_hi[:, k, cols], start=False, stop=(k == KD - 1))
                ins.then_inc(group_done, 1)

            def query_all_partitions(b):
                if b == 0:
                    wait_emptied(pe, number["rows", 0, 0])
                if b >= 2:
                    pe.wait_ge(scored, b - 1)
                mm(bank(4 + b % 2), ident[0:NS, b:b + 1].broadcast_to([NS, P]), srow[:, 0, :],
                   start=True, stop=True).then_inc(qb_ready, 1)

            def sample_scores_turned():
                pe.wait_ge(scored, NS + 1)
                ps = bank(6)[0:64, :]
                for r in range(3):
                    nc.tensor.transpose(ps[:, r * P:(r + 1) * P], sscore[:, r, :], ident)
                nc.tensor.transpose(ps[:, 3 * P:3 * P + NS], sscore[0:NS, 3, :], ident[0:NS, 0:NS]
                                    ).then_inc(sT_ready, 1)

            def sample_probs_turned():
                pe.wait_ge(sp_ready, 1)
                ps = bank(7)
                for r in range(3):
                    nc.tensor.transpose(ps[:, r * 64:(r + 1) * 64], sprob[:, r * P:(r + 1) * P], ident[0:64, 0:64])
                nc.tensor.transpose(ps[0:NS, 192:256], sprob[:, 3 * P:3 * P + NS], ident[0:64, 0:64]
                                    ).then_inc(spT_ready, 1)

            def sample_values(b):
                out = bank(4).rearrange("p (m c) -> p m c", m=8)
                if b == 0:
                    pe.wait_ge(spT_copied, 1)
                    for m in range(MA):
                        mm(out[:, m, :], srow[:, 2, m * P:(m + 1) * P], sprobT[0:NS, 3, :],
                           start=(m == 0), stop=False, skip_group_check=True)
                n = NS + b
                pe.wait_ge(kv_in[n % 2], 48 * (n // 2 + 1))
                for r in range(3):
                    for m in range(MA):
                        ins = mm(out[:, m, b * H:(b + 1) * H], kv[:, n % 2, r * DA + m * P:r * DA + (m + 1) * P],
                                 sprobT[:, r, b * H:(b + 1) * H], start=False, stop=(r == 2),
                                 skip_group_check=True)
                if b < NS - 1:
                    ins.then_inc(spv_used, 1)
                else:
                    ins.then_inc(spv_ready, 1)

            for g, (kind, i, n) in enumerate(groups):
                proj(g)
                if n < 2 or (kind, i) not in tiles:
                    continue
                t = tiles.index((kind, i))
                if SCORE_AT <= t < SCORE_AT + NS:
                    query_all_partitions(t - SCORE_AT)
                if t == TURN_AT:
                    sample_scores_turned()
                if t == TURN_AT + 4:
                    sample_probs_turned()
                for b in values_after(t):
                    sample_values(b)

            def scores(n):
                i, h = steps_of[n]
                m, lo = h // 2, DH * (h % 2)
                if n >= 2:
                    pe.wait_ge(masked, n - 1)
                ps = bank(2 * (n % 2), 2)
                width = (i + 1) * P
                for at in range(0, width, 512):
                    w = min(512, width - at)
                    ins = mm(ps[:, at:at + w], qT[lo:lo + DH, m, i * P:(i + 1) * P], kT[lo:lo + DH, m, at:at + w],
                             start=True, stop=True)
                ins.then_inc(s_ready, 1)

            def pT_wait(n):
                if n % 3 == 0:
                    pe.wait_ge(pT_dve, n // 3 + 1)
                else:
                    pe.wait_ge(pT_act, n - n // 3)

            def turn_probs(n):
                i = steps_of[n][0]
                pe.wait_ge(exped, n + 1)
                if n >= 1:
                    pT_wait(n - 1)
                ps = bank(4, 2)
                for j in range(i + 1):
                    ins = nc.tensor.transpose(ps[:, j * P:(j + 1) * P], sm[n % 3][:, j * P:(j + 1) * P], ident)
                ins.then_inc(pT_ready, 1)

            def weigh_values(n):
                i, h = steps_of[n]
                pT_wait(n)
                if n >= 2:
                    pe.wait_ge(an_ready, n - 1)
                if n + 2 in turn_step:
                    pe.wait_ge(aT_copied, turn_step[n + 2] + 1)
                pair = slice(h // 2 * P, (h // 2 + 1) * P)
                for j in range(i + 1):
                    ins = mm(bank(6 + n % 2)[:, 0:P], pt[n % 2][:, j * P:(j + 1) * P], v[:, j, pair],
                             start=(j == 0), stop=(j == i))
                ins.then_inc(pv_done, 1)

            def turn_attention(n, k):
                a_slot = turned(k)[1]
                pe.wait_ge(an_ready, min(n - 3, NSTEP))
                if k and n - 4 >= NSTEP:
                    pe.wait_ge(aT_copied, k)
                for m in range(MA):
                    ins = nc.tensor.transpose(bank(7)[:, m * P:(m + 1) * P], an[a_slot][:, m * P:(m + 1) * P], ident)
                ins.then_inc(aT_ready, 1)

            for g in range(len(groups) - 4, len(groups)):
                wait_emptied(pe, g)
            pe.wait_ge(s_attn, 1)
            for n in range(NSTEP + 8):
                if n < NSTEP:
                    scores(n)
                if 3 <= n < NSTEP + 3:
                    weigh_values(n - 3)
                if 2 <= n < NSTEP + 2:
                    turn_probs(n - 2)
                if n in turn_step:
                    turn_attention(n, turn_step[n])

            def project(t):
                w = rows(t)
                if t == 0:
                    pe.wait_ge(wo_ready, KD)
                pe.wait_ge(sq_summed, t + 1)
                if t:
                    pe.wait_ge(std_ac_ready, t)
                for c in range(2):
                    ins = mm(bank(6)[0:w, 2 * t + c:2 * t + c + 1], sqs[t % 2][:, c, 0:w], ones[:, 0:1],
                             start=True, stop=True)
                ins.then_inc(ssq_ready, 1)
                pe.wait_ge(a_ready, t + 1)
                for half in range(2):
                    for c in range(2):
                        g = 4 * t + 2 * half + c
                        if g >= 4:
                            pe.wait_ge(o_used, g - 3)
                        out = bank(2 * half + c)[0:w, :]
                        cols = slice(half * 512, (half + 1) * 512)
                        for m in range(c * MA, (c + 1) * MA):
                            first_m, last_m = m == c * MA, m == (c + 1) * MA - 1
                            hi, lo = a_hi[t % 2][:, m, :], a_lo[t % 2][:, m, :]
                            if w < P:
                                out = bank(2 * half + c)
                            mm(out, hi, wo_hi[:, m, cols], start=first_m, stop=False)
                            mm(out, lo, wo_hi[:, m, cols], start=False, stop=False)
                            ins = mm(out, hi, wo_lo[:, m, cols], start=False, stop=last_m)
                        ins.then_inc(o_ready, 1)

            def route(t):
                w = rows(t)
                pe.wait_ge(h2_ready, t + 1)
                if t == 0:
                    pe.wait_ge(router_in, 48)
                for half in range(2):
                    if t >= 1:
                        pe.wait_ge(h2T_copied, 2 * t)
                    for c in range(4):
                        k = 4 * half + c
                        ins = nc.tensor.transpose(bank(4 + half)[:, c * w:(c + 1) * w],
                                                  h2[t % 2][0:w, k * P:(k + 1) * P], ident[0:w, 0:w])
                    ins.then_inc(h2T_ready, 1)
                pe.wait_ge(h2T_copied, 2 * t + 2)
                if t:
                    pe.wait_ge(lg_used, t)
                NR = NGRP + NE
                for k in range(KD):
                    ins = mm(bank(7)[0:w, t * NR:(t + 1) * NR], h2T[t % 2][:, k, 0:w], wr[:, k, :],
                             start=(k == 0), stop=(k == KD - 1))
                ins.then_inc(lg_ready, 1)

            for t in range(NT + 1):
                if t < NT:
                    project(t)
                if t >= 1:
                    route(t - 1)

            pe.wait_ge(assigned, 1)
            pe.wait_ge(o_used, 4 * NT)
            mm(bank(0)[:, 0:NT * NE], before, r_hot.rearrange("p t e -> p (t e)"), start=True, stop=False)
            mm(bank(0)[:, 0:NT * NE], ones, r_sum.rearrange("p t e -> p (t e)"), start=False, stop=True)
            mm(bank(0)[:, NT * NE:(NT + 1) * NE], ones, r_sum[:, NQ, :], start=True, stop=False)
            mm(bank(0)[:, NT * NE:(NT + 1) * NE], ones[0:NS, :], r_hot[0:NS, NQ, :], start=False, stop=True
               ).then_inc(ranked, 1)
            for n in range(2 * NT):
                w = rows(n // 2)
                pe.wait_ge(hot_ready, n + 1)
                ins = mm(bank(1)[0:SLOTS, 0:NBLK], hot_slot[n % 2][0:w, :], hot_blk[n % 2][0:w, :],
                         start=(n == 0), stop=(n == 2 * NT - 1))
                ins.then_inc(hot_used, 1)

            def turn_rows(f):
                for k in range(KD):
                    ins = nc.tensor.transpose(bank(4 + k // 4)[:, (k % 4) * SLOTS:(k % 4 + 1) * SLOTS],
                                              xg[:, k * P:(k + 1) * P], ident[0:SLOTS, 0:SLOTS])
                    if k % 4 == 3:
                        ins.then_inc(f.xT_ready, 1)

            def gate_or_up(w, s, b, done):
                for m in range(DE // P):
                    for k in range(KD):
                        ins = mm(bank(b)[:, m * SLOTS:(m + 1) * SLOTS], w[s][:, k, m * P:(m + 1) * P], xT[:, k, :],
                                 start=(k == 0), stop=(k == KD - 1))
                ins.then_inc(done, 1)

            def down(f, s, b):
                pe.wait_ge(f.down_split, b + 1)
                for half in range(2):
                    cols = slice(half * 512, (half + 1) * 512)
                    out = bank(2 + half)[0:SLOTS, :]
                    for m in range(DE // P):
                        if half == 0 and m % 2 == 0:
                            pe.wait_ge(f.hid_hi_done, 2 * b + (m // 2 + 1))
                        mm(out, hid_hi[:, m, :], wd_hi[:, m, cols], start=(m == 0), stop=False)
                        mm(out, hid_hi[:, m, :], wd_lo[s][:, m, cols], start=False, stop=False)
                    if half == 0:
                        pe.wait_ge(f.hid_done, b + 1)
                    for m in range(DE // P):
                        ins = mm(out, hid_lo[:, m, :], wd_hi[:, m, cols], start=False, stop=(m == DE // P - 1))
                ins.then_inc(f.y_done, 1)

            def expert(b, turns, s, sd, turn_next=True):
                pe.wait_ge(first.xT_act, b + 1)
                pe.wait_ge(first.xT_dve, b + 1)
                pe.wait_ge(first.gate_in[s], 16 * turns + 16)
                gate_or_up(wg, s, 0, first.gate_done)
                pe.wait_ge(first.up_in[s], 16 * turns + 16)
                gate_or_up(wu, s, 1, first.up_done)
                if turn_next:
                    pe.wait_ge(first.rows_in, 16 * b + 32)
                    turn_rows(first)
                if not isinstance(b, int) or b > 0:
                    pe.wait_ge(first.y_act, b)
                    pe.wait_ge(first.y_dve, b)
                down(first, sd, b)

            pe.wait_ge(routed, 1)
            pe.wait_ge(first.rows_in, 16)
            turn_rows(first)
            expert(0, 0, 0, 0)
            expert(1, 0, 1, 1)
            with pe.Fori(0, (NE - 3) // 6, 1) as j:
                for k in range(6):
                    expert(6 * j + (2 + k), 2 * j + (2 + k) // 3, (2 + k) % 3, k % 2)
            for b in range(2 + (NE - 3) // 6 * 6, NE):
                expert(b, b // 3, b % 3, b % 2, b < NE - 1)
            pe.wait_ge(first.y_act, NE)
            pe.wait_ge(first.y_dve, NE)
            more = pe.value_load(oexp[0:1, OVER:OVER + 1], min_val=0, max_val=OVER)
            with pe.If(more > 0):
                with pe.Fori(0, more, 1) as o:
                    pe.wait_ge(further.rows_in, 16 * o + 16)
                    turn_rows(further)
                    pe.wait_ge(further.xT_act, o + 1)
                    pe.wait_ge(further.xT_dve, o + 1)
                    pe.wait_ge(further.gate_in[0], 16 * o + 16)
                    gate_or_up(wg, 0, 0, further.gate_done)
                    pe.wait_ge(further.up_in[0], 16 * o + 16)
                    gate_or_up(wu, 0, 1, further.up_done)
                    down(further, 0, o)
                    pe.wait_ge(further.y_act, o + 1)
                    pe.wait_ge(further.y_dve, o + 1)

        def unload_group(eng, copy, g):
            kind, i, n = groups[g]
            ps = group_psum(g)
            if kind == "k":
                return copy(kT[:, i, n * TC:(n + 1) * TC], ps[:, 0:TC])
            if kind == "rows":
                return copy(srow[:, i, :], ps[0:NS, :])
            if kind == "v":
                return copy(vT[i % 2][:, n * TC:(n + 1) * TC], ps[:, 0:TC])
            if kind == "vn":
                cols = slice(i * P, (i + 1) * P)
                if n == 2:
                    return copy(srow[:, 2, cols], ps[0:NS, 0:P])
                return copy(v[:, 4 * n:4 * n + 4, cols], ps[:, :].rearrange("p (t c) -> p t c", t=4))
            if kind == "kn":
                return copy(kn[:, i, :], ps[:, :])

        @block.scalar
        def _(act):
            steps = [0]

            def step(ins):
                steps[0] += 1
                ins.then_inc(act_step, 1)
                act.wait_ge(act_step, steps[0])

            def square_sum(t):
                w = rows(t)
                act.wait_ge(x_in[t], 16)
                step(nc.scalar.activation(junk[0:w, :], xt[t % NXT][0:w, :], ACT.Square, accum_out=ssq_x[0:w, t:t + 1]))
                nc.scalar.activation(std_x[0:w, t:t + 1], ssq_x[0:w, t:t + 1], ACT.Sqrt, bias=eps[0:w, :],
                                     scale=1.0 / D).then_inc(std_ready, 1)

            def upper_weights(t):
                act.wait_ge(win_in[t % 3], 16 * (t // 3 + 1))
                if t >= 2:
                    kind, m = tiles[t - 2]
                    act.wait_ge(group_done, number[kind, m, 2] + 1)
                nc.scalar.copy(w_hi[t % 2], w_raw[t % 3]).then_inc(w_hi_ready, 1)

            act.wait_ge(const_in, 16)
            for t in range(NXN):
                square_sum(t)
            upper_weights(0)
            for g, (kind, i, n) in enumerate(groups):
                if n == 0 and (kind, i) in tiles and tiles.index((kind, i)) + 1 < len(tiles):
                    upper_weights(tiles.index((kind, i)) + 1)
                if kind == "x":
                    w = rows(i)
                    act.wait_ge(group_done, g + 1)
                    nc.scalar.copy(h_hi[:, 4 * n:4 * n + 4, i * P:i * P + w],
                                   group_psum(g)[:, 0:4 * w].rearrange("p (k t) -> p k t", k=4)
                                   ).then_inc(h_hi_ready, 1)
                    if n == 0 and i + NXN < NT:
                        square_sum(i + NXN)
                if taker[g][0] == "act":
                    act.wait_ge(group_done, g + 1)
                    if kind == "q":
                        ins = nc.scalar.mul(qT[:, i, n * TC:(n + 1) * TC], group_psum(g)[:, 0:TC], DH ** -0.5)
                    elif kind == "c":
                        if i >= 1:
                            wait_emptied(act, number["u", i - 1, n])
                        else:
                            act.wait_ge(group_done, number["vn", MA - 1, 2] + 1)
                        ins = nc.scalar.copy(cc[:, n * TC:(n + 1) * TC], group_psum(g)[:, 0:TC])
                    else:
                        if kind == "v" and i >= 2:
                            act.wait_ge(group_done, number["vn", i - 2, 2] + 1)
                        ins = unload_group(act, nc.scalar.copy, g)
                    ins.then_inc(act_emptied, 1)
                if n < 2 or (kind, i) not in tiles:
                    continue
                if tiles.index((kind, i)) == TURN_AT + 2:
                    act.wait_ge(smax_ready, 1)
                    nc.scalar.activation(sprob, bank(6)[0:64, 0:3 * P + NS], ACT.Exp, bias=sneg,
                                         accum_out=sl).then_inc(sexp_ready, 1)
                if tiles.index((kind, i)) == TURN_AT + 4:
                    act.wait_ge(spT_ready, 1)
                    nc.scalar.copy(sprobT[0:NS, 3, :], bank(7)[0:NS, 192:256])
                    nc.scalar.copy(sprobT[:, 0:3, :], bank(7)[:, 0:192].rearrange("p (r c) -> p r c", r=3)
                                   ).then_inc(spT_copied, 1)

            def copy_pT(n):
                w = (steps_of[n][0] + 1) * P
                act.wait_ge(pT_ready, n + 1)
                if n >= 2:
                    act.wait_ge(pv_done, n - 1)
                nc.scalar.copy(pt[n % 2][:, 0:w], bank(4, 2)[:, 0:w]).then_inc(pT_act, 1)

            def exponent(n):
                i, h = steps_of[n]
                w = (i + 1) * P
                act.wait_ge(masked, n + 1)
                if n >= 2 * PAIR:
                    act.wait_ge(an_ready, n - 2 * PAIR + 1)
                c = sum_column(n)
                nc.scalar.activation(sm[n % 3][:, 0:w], sm[n % 3][:, 0:w], ACT.Exp, bias=neg_n[:, n % 3:n % 3 + 1],
                                     accum_out=lsum[:, c:c + 1]).then_inc(exped, 1)

            def copy_aT(k):
                i = turned(k)[0]
                act.wait_ge(aT_ready, k + 1)
                nc.scalar.copy(qT[:, :, i * P:(i + 1) * P], bank(7).rearrange("p (m t) -> p m t", m=MA)
                               ).then_inc(aT_copied, 1)

            def upper_wo(k):
                act.wait_ge(wo_in[k % 4], 16 * (k // 4 + 1))
                nc.scalar.activation(wo_hi[:, k, :], wo_raw[k % 4], ACT.Copy, scale=gout[:, k:k + 1]
                                     ).then_inc(wo_hi_ready, 1)

            for n in range(NSTEP + 8):
                if 2 <= n < NSTEP + 2 and (n - 2) % 3:
                    copy_pT(n - 2)
                if n < NSTEP:
                    exponent(n)
                if n in turn_step:
                    copy_aT(turn_step[n])
                if n in split_step:
                    upper_wo(split_step[n])

            def squares(t):
                w = rows(t)
                if t == 0:
                    act.wait_ge(wo_ready, KD)
                    act.wait_ge(pT_ready, NSTEP)
                    act.wait_ge(pv_done, NSTEP)
                if t >= 2:
                    act.wait_ge(o_ready, 4 * (t - 1))
                    act.wait_ge(sq_summed, t - 1)
                cols = slice(t * P, t * P + w)
                nc.scalar.activation(sq[t % 2][:, 0:MA, 0:w], qT[:, :, cols], ACT.Square)
                nc.scalar.activation(sq[t % 2][:, MA:2 * MA, 0:w], cT[:, :, cols], ACT.Square).then_inc(sq_ready, 1)
                nc.scalar.copy(a_hi[t % 2][:, 0:MA, 0:w], qT[:, :, cols])
                nc.scalar.copy(a_hi[t % 2][:, MA:2 * MA, 0:w], cT[:, :, cols]).then_inc(a_hi_ready, 1)

            def roots(t):
                w = rows(t)
                act.wait_ge(ssq_ready, t + 1)
                if t >= 1:
                    act.wait_ge(o_used, 4 * t)
                nc.scalar.activation(std_ac[0:w, :], bank(6)[0:w, 2 * t:2 * t + 2], ACT.Sqrt, bias=eps[0:w, :],
                                     scale=1.0 / DA).then_inc(std_ac_ready, 1)

            def root_ffn(t):
                w = rows(t)
                act.wait_ge(o_used, 4 * t + 4)
                if t >= 2:
                    act.wait_ge(h2T_ready, 2 * (t - 1))
                    act.wait_ge(h2_out[t % 2], 16 * (t // 2))
                c = t % 2
                step(nc.scalar.activation(h2[c][0:w, :], xres[0:w, t, :], ACT.Square, accum_out=ssq_f[0:w, c:c + 1]))
                nc.scalar.activation(std_f[0:w, c:c + 1], ssq_f[0:w, c:c + 1], ACT.Sqrt, bias=eps[0:w, :],
                                     scale=1.0 / D).then_inc(std_f_ready, 1)

            def copy_h2T(t):
                w = rows(t)
                for half in range(2):
                    act.wait_ge(h2T_ready, 2 * t + half + 1)
                    if t >= 2:
                        act.wait_ge(lg_ready, t - 1)
                    nc.scalar.copy(h2T[t % 2][:, 4 * half:4 * half + 4, 0:w],
                                   bank(4 + half)[:, 0:4 * w].rearrange("p (k t) -> p k t", k=4)
                                   ).then_inc(h2T_copied, 1)

            squares(0)
            for t in range(NT):
                roots(t)
                if t + 1 < NT:
                    squares(t + 1)
                if t >= 1:
                    copy_h2T(t - 1)
                root_ffn(t)
            copy_h2T(NT - 1)
            act.wait_ge(gd_ready, 1)
            nc.scalar.activation(r_d, r_d, ACT.Exp).then_inc(gexp_ready, 1)
            act.wait_ge(vd_ready, 1)
            nc.scalar.activation(r_vd, r_vd, ACT.Exp).then_inc(vexp_ready, 1)

            def copy_xT(f, n):
                act.wait_ge(f.xT_ready, 2 * n + 1)
                nc.scalar.copy(xT[:, 0:4, :], bank(4)[:, 0:4 * SLOTS].rearrange("p (k t) -> p k t", k=4)
                               ).then_inc(f.xT_act, 1)

            def silu(f, n):
                act.wait_ge(f.gate_done, n + 1)
                nc.scalar.activation(sg, bank(0)[:, 0:4 * SLOTS].rearrange("p (m t) -> p m t", m=4), ACT.Silu
                                     ).then_inc(f.silu_done, 1)

            def copy_y(f, n, before=0):
                act.wait_ge(f.y_done, n + (before + 1))
                nc.scalar.copy(ysb[:, 0:512], bank(2)[0:SLOTS, :]).then_inc(f.y_act, 1)

            def upper_down(f, b, turns, s):
                act.wait_ge(f.down_in[s], 16 * turns + 16)
                if f is first and (not isinstance(b, int) or b > 0):
                    act.wait_ge(f.y_done, b)
                nc.scalar.copy(wd_hi, wd[s]).then_inc(f.down_hi, 1)

            def expert(b, turns, s, turn_next=True):
                upper_down(first, b, turns, s)
                silu(first, b)
                if turn_next:
                    copy_xT(first, b + 1)
                if not isinstance(b, int) or b > 0:
                    act.wait_ge(first.sent, 16 * b)
                copy_y(first, b)

            copy_xT(first, 0)
            expert(0, 0, 0)
            with act.Fori(0, NE // 2 - 1, 1) as j:
                expert(2 * j + 1, j, 1)
                expert(2 * j + 2, j + 1, 0)
            expert(NE - 1, NE // 2 - 1, 1, False)
            act.wait_ge(first.sent, 16 * NE)
            more = act.value_load(oexp[0:1, OVER:OVER + 1], min_val=0, max_val=OVER)
            with act.If(more > 0):
                with act.Fori(0, more, 1) as o:
                    copy_xT(further, o)
                    upper_down(further, o, o, 0)
                    silu(further, o)
                    copy_y(further, o, NE)
                    act.wait_ge(further.sent, 16 * o + 16)

            for t in range(NT):
                w = rows(t)
                act.wait_ge(fin_res, t + 1)
                c = t % 2
                step(nc.scalar.activation(fjunk[0:w, :], xres[0:w, t, :], ACT.Square, accum_out=ssq_f[0:w, c:c + 1]))
                if t >= 2:
                    act.wait_ge(fin_out, t - 1)
                nc.scalar.activation(std_f[0:w, c:c + 1], ssq_f[0:w, c:c + 1], ACT.Sqrt, bias=eps[0:w, :],
                                     scale=1.0 / D).then_inc(fin_std, 1)

        @block.vector
        def _(dve):
            vec = nc.vector
            steps = [0]

            def step(ins):
                steps[0] += 1
                ins.then_inc(dve_step, 1)
                dve.wait_ge(dve_step, steps[0])

            def normalise(t):
                w = rows(t)
                dve.wait_ge(std_ready, t + 1)
                step(vec.reciprocal(rst_x[0:w, t:t + 1], std_x[0:w, t:t + 1]))
                if t >= NXN:
                    dve.wait_ge(group_done, number["x", t - NXN, 1] + 1)
                vec.scalar_tensor_tensor(out=xn[t % NXN][0:w, :], in0=xt[t % NXT][0:w, :], scalar=rst_x[0:w, t:t + 1],
                                         in1=gmix[0:w, :], op0=ALU.mult, op1=ALU.mult).then_inc(xn_ready, 1)

            def lower_weights(t):
                dve.wait_ge(w_hi_ready, t + 1)
                vec.tensor_tensor(w_lo[t % 2], w_raw[t % 3], w_hi[t % 2].bitcast(F32), ALU.subtract
                                  ).then_inc(w_ready, 1)

            def sample_scores(b):
                dve.wait_ge(kv_in[b % 2], 48 * (b // 2 + 1))
                dve.wait_ge(qb_ready, b + 1)
                q = bank(4 + b % 2)
                for r in range(3):
                    keys = kv[:, b % 2, r * DA:(r + 1) * DA]
                    step(vec.tensor_tensor(keys, keys, q, ALU.mult))
                    ins = vec.tensor_reduce(sscore[:, r, b * H:(b + 1) * H], keys.rearrange("p (h d) -> p h d", h=H),
                                            X, ALU.add)
                ins.then_inc(scored, 1)

            def own_scores():
                dve.wait_ge(small_in, 16 * 4)
                step(vec.tensor_tensor(own, srow[:, 1, :], srow[:, 0, :], ALU.mult))
                step(vec.tensor_reduce(own_sum, own.rearrange("p (h d) -> p h d", h=H), X, ALU.add))
                vec.tensor_tensor(sscore[0:NS, 3, :].rearrange("p (b h) -> p b h", b=NS),
                                  ssm.rearrange("p (b h) -> p b h", b=NS),
                                  own_sum.unsqueeze(1).broadcast_to([NS, NS, H]), ALU.add).then_inc(scored, 1)

            def conv(m):
                step(vec.tensor_scalar(z[:, 0:SEQ], u[:, 0:SEQ], cw[:, m, 0:1], None, ALU.mult))
                for j in (1, 2):
                    step(vec.scalar_tensor_tensor(out=z[:, 0:SEQ], in0=u[:, j:j + SEQ], scalar=cw[:, m, j:j + 1],
                                                  in1=z[:, 0:SEQ], op0=ALU.mult, op1=ALU.add))
                zs = z[:, SEQ:NTOK]
                step(vec.tensor_scalar(zs, cstate[:, m, 0, :], cw[:, m, 0:1], None, ALU.mult))
                for j in (1, 2):
                    src = cstate[:, m, 1, :] if j == 1 else u[:, SEQ + 2:NTOK + 2]
                    step(vec.scalar_tensor_tensor(out=zs, in0=src, scalar=cw[:, m, j:j + 1], in1=zs,
                                                  op0=ALU.mult, op1=ALU.add))
                vec.tensor_copy(uout[:, m, :], u[:, SEQ:NTOK + 2]).then_inc(u_ready, 1)

            dve.wait_ge(const_in, 16)
            dve.wait_ge(gmix_in, 16)
            for t in range(NXN):
                normalise(t)
            lower_weights(0)
            for g, (kind, i, n) in enumerate(groups):
                if n == 0 and (kind, i) in tiles and tiles.index((kind, i)) + 1 < len(tiles):
                    lower_weights(tiles.index((kind, i)) + 1)
                if taker[g][0] == "dve":
                    dve.wait_ge(group_done, g + 1)
                    ps = group_psum(g)
                    if kind == "x":
                        w = rows(i)
                        dve.wait_ge(h_hi_ready, 2 * i + n + 1)
                        there = slice(i * P, i * P + w)
                        ins = vec.tensor_tensor(h_lo[:, 4 * n:4 * n + 4, there],
                                                ps[:, 0:4 * w].rearrange("p (k t) -> p k t", k=4),
                                                h_hi[:, 4 * n:4 * n + 4, there].bitcast(F32), ALU.subtract)
                    elif kind == "q":
                        ins = vec.tensor_scalar(qT[:, i, n * TC:(n + 1) * TC], ps[:, 0:TC], DH ** -0.5, None, ALU.mult)
                    elif kind == "u":
                        if i == 0 and n == 0:
                            step(vec.memset(u[:, 0:2], 0.0))
                        wait_emptied(dve, number["c", i, n])
                        ins = vec.tensor_tensor(u[:, 2 + n * TC:2 + (n + 1) * TC], ps[:, 0:TC],
                                                cc[:, n * TC:(n + 1) * TC], ALU.mult)
                    elif kind == "b":
                        if i == 0 and n == 0:
                            dve.wait_ge(kn_out, 16)
                        ins = vec.tensor_tensor(cT[:, i, n * TC:(n + 1) * TC], ps[:, 0:TC],
                                                z[:, n * TC:(n + 1) * TC], ALU.mult)
                    else:
                        if kind == "v" and i >= 2:
                            dve.wait_ge(group_done, number["vn", i - 2, 2] + 1)
                        ins = unload_group(dve, vec.tensor_copy, g)
                    ins.then_inc(dve_emptied, 1)
                    if kind == "x" and n == 1 and i + NXN < NT:
                        normalise(i + NXN)
                if n < 2 or (kind, i) not in tiles:
                    continue
                t = tiles.index((kind, i))
                if kind == "u":
                    if i == 0:
                        dve.wait_ge(small_in, 16 * 4)
                    dve.wait_ge(dve_emptied, taker[g][1])
                    conv(i)
                if SCORE_AT <= t < SCORE_AT + NS:
                    sample_scores(t - SCORE_AT)
                if t == SCORE_AT + NS - 1:
                    own_scores()
                if t == TURN_AT + 1:
                    dve.wait_ge(sT_ready, 1)
                    step(vec.tensor_reduce(smx, bank(6)[0:64, 0:3 * P + NS], X, ALU.max))
                    vec.tensor_scalar(sneg, smx, -1.0, None, ALU.mult).then_inc(smax_ready, 1)
                if t == TURN_AT + 3:
                    dve.wait_ge(sexp_ready, 1)
                    step(vec.reciprocal(srl, sl))
                    vec.tensor_scalar(sprob, sprob, srl, None, ALU.mult).then_inc(sp_ready, 1)
            dve.wait_ge(spv_ready, 1)
            out = bank(4).rearrange("p (m b h) -> p m b h", m=8, b=NS)
            for m in range(MA):
                for e in range(2):
                    part = slice(e * DH, (e + 1) * DH)
                    ins = vec.tensor_copy(qT[part, m, SEQ:NTOK], out[part, m, :, 2 * m + e])
            ins.then_inc(s_attn, 1)

            def mask(n):
                i = steps_of[n][0]
                w = (i + 1) * P
                if n == 0:
                    dve.wait_ge(mask_in, 16)
                dve.wait_ge(s_ready, n + 1)
                if n >= 3:
                    dve.wait_ge(pT_ready, n - 2)
                c = n % 3
                step(vec.tensor_tensor_reduce(sm[c][:, 0:w], bank(2 * (n % 2), 2)[:, 0:w], amask[:, SEQ - w:SEQ],
                                              1.0, NEG, ALU.add, ALU.max, mx_n[:, c:c + 1]))
                vec.tensor_scalar(neg_n[:, c:c + 1], mx_n[:, c:c + 1], -1.0, None, ALU.mult).then_inc(masked, 1)

            def copy_pT(n):
                w = (steps_of[n][0] + 1) * P
                dve.wait_ge(pT_ready, n + 1)
                if n >= 2:
                    dve.wait_ge(pv_done, n - 1)
                vec.tensor_copy(pt[n % 2][:, 0:w], bank(4, 2)[:, 0:w]).then_inc(pT_dve, 1)

            def divide(n):
                i, h = steps_of[n]
                c = sum_column(n)
                r = rl[:, n % 2:n % 2 + 1]
                dve.wait_ge(exped, n + 1)
                step(vec.reciprocal(r, lsum[:, c:c + 1]))
                dve.wait_ge(pv_done, n + 1)
                if n >= 2 * PAIR and n % PAIR == 0:
                    dve.wait_ge(aT_ready, 2 * (n // PAIR - 1))
                half = h % 2 * DH
                vec.tensor_scalar(an[c // H][:, h * DH:(h + 1) * DH], bank(6 + n % 2)[:, half:half + DH],
                                  r, None, ALU.mult).then_inc(an_ready, 1)

            def lower_wo(k):
                dve.wait_ge(wo_hi_ready, k + 1)
                vec.scalar_tensor_tensor(out=wo_lo[:, k, :], in0=wo_raw[k % 4], scalar=gout[:, k:k + 1],
                                         in1=wo_hi[:, k, :].bitcast(F32), op0=ALU.mult, op1=ALU.subtract
                                         ).then_inc(wo_ready, 1)

            for n in range(NSTEP + 8):
                if n < NSTEP:
                    mask(n)
                if 3 <= n < NSTEP + 3:
                    divide(n - 3)
                if 2 <= n < NSTEP + 2 and (n - 2) % 3 == 0:
                    copy_pT(n - 2)
                if n in split_step:
                    lower_wo(split_step[n])

            def lower_attention(t):
                w = rows(t)
                dve.wait_ge(sq_ready, t + 1)
                if t >= 2:
                    dve.wait_ge(ssq_ready, t - 1)
                vec.tensor_reduce(sqs[t % 2][:, :, 0:w],
                                  sq[t % 2][:, :, 0:w].rearrange("p (c m) t -> p c t m", c=2), X, ALU.add
                                  ).then_inc(sq_summed, 1)
                dve.wait_ge(a_hi_ready, t + 1)
                for c, src in enumerate((qT, cT)):
                    m = slice(c * MA, (c + 1) * MA)
                    ins = vec.tensor_tensor(a_lo[t % 2][:, m, 0:w], src[:, :, t * P:t * P + w],
                                            a_hi[t % 2][:, m, 0:w].bitcast(F32), ALU.subtract)
                ins.then_inc(a_ready, 1)

            def residual(t):
                w = rows(t)
                dve.wait_ge(xres_in[t], 16)
                dve.wait_ge(std_ac_ready, t + 1)
                step(vec.reciprocal(rst_ac[0:w, :], std_ac[0:w, :]))
                for half in range(2):
                    x = xres[0:w, t, half * 512:(half + 1) * 512]
                    for c in range(2):
                        dve.wait_ge(o_ready, 4 * t + 2 * half + c + 1)
                        ins = vec.scalar_tensor_tensor(out=x, in0=bank(2 * half + c)[0:w, :], scalar=rst_ac[0:w, c:c + 1],
                                                       in1=x, op0=ALU.mult, op1=ALU.add)
                        ins.then_inc(o_used, 1)
                        dve.wait_ge(o_used, 4 * t + 2 * half + c + 1)

            def router_rows(t):
                w = rows(t)
                c = t % 2
                dve.wait_ge(std_f_ready, t + 1)
                step(vec.reciprocal(rst_f[0:w, c:c + 1], std_f[0:w, c:c + 1]))
                vec.scalar_tensor_tensor(out=h2[c][0:w, :], in0=xres[0:w, t, :], scalar=rst_f[0:w, c:c + 1],
                                         in1=gffn[0:w, :], op0=ALU.mult, op1=ALU.mult).then_inc(h2_ready, 1)

            dve.wait_ge(router_in, 48)
            step(vec.memset(lg, 0.0))
            lower_attention(0)
            for t in range(NT):
                if t + 1 < NT:
                    lower_attention(t + 1)
                residual(t)
                NR = NGRP + NE
                if t >= 1:
                    w = rows(t - 1)
                    dve.wait_ge(lg_ready, t)
                    vec.tensor_tensor(lg[0:w, t - 1, :], bank(7)[0:w, (t - 1) * NR:t * NR], rbias[0:w, :], ALU.add
                                      ).then_inc(lg_used, 1)
                router_rows(t)
            dve.wait_ge(lg_ready, NT)
            vec.tensor_tensor(lg[0:NS, NQ, :], bank(7)[0:NS, NQ * NR:NT * NR], rbias[0:NS, :], ALU.add
                              ).then_inc(lg_used, 1)
            dve.wait_ge(lg_used, NT)
            dve.wait_ge(h2_out[0], 16 * 5)
            dve.wait_ge(h2_out[1], 16 * 4)

            def wide(x9, n):
                return x9.unsqueeze(2).broadcast_to([P, NT, n])

            def ramps(n):
                return ramp[:, 0:n].unsqueeze(1).broadcast_to([P, NT, n])

            def first_index(dst, eq, n):
                step(vec.scalar_tensor_tensor(out=eq, in0=eq, scalar=-float(n), in1=ramps(n), op0=ALU.mult,
                                              op1=ALU.add))
                step(vec.tensor_reduce(dst, eq, X, ALU.min))
                step(vec.tensor_scalar(dst, dst, float(n), None, ALU.add))

            gl = lg[:, :, 0:NGRP]
            step(vec.tensor_reduce(r_gm, gl, X, ALU.max))
            step(vec.tensor_tensor(r_eq, gl, wide(r_gm, NGRP), ALU.is_equal))
            vec.tensor_tensor(r_d, gl, wide(r_gm, NGRP), ALU.subtract).then_inc(gd_ready, 1)
            first_index(r_gi, r_eq, NGRP)
            step(vec.tensor_tensor(r_goh, ramps(NGRP), wide(r_gi, NGRP), ALU.is_equal))
            for g in range(NGRP):
                el = lg[:, :, NGRP + g * EPG:NGRP + (g + 1) * EPG]
                dst = r_le if g == 0 else r_eq8
                step(vec.tensor_tensor(dst, el, r_goh[:, :, g:g + 1].broadcast_to([P, NT, EPG]), ALU.mult))
                if g:
                    step(vec.tensor_tensor(r_le, r_le, r_eq8, ALU.add))
            step(vec.tensor_reduce(r_v1, r_le, X, ALU.max))
            step(vec.tensor_tensor(r_eq8, r_le, wide(r_v1, EPG), ALU.is_equal))
            first_index(r_i1, r_eq8, EPG)
            step(vec.tensor_tensor(r_oh, ramps(EPG), wide(r_i1, EPG), ALU.is_equal))
            step(vec.scalar_tensor_tensor(out=r_le2, in0=r_oh, scalar=-3e38, in1=r_le, op0=ALU.mult, op1=ALU.add))
            step(vec.tensor_reduce(r_v2, r_le2, X, ALU.max))
            step(vec.tensor_tensor(r_eq8, r_le2, wide(r_v2, EPG), ALU.is_equal))
            first_index(r_i2, r_eq8, EPG)
            vec.tensor_tensor(r_vd, r_v2, r_v1, ALU.subtract).then_inc(vd_ready, 1)
            for c, idx in enumerate((r_i1, r_i2)):
                step(vec.scalar_tensor_tensor(out=r_e[:, c, :], in0=r_gi, scalar=float(EPG), in1=idx, op0=ALU.mult,
                                              op1=ALU.add))
            step(vec.tensor_tensor(r_hot1, ramps(NE), wide(r_e[:, 0, :], NE), ALU.is_equal))
            step(vec.tensor_tensor(r_hot2, ramps(NE), wide(r_e[:, 1, :], NE), ALU.is_equal))
            step(vec.tensor_tensor(r_hot, r_hot1, r_hot2, ALU.add))
            step(vec.memset(r_sum[:, 0, :], 0.0))
            for t in range(1, NT):
                ins = vec.tensor_tensor(r_sum[:, t, :], r_sum[:, t - 1, :], r_hot[:, t - 1, :], ALU.add)
                if t < NT - 1:
                    step(ins)
            ins.then_inc(assigned, 1)
            dve.wait_ge(gexp_ready, 1)
            step(vec.tensor_reduce(r_sg, r_d, X, ALU.add))
            step(vec.reciprocal(r_pg, r_sg))
            dve.wait_ge(vexp_ready, 1)
            step(vec.tensor_scalar(r_den, r_vd, 1.0, None, ALU.add))
            step(vec.reciprocal(r_t9, r_den))
            step(vec.tensor_tensor(gates[:, 0, :], r_t9, r_pg, ALU.mult))
            step(vec.tensor_tensor(gates[:, 1, :], gates[:, 0, :], r_vd, ALU.mult))
            step(vec.tensor_scalar(r_mul, ramp[:, 1:MORE + 1], float(SLOTS), None, ALU.mult))
            dve.wait_ge(ranked, 1)
            step(vec.tensor_copy(r_rank, bank(0)[:, 0:(NT + 1) * NE].rearrange("p (t e) -> p t e", t=NT + 1)))
            count = r_rank[:, NT, :]
            step(vec.tensor_tensor(r_gt, count.unsqueeze(2).broadcast_to([P, NE, MORE]),
                                   r_mul.unsqueeze(1).broadcast_to([P, NE, MORE]), ALU.is_gt))
            step(vec.tensor_reduce(r_ob, r_gt, X, ALU.add))
            step(vec.tensor_tensor_scan(r_inc, ones[:, 0:NE], r_ob, 0.0, ALU.mult, ALU.add))
            step(vec.tensor_tensor(r_exc, r_inc, r_ob, ALU.subtract))
            for c, hot in enumerate((r_hot1, r_hot2)):
                step(vec.tensor_tensor(r_big, hot, r_rank[:, 0:NT, :], ALU.mult))
                step(vec.tensor_reduce(r_r[:, c, :], r_big, X, ALU.add))
                step(vec.tensor_tensor(r_big, hot, r_exc.unsqueeze(1).broadcast_to([P, NT, NE]), ALU.mult))
                step(vec.tensor_reduce(r_so[:, c, :], r_big, X, ALU.add))
            pairs = r_r.rearrange("p c t -> p (c t)")
            vec.tensor_scalar(r_is, r_r, float(SLOTS), None, ALU.is_ge)
            step(vec.tensor_tensor(r_ge, pairs.unsqueeze(2).broadcast_to([P, 2 * NT, MORE]),
                                   r_mul.unsqueeze(1).broadcast_to([P, 2 * NT, MORE]), ALU.is_ge))
            step(vec.tensor_reduce(r_q.rearrange("p c t -> p (c t)"), r_ge, X, ALU.add))
            step(vec.scalar_tensor_tensor(out=r_j, in0=r_q, scalar=-float(SLOTS), in1=r_r, op0=ALU.mult, op1=ALU.add))
            step(vec.tensor_tensor(r_blk, r_so, r_q, ALU.add))
            step(vec.tensor_tensor(r_blk, r_blk, r_e, ALU.subtract))
            step(vec.scalar_tensor_tensor(out=r_blk, in0=r_blk, scalar=float(NE - 1), in1=r_is, op0=ALU.add,
                                          op1=ALU.mult))
            step(vec.tensor_tensor(r_blk, r_blk, r_e, ALU.add))
            for n in range(2 * NT):
                t, c = divmod(n, 2)
                w = rows(t)
                if n >= 2:
                    dve.wait_ge(hot_used, n - 1)
                vec.tensor_scalar(hot_slot[c][0:w, :], ramp[0:w, 0:SLOTS], r_j[0:w, c, t:t + 1],
                                  (tokv, destv)[c][0:w, t:t + 1], ALU.is_equal, ALU.mult)
                vec.tensor_scalar(hot_blk[c][0:w, :], ramp[0:w, 0:NBLK], r_blk[0:w, c, t:t + 1], None, ALU.is_equal
                                  ).then_inc(hot_ready, 1)
            step(vec.tensor_tensor(r_cmp[0:1], r_inc[0:1].unsqueeze(1).broadcast_to([1, OVER, NE]),
                                   ramp[0:1, 0:OVER].unsqueeze(2).broadcast_to([1, OVER, NE]), ALU.is_le))
            step(vec.tensor_reduce(r_tab2[0:1, 0:OVER], r_cmp[0:1], X, ALU.add))
            step(vec.tensor_scalar(r_tab2[0:1, 0:OVER], r_tab2[0:1, 0:OVER], float(NE - 1), None, ALU.min))
            vec.tensor_copy(oexp[0:1, 0:OVER], r_tab2[0:1, 0:OVER])
            vec.tensor_copy(oexp[0:1, OVER:OVER + 1], r_inc[0:1, NE - 1:NE])
            dve.wait_ge(hot_used, 2 * NT)
            tab, row, dest = bank(1)[0:SLOTS, 0:NBLK], r_tab[0:SLOTS, 0, :], r_tab[0:SLOTS, 1, :]
            step(vec.tensor_scalar(row, tab, float(NTOK), -float(NTOK), ALU.is_gt, ALU.mult))
            step(vec.scalar_tensor_tensor(out=row, in0=tab, scalar=-1.0, in1=row, op0=ALU.add, op1=ALU.add))
            step(vec.tensor_scalar(row, row, 0.0, None, ALU.max))
            step(vec.tensor_scalar(r_tab2[0:SLOTS], tab, 0.0, DROP, ALU.is_equal, ALU.mult))
            step(vec.scalar_tensor_tensor(out=dest, in0=tab, scalar=-1.0, in1=r_tab2[0:SLOTS], op0=ALU.add,
                                          op1=ALU.add))
            vec.tensor_copy(gi_s, r_tab[0:SLOTS, 0, 0:1])
            step(vec.tensor_copy(gidx[:], r_tab[0:SLOTS, 0, :]))
            vec.tensor_copy(sidx[:], r_tab[0:SLOTS, 1, :]).then_inc(routed, 1)

            def copy_xT(f, n):
                dve.wait_ge(f.xT_ready, 2 * n + 2)
                vec.tensor_copy(xT[:, 4:8, :], bank(5)[:, 0:4 * SLOTS].rearrange("p (k t) -> p k t", k=4)
                                ).then_inc(f.xT_dve, 1)

            def lower_down(f, n, s):
                dve.wait_ge(f.down_hi, n + 1)
                vec.tensor_tensor(wd_lo[s], wd[s], wd_hi.bitcast(F32), ALU.subtract).then_inc(f.down_split, 1)

            def hidden(f, n):
                dve.wait_ge(f.silu_done, n + 1)
                dve.wait_ge(f.up_done, n + 1)
                up = bank(1)[:, 0:4 * SLOTS].rearrange("p (m t) -> p m t", m=4)
                pieces = (slice(0, 2), slice(2, 4))
                for m in pieces:
                    vec.tensor_tensor(hid[:, m, :], up[:, m, :], sg[:, m, :], ALU.mult).then_inc(f.pieces, 1)
                for k, m in enumerate(pieces):
                    dve.wait_ge(f.pieces, 2 * n + (k + 1))
                    vec.tensor_copy(hid_hi[:, m, :], hid[:, m, :]).then_inc(f.hid_hi_done, 1)
                dve.wait_ge(f.hid_hi_done, 2 * n + 2)
                vec.tensor_tensor(hid_lo, hid, hid_hi.bitcast(F32), ALU.subtract).then_inc(f.hid_done, 1)

            def copy_y(f, n, before=0):
                dve.wait_ge(f.y_done, n + (before + 1))
                vec.tensor_copy(ysb[:, 512:1024], bank(3)[0:SLOTS, :]).then_inc(f.y_dve, 1)

            def stage(dst, src, blk):
                return vec.tensor_scalar(dst, src[:, bass.ds(blk, 1)], 0.0, None, ALU.add)

            def expert(b, s, turn_next=True, fetch_next=True):
                lower_down(first, b, s)
                hidden(first, b)
                if turn_next:
                    copy_xT(first, b + 1)
                if not isinstance(b, int) or b > 0:
                    dve.wait_ge(first.sent, 16 * b)
                stage(si_s, sidx, b)
                if fetch_next:
                    stage(gi_s, gidx, b + 2)
                if not isinstance(b, int) or b > 0:
                    dve.wait_ge(first.held, b)
                copy_y(first, b)

            copy_xT(first, 0)
            stage(gi_s, gidx, 1).then_inc(first.staged, 1)
            expert(0, 0)
            with dve.Fori(0, NE // 2 - 2, 1) as j:
                expert(2 * j + 1, 1)
                expert(2 * j + 2, 0)
            expert(NE - 3, 1)
            expert(NE - 2, 0, True, False)
            expert(NE - 1, 1, False, False)
            dve.wait_ge(first.sent, 16 * NE)
            dve.wait_ge(first.held, NE)
            more = dve.value_load(oexp[0:1, OVER:OVER + 1], min_val=0, max_val=OVER)
            with dve.If(more > 0):
                with dve.Fori(0, more, 1) as o:
                    stage(si_s, sidx, o + NE)
                    stage(gi_s, gidx, o + NE).then_inc(further.staged, 1)
                    copy_xT(further, o)
                    lower_down(further, o, 0)
                    hidden(further, o)
                    dve.wait_ge(further.held, 2 * o + 1)
                    copy_y(further, o, NE)
                    dve.wait_ge(further.sent, 16 * o + 16)
                    dve.wait_ge(further.held, 2 * o + 2)

            def add_experts(t):
                w = rows(t)
                dve.wait_ge(y_in[t % NY], 32 * (t // NY + 1))
                x = xres[0:w, t, :]
                for c in range(2):
                    ins = vec.scalar_tensor_tensor(out=x, in0=yt[t % NY][0:w, c, :], scalar=gates[0:w, c, t:t + 1], in1=x,
                                                   op0=ALU.mult, op1=ALU.add)
                    if c == 0:
                        step(ins)
                ins.then_inc(fin_res, 1)

            def finish(t):
                w = rows(t)
                c = t % 2
                dve.wait_ge(fin_std, t + 1)
                step(vec.reciprocal(rst_f[0:w, c:c + 1], std_f[0:w, c:c + 1]))
                if t >= NO:
                    dve.wait_ge(out_sent[t % NO], 16 * (t // NO))
                vec.scalar_tensor_tensor(out=ot[t % NO][0:w, :], in0=xres[0:w, t, :], scalar=rst_f[0:w, c:c + 1],
                                         in1=gfin[0:w, :], op0=ALU.mult, op1=ALU.mult).then_inc(fin_out, 1)

            dve.wait_ge(gfin_in, 16)
            add_experts(0)
            for t in range(NT):
                if t + 1 < NT:
                    add_experts(t + 1)
                finish(t)

        @block.gpsimd
        def _(pool):
            gp = nc.gpsimd

            def hold(f, cell):
                gp.tensor_tensor(stat[0:1, cell:cell + 1], ones[0:1, 0:1], ones[0:1, 0:1], ALU.mult
                                 ).then_inc(f.held, 1)

            def fetch(f):
                gp.indirect_dma_start(xg, None, h2_d[:, :], bass.IndirectOffsetOnAxis(ap=gi_s, axis=0)
                                      ).then_inc(f.rows_in, 16)

            def send(f):
                gp.indirect_dma_start(y_d[:, :], bass.IndirectOffsetOnAxis(ap=si_s, axis=0), ysb, None,
                                      bounds_check=2 * NTOK - 1, oob_is_err=False).then_inc(f.sent, 16)

            pool.wait_ge(x_in[NQ], 16)
            for n in range(2 * NS):
                b, src = n % NS, a["cache_k"] if n < NS else a["cache_v"]
                if 2 <= n < NS + 2:
                    pool.wait_ge(scored, n - 1)
                elif n >= NS + 2:
                    pool.wait_ge(spv_used, n - NS - 1)
                for r, d in enumerate(DIL):
                    keys = src[b, WBUF - d * WIN:WBUF, :].rearrange("(j d) c -> j d c", d=d)[:, 0, :]
                    gp.dma_start(kv[:, n % 2, r * DA:(r + 1) * DA], keys).then_inc(kv_in[n % 2], 16)

            pool.wait_ge(h2_out[0], 16 * 5)
            pool.wait_ge(h2_out[1], 16 * 4)
            pool.wait_ge(routed, 1)
            fetch(first)
            pool.wait_ge(first.xT_ready, 2)
            pool.wait_ge(first.staged, 1)
            fetch(first)

            def expert(b, s, fetch_next=True):
                pool.wait_ge(first.y_act, b + 1)
                pool.wait_ge(first.y_dve, b + 1)
                hold(first, 93 + s)
                send(first)
                if fetch_next:
                    fetch(first)

            with pool.Fori(0, NE // 2 - 1, 1) as j:
                expert(2 * j, 0)
                expert(2 * j + 1, 1)
            expert(NE - 2, 0, False)
            expert(NE - 1, 1, False)
            pool.wait_ge(first.sent, 16 * NE)
            more = pool.value_load(oexp[0:1, OVER:OVER + 1], min_val=0, max_val=OVER)
            with pool.If(more > 0):
                with pool.Fori(0, more, 1) as o:
                    pool.wait_ge(further.staged, o + 1)
                    hold(further, 93)
                    fetch(further)
                    pool.wait_ge(further.y_act, o + 1)
                    pool.wait_ge(further.y_dve, o + 1)
                    hold(further, 94)
                    send(further)
                    pool.wait_ge(further.sent, 16 * o + 16)
            gp.memset(stat[0:1, 95:96], 0.0).then_inc(all_sent, 1)


_OUT = {
    "y_prompt": (SEQ, D), "y_sample": (NS, D), "k_prompt": (SEQ, DA), "v_prompt": (SEQ, DA),
    "conv_u": (P, MA, NS + 2), "k_sample": (NS, DA), "v_sample": (NS, DA), "conv_sample_old": (NS, DA),
}


def kernel(**inputs):
    import concourse.bacc as _bacc
    from concourse.bass_utils import run_bass_kernel_spmd as _run

    x = {n: np.ascontiguousarray(v) for n, v in inputs.items()}
    const, amask, smask = constants()
    gain_out = np.concatenate([x["norm_out_attn"][0], x["norm_out_conv"][0]]).reshape(KD, P).T
    arrays = {
        "x_prompt": x["x_prompt"][0], "x_sample": x["x_sample"][:, 0], "w_in": x["w_in"][0],
        "cache_k": x["cache_k"][0].reshape(NS, WBUF, DA), "cache_v": x["cache_v"][0].reshape(NS, WBUF, DA),
        "state_conv": x["state_conv"][0],
        "conv_state": x["state_conv"][0].reshape(NS, 2, MA, P).transpose(3, 2, 1, 0),
        "conv_w": x["conv_w"][0].reshape(CONV, MA, P).transpose(2, 1, 0),
        "gain_out": gain_out, "norm_mix": x["norm_mix"][0], "norm_ffn": x["norm_ffn"][0],
        "norm_final": x["norm_final"], "w_out": x["w_out"][0],
        "w_router": np.concatenate([x["w_router_group"][0], x["w_router_expert"][0]], axis=1)
        .reshape(KD, P, NGRP + NE).transpose(1, 0, 2),
        "b_router": np.concatenate([x["b_router_group"][0], x["b_router_expert"][0]]),
        "w_gate": x["w_gate"][0], "w_up": x["w_up"][0], "w_down": x["w_down"][0],
        "const": const, "amask": amask, "smask": smask,
    }
    nc = _bacc.Bacc("TRN2", target_bir_lowering=False, num_devices=1)
    feed, aps = {}, {}
    for name, arr in arrays.items():
        arr = np.ascontiguousarray(arr)
        feed[f"in_{name}"] = arr
        aps[name] = nc.dram_tensor(f"in_{name}", arr.shape, mybir.dt.from_np(arr.dtype), kind="ExternalInput").ap()
    for name in ("w_gate", "w_up", "w_down"):
        aps[name + "_flat"] = aps[name].rearrange("e d n -> (e d) n")
    for name, shape in _OUT.items():
        aps[name] = nc.dram_tensor(f"out_{name}", shape, F32, kind="ExternalOutput").ap()
    program(nc, aps)
    r = _run(nc, [feed], core_ids=[0]).results[0]
    got = {n: r[f"out_{n}"] for n in _OUT}
    u = got["conv_u"].transpose(2, 1, 0).reshape(NS + 2, DA)
    conv_sample = np.stack([got["conv_sample_old"], u[2:]], axis=1)
    return (got["y_prompt"][None], got["y_sample"][:, None], got["k_prompt"].reshape(1, 1, SEQ, H, DH),
            got["v_prompt"].reshape(1, 1, SEQ, H, DH), u[None, None, 0:2],
            got["k_sample"].reshape(1, NS, 1, H, DH), got["v_sample"].reshape(1, NS, 1, H, DH), conv_sample[None])
```
